# Optimizing a Trainium2 kernel written in Bass

```python
import jax, jax.numpy as jnp
from jax import lax
import numpy as np

D_MODEL = 1024
BATCH = 1
SEQ = 2048
DEPTH = 1

D_MIX = D_MODEL
D_MLSTM = D_MIX // 2
D_CONV = D_MIX - D_MLSTM
N_MLSTM_HEADS = 4
HEAD_DIM = D_MLSTM // N_MLSTM_HEADS
N_CONV_GROUPS = 4
CONV_GROUP_DIM = D_CONV // N_CONV_GROUPS
CONV_WIDTH = 31
QK_CONV_WIDTH = 4
CHUNK = 128
D_FF = 4 * D_MODEL
EPS = 1e-6
D_IN_PROJ = 4 * D_MLSTM + 2 * N_MLSTM_HEADS + 2 * D_CONV

kernel_name = "hybrid_mlstm_conformerconv_sqrelu_sandwich"

def rms_norm(x, w):
    xf = x.astype(jnp.float32)
    y = xf * lax.rsqrt(jnp.mean(xf * xf, axis=-1, keepdims=True) + EPS)
    return (y * w.astype(jnp.float32)).astype(x.dtype)

def causal_depthwise_conv(x, w, b):
    width, ch = w.shape
    y = lax.conv_general_dilated(
        x, w[:, None, :].astype(x.dtype), window_strides=(1,), padding=((width - 1, 0),),
        dimension_numbers=("NWC", "WIO", "NWC"), feature_group_count=ch)
    return y + b.astype(x.dtype)

def mlstm_chunkwise(q, k, v, i_pre, f_pre):
    B, H, S, dh = q.shape
    nc = S // CHUNK

    def to_chunks(t):
        t = t.reshape((B, H, nc, CHUNK) + t.shape[3:])
        return jnp.moveaxis(t, 2, 0)

    q = q * (dh ** -0.5)
    log_f = jax.nn.log_sigmoid(f_pre)
    b_cum = jnp.cumsum(to_chunks(log_f), axis=-1)
    causal = jnp.tril(jnp.ones((CHUNK, CHUNK), dtype=bool))

    def step(carry, xs):
        C, n, m = carry
        qc, kc, vc, li, bc = xs
        inter = bc + m[..., None]
        D = bc[..., :, None] - bc[..., None, :] + li[..., None, :]
        D = jnp.where(causal, D, -jnp.inf)
        m_row = jnp.maximum(inter, jnp.max(D, axis=-1))
        w_inter = jnp.exp(inter - m_row)
        P = jnp.einsum("bhld,bhsd->bhls", qc, kc) * jnp.exp(D - m_row[..., None])
        num = w_inter[..., None] * jnp.einsum("bhld,bhde->bhle", qc, C) + jnp.einsum("bhls,bhse->bhle", P, vc)
        den = w_inter * jnp.einsum("bhld,bhd->bhl", qc, n) + jnp.sum(P, axis=-1)
        h = num / jnp.maximum(jnp.abs(den), jnp.exp(-m_row))[..., None]
        b_last = bc[..., -1]
        g = b_last[..., None] - bc + li
        m_new = jnp.maximum(b_last + m, jnp.max(g, axis=-1))
        decay = jnp.exp(b_last + m - m_new)
        wk = jnp.exp(g - m_new[..., None])[..., None] * kc
        C_new = decay[..., None, None] * C + jnp.einsum("bhsd,bhse->bhde", wk, vc)
        n_new = decay[..., None] * n + jnp.sum(wk, axis=-2)
        return (C_new, n_new, m_new), h

    init = (jnp.zeros((B, H, dh, dh), jnp.float32), jnp.zeros((B, H, dh), jnp.float32),
            jnp.zeros((B, H), jnp.float32))
    xs = (to_chunks(q), to_chunks(k), to_chunks(v), to_chunks(i_pre), b_cum)
    _, h = lax.scan(step, init, xs)
    return jnp.moveaxis(h, 0, 2).reshape(B, H, S, dh)

def setup_inputs(seed: int = 0) -> dict:
    key = jax.random.key(seed)
    ks = jax.random.split(key, 20)
    f32 = jnp.float32

    def gain(k, shape):
        return (1.0 + 0.1 * jax.random.normal(k, shape)).astype(f32)

    def dense(k, shape, fan_in):
        return (jax.random.normal(k, shape) * fan_in ** -0.5).astype(f32)

    f_bias = jnp.linspace(3.0, 6.0, N_MLSTM_HEADS)[None, :] + 0.1 * jax.random.normal(ks[4], (DEPTH, N_MLSTM_HEADS))
    i_bias = 0.1 * jax.random.normal(ks[5], (DEPTH, N_MLSTM_HEADS))
    return {
        "x": jax.random.normal(ks[0], (BATCH, SEQ, D_MODEL), f32),
        "pre_mix_norm_w": gain(ks[1], (DEPTH, D_MODEL)),
        "w_in": dense(ks[2], (DEPTH, D_MODEL, D_IN_PROJ), D_MODEL),
        "qk_conv_w": dense(ks[3], (DEPTH, QK_CONV_WIDTH, 2 * D_MLSTM), QK_CONV_WIDTH),
        "qk_conv_b": (0.02 * jax.random.normal(ks[6], (DEPTH, 2 * D_MLSTM))).astype(f32),
        "gate_bias": jnp.concatenate([i_bias, f_bias], axis=-1).astype(f32),
        "mlstm_norm_w": gain(ks[7], (DEPTH, D_MLSTM)),
        "conv_w": dense(ks[8], (DEPTH, CONV_WIDTH, D_CONV), CONV_WIDTH),
        "conv_b": (0.02 * jax.random.normal(ks[9], (DEPTH, D_CONV))).astype(f32),
        "conv_norm_w": gain(ks[10], (DEPTH, D_CONV)),
        "conv_norm_b": (0.02 * jax.random.normal(ks[11], (DEPTH, D_CONV))).astype(f32),
        "w_out": dense(ks[12], (DEPTH, D_MIX, D_MODEL), D_MIX),
        "post_mix_norm_w": gain(ks[13], (DEPTH, D_MODEL)),
        "pre_mlp_norm_w": gain(ks[14], (DEPTH, D_MODEL)),
        "w_ff1": dense(ks[15], (DEPTH, D_MODEL, D_FF), D_MODEL),
        "w_ff2": dense(ks[16], (DEPTH, D_FF, D_MODEL), D_FF),
        "post_mlp_norm_w": gain(ks[17], (DEPTH, D_MODEL)),
    }

def reference(x, pre_mix_norm_w, w_in, qk_conv_w, qk_conv_b, gate_bias, mlstm_norm_w, conv_w, conv_b,
              conv_norm_w, conv_norm_b, w_out, post_mix_norm_w, pre_mlp_norm_w, w_ff1, w_ff2, post_mlp_norm_w):
    B, S, _ = x.shape
    H, dh = N_MLSTM_HEADS, HEAD_DIM
    for layer in range(DEPTH):
        h_in = rms_norm(x, pre_mix_norm_w[layer])
        proj = jnp.einsum("bsd,de->bse", h_in, w_in[layer])
        o1 = 2 * D_MLSTM
        o2 = o1 + D_MLSTM
        o3 = o2 + D_MLSTM
        o4 = o3 + 2 * H
        o5 = o4 + D_CONV
        qk_raw, v_raw, o_pre, gates, conv_val, conv_gate = (
            proj[..., :o1], proj[..., o1:o2], proj[..., o2:o3], proj[..., o3:o4], proj[..., o4:o5], proj[..., o5:])

        qk = jax.nn.silu(causal_depthwise_conv(qk_raw, qk_conv_w[layer], qk_conv_b[layer]))
        q, k = qk[..., :D_MLSTM], qk[..., D_MLSTM:]
        gates = gates.astype(jnp.float32) + gate_bias[layer].astype(jnp.float32)
        i_pre = jnp.transpose(gates[..., :H], (0, 2, 1))
        f_pre = jnp.transpose(gates[..., H:], (0, 2, 1))

        def heads(t):
            return jnp.transpose(t.reshape(B, S, H, dh), (0, 2, 1, 3)).astype(jnp.float32)

        h_tilde = mlstm_chunkwise(heads(q), heads(k), heads(v_raw), i_pre, f_pre)
        mu = jnp.mean(h_tilde, axis=-1, keepdims=True)
        var = jnp.mean(jnp.square(h_tilde - mu), axis=-1, keepdims=True)
        h_norm = (h_tilde - mu) * lax.rsqrt(var + EPS)
        h_norm = jnp.transpose(h_norm, (0, 2, 1, 3)).reshape(B, S, D_MLSTM)
        y_mlstm = (jax.nn.sigmoid(o_pre.astype(jnp.float32)) * h_norm
                   * mlstm_norm_w[layer].astype(jnp.float32)).astype(x.dtype)

        u = conv_val * jax.nn.sigmoid(conv_gate)
        u = causal_depthwise_conv(u, conv_w[layer], conv_b[layer])
        uf = u.astype(jnp.float32).reshape(B, S, N_CONV_GROUPS, CONV_GROUP_DIM)
        mu_c = jnp.mean(uf, axis=-1, keepdims=True)
        var_c = jnp.mean(jnp.square(uf - mu_c), axis=-1, keepdims=True)
        uf = ((uf - mu_c) * lax.rsqrt(var_c + EPS)).reshape(B, S, D_CONV)
        uf = uf * conv_norm_w[layer].astype(jnp.float32) + conv_norm_b[layer].astype(jnp.float32)
        y_conv = jax.nn.silu(uf).astype(x.dtype)

        y = jnp.einsum("bse,ed->bsd", jnp.concatenate([y_mlstm, y_conv], axis=-1), w_out[layer])
        x = x + rms_norm(y, post_mix_norm_w[layer])

        h2 = rms_norm(x, pre_mlp_norm_w[layer])
        a = jax.nn.relu(jnp.einsum("bsd,df->bsf", h2, w_ff1[layer]))
        m_out = jnp.einsum("bsf,fd->bsd", a * a, w_ff2[layer])
        x = x + rms_norm(m_out, post_mlp_norm_w[layer])
    return x


_drawn_inputs = setup_inputs


def setup_inputs(seed=0):
    import zlib

    import numpy as np

    out = dict(_drawn_inputs(seed))
    spreads = {}
    factors = {'qk_conv_b': 4.72, 'conv_norm_b': 4.86}
    for name, (base, spread) in spreads.items():
        noise = np.random.default_rng([zlib.crc32(name.encode()), seed]).standard_normal(out[name].shape)
        drawn = base * np.exp(spread * noise) if base else spread * noise
        out[name] = __import__('jax').numpy.asarray(drawn.astype(out[name].dtype))
    for name, factor in factors.items():
        out[name] = (out[name] * factor).astype(out[name].dtype)
    return out
```

```python
from contextlib import ExitStack

import numpy as np
import concourse.bass as bass
from concourse import mybir
from concourse.alu_op_type import AluOpType as ALU

ACT = mybir.ActivationFunctionType
F32 = mybir.dt.float32
F32R = mybir.dt.float32r

P = 128
S = 2048
D = 1024
KT = D // P
DH = 512
H = 4
HD = 128
FF = 4096
CW = 31
QW = 4
TB = 512
NTB = S // TB
HALF = 1024
NCH = S // P
EPS = 1e-6
SCALE = float(HD) ** -0.5
LN_EXP = "natural_log_exp_and_others"
SILU_TANH = "silu_and_others"
FAR = -1e30

PRE_W, CONV_W, CONV_B, CN_W, CN_B = 0, 8, 8 + H * CW, 8 + H * CW + 4, 8 + H * CW + 8
QKC_W = CN_B + 4
QKC_B = QKC_W + 8 * QW
PAR_A = QKC_B + 8

SLOTS = []
for _g in range(H):
    for _tb in range(NTB):
        SLOTS += [("gate", _g, _tb), ("val", _g, _tb)]
    for _j in (2 * _g, 2 * _g + 1):
        SLOTS += [("qk", _j, _tb) for _tb in range(NTB)]
SLOTS += [("gates", 0, _tb) for _tb in range(NTB)]
SLOTS += [("v", 0, _m) for _m in range(NCH)] + [("o", 0, _m) for _m in range(NCH)]
N_SLOTS = len(SLOTS)
N_TILES = 25
W_RING = 4
VO_HEADS = [1, 2, 3, 0]
BANKS_A = 6
N_UNITS = 2 * H
U_RING = 3


def tile_of(slot):
    kind, n, _ = slot
    return {"gate": 4 * n, "val": 4 * n + 1, "qk": 4 * (n // 2) + 2 + n % 2, "gates": 16, "v": 17, "o": 21}[kind]


def first_use(tile):
    base = tile if tile < 17 else 17 + 4 * ((tile - 17) // 4)
    return min(i for i, s in enumerate(SLOTS) if tile_of(s) == base)


def last_use(tile):
    base = tile if tile < 17 else 17 + 4 * ((tile - 17) // 4)
    return max(i for i, s in enumerate(SLOTS) if tile_of(s) == base)


def split_slot(tile):
    if tile < 4:
        return 0
    return max(first_use(tile) - 5, last_use(tile - W_RING) + 1)


def tiles_split_at(s):
    return [t for t in range(N_TILES) if split_slot(t) == s]


def evacs(s, engine):
    return sum((k == "val") == (engine == "dve") for k, _, _ in SLOTS[: s + 1])


def glu_slot(u):
    return SLOTS.index(("val", u // 2, 2 * (u % 2)))


def tap_plan():
    out = []
    for s in range(N_SLOTS):
        n = max(0, 3 * (s - 3))
        for u in range(U_RING, N_UNITS):
            if s + 1 >= glu_slot(u):
                n = max(n, CW * (u - U_RING + 1))
        out.append(min(n, CW * N_UNITS))
    return out


TAPS = tap_plan()
CONV_END = [min(s for s in range(N_SLOTS) if TAPS[s] >= CW * (u + 1)) for u in range(N_UNITS)]
AT_MEAN, AT_CENTER, AT_SQUARE, AT_VAR, AT_RSTD, AT_NORM, AT_SILU = 1, 2, 3, 4, 5, 6, 7


def units_at(s, step):
    return [u for u in range(N_UNITS) if CONV_END[u] + step == s]


def th_uses(s):
    return sum(k in ("gate", "gates", "v", "o") for k, _, _ in SLOTS[: s + 1])


def th_stores(s, parity):
    n = 0
    for i in range(s + 1):
        k = SLOTS[i][0]
        if k in ("gates", "v", "o") and (th_uses(i) - 1) % 2 == parity:
            n += 2 if k == "gates" else 1
    return n


def last_th_user(s):
    n = th_uses(s) - 1
    for i in range(s):
        if SLOTS[i][0] in ("gate", "gates", "v", "o") and th_uses(i) - 1 == n - 2:
            return i
    return None


def phase_a(nc, sem, psum, dram):
    with ExitStack() as ctx:
        def sb(name, shape, dt=F32):
            return ctx.enter_context(nc.sbuf_tensor(name, shape, dt))

        h_hi = sb("h_hi", [P, KT, S], F32R)
        with nc.sbuf_tensor("x_raw", [P, KT, S], F32) as x_raw:
            pass
        h_lo = sb("h_lo", [P, KT, S], F32R)
        w_hi = sb("w_hi", [P, W_RING, KT, P], F32R)
        with nc.sbuf_tensor("w_raw", [P, W_RING, KT, P], F32) as w_raw:
            pass
        w_lo = sb("w_lo", [P, W_RING, KT, P], F32R)
        par = sb("par_a", [P, PAR_A])
        ones = sb("ones_a", [P, P])
        eps = sb("eps_a", [P, 1])
        th = sb("th", [P, 2, TB])
        qout = sb("qout", [P, HALF])
        rstd = sb("rstd_a", [P, HALF])
        qraw = sb("qraw", [P, 2, QW - 1 + HALF])
        u_buf = sb("u_buf", [P, U_RING, CW - 1 + HALF])
        c_buf = sb("c_buf", [P, 2, HALF])
        ln_ps = psum[:, 6:8, :].rearrange("p a b -> p (a b)")

        def x_at(tb, kt):
            return x_raw[:, kt, tb * TB:(tb + 1) * TB]

        block = ctx.enter_context(nc.Block())

        @block.sync
        def _(sp):
            def load_w(t):
                if t >= W_RING:
                    sp.wait_ge(sem["proj"], last_use(t - W_RING) + 1)
                sp.dma_start(w_raw[:, t % W_RING], dram["w_in"][t]).then_inc(sem["w_raw"][t % W_RING], 16)

            def load_x(tb):
                for half in range(2):
                    kt = slice(half * KT // 2, (half + 1) * KT // 2)
                    cols = slice(tb * TB, (tb + 1) * TB)
                    sp.dma_start(x_raw[:, kt, cols], dram["xt"][:, kt, cols]).then_inc(sem["x_in"][2 * tb + half], 16)

            sp.dma_start(par[:], dram["params_a"]).then_inc(sem["par_a"], 16)
            load_x(0)
            load_w(0)
            load_w(1)
            load_x(1)
            load_w(2)
            load_w(3)
            load_x(2)
            load_x(3)
            for t in range(4, N_TILES):
                load_w(t)

        @block.gpsimd
        def _(pool):
            nc.gpsimd.memset(ones[:], 1.0).then_inc(sem["ones_a"], 1)

        @block.tensor
        def _(pe):
            def sum_squares(tb):
                if tb == 0:
                    pe.wait_ge(sem["ones_a"], 1)
                if tb >= 2:
                    pe.wait_ge(sem["x_rstd"], tb - 1)
                for kt in range(KT):
                    pe.wait_ge(sem["x_sq"], KT * tb + kt + 1)
                    nc.tensor.matmul(psum[:, 6 + tb % 2, :], ones[:], qout[:, (kt % 2) * TB:(kt % 2 + 1) * TB],
                                     start=kt == 0, stop=kt == KT - 1).then_inc(sem["x_sum"], 1)

            def slot(s):
                kind, n, tb = SLOTS[s]
                tile = tile_of(SLOTS[s])
                out = psum[:, s % BANKS_A, :]
                pe.wait_ge(sem["w_hi"], tile + 1 if tile < 17 else tile + 4)
                pe.wait_ge(sem["w_lo"], tile + 1 if tile < 17 else tile + 4)
                if kind in ("gate", "val") and n == 0:
                    pe.wait_ge(sem["h_hi"], KT * (tb + 1))
                    pe.wait_ge(sem["h_lo"], KT * (tb + 1))
                if s >= BANKS_A:
                    by = "dve" if SLOTS[s - BANKS_A][0] == "val" else "act"
                    pe.wait_ge(sem["evac"][by], evacs(s - BANKS_A, by))
                for kt in range(KT):
                    if kind in ("v", "o"):
                        cols = slice(tb * P, (tb + 1) * P)
                        o = out.rearrange("p (a b) -> p a b", a=H)
                        pairs = [(h_hi[:, kt, cols], w_hi[:, :, kt, :]), (h_hi[:, kt, cols], w_lo[:, :, kt, :]),
                                 (h_lo[:, kt, cols], w_hi[:, :, kt, :])]
                    else:
                        cols = slice(tb * TB, (tb + 1) * TB)
                        o, r = out, tile % W_RING
                        pairs = [(w_hi[:, r, kt, :], h_hi[:, kt, cols]), (w_hi[:, r, kt, :], h_lo[:, kt, cols]),
                                 (w_lo[:, r, kt, :], h_hi[:, kt, cols])]
                    for i, (a, b) in enumerate(pairs):
                        mm = nc.tensor.matmul(o, a, b, start=kt == 0 and i == 0, stop=kt == KT - 1 and i == 2)
                mm.then_inc(sem["proj"], 1)

            def group_sum(src, b):
                nc.tensor.matmul(psum[:, 6 + b, :], ones[:], src[:, b * TB:(b + 1) * TB],
                                 start=True, stop=True).then_inc(sem["ln_sum"], 1)

            sum_squares(0)
            sum_squares(1)
            for s in range(N_SLOTS):
                slot(s)
                if s in (1, 3):
                    sum_squares(2 + s // 2)
                for u in units_at(s, AT_MEAN):
                    pe.wait_ge(sem["tap"], CW * (u + 1))
                    if u == 0:
                        pe.wait_ge(sem["x_rstd"], NTB)
                    else:
                        pe.wait_ge(sem["c_rstd"], 2 * u)
                    for b in range(2):
                        group_sum(c_buf[:, u % 2], b)
                for u in units_at(s, AT_VAR):
                    pe.wait_ge(sem["c_sq"], u + 1)
                    for b in range(2):
                        group_sum(rstd, b)

        @block.scalar
        def _(act):
            def normalise_x(tb):
                for kt in range(KT):
                    n = KT * tb + kt
                    act.wait_ge(sem["x_in"][2 * tb + kt // (KT // 2)], 16)
                    if n >= 2:
                        act.wait_ge(sem["x_sum"], n - 1)
                    nc.scalar.activation(qout[:, (kt % 2) * TB:(kt % 2 + 1) * TB], x_at(tb, kt),
                                         ACT.Square).then_inc(sem["x_sq"], 1)
                r = rstd[:, (tb % 2) * TB:(tb % 2 + 1) * TB]
                act.wait_ge(sem["x_sum"], KT * (tb + 1))
                if tb >= 2:
                    act.wait_ge(sem["h"], KT * (tb - 1))
                nc.scalar.activation(r, psum[:, 6 + tb % 2, :], ACT.Ln, scale=1.0 / D, bias=eps[:, 0:1]).then_inc(sem["x_ln"], 1)
                act.wait_ge(sem["x_ln"], tb + 1)
                nc.scalar.activation(r, r, ACT.Exp, scale=-0.5).then_inc(sem["x_rstd"], 1)
                for kt in range(KT):
                    act.wait_ge(sem["h"], KT * tb + kt + 1)
                    nc.scalar.activation(h_hi[:, kt, tb * TB:(tb + 1) * TB], x_at(tb, kt),
                                         ACT.Copy).then_inc(sem["h_hi"], 1)

            def split_w(t):
                act.wait_ge(sem["w_raw"][t % W_RING], 16 * (t // W_RING + 1))
                nc.scalar.activation(w_hi[:, t % W_RING], w_raw[:, t % W_RING], ACT.Copy).then_inc(sem["w_hi"], 1)

            def evacuate(s):
                kind, n, tb = SLOTS[s]
                if kind == "val":
                    return
                ps = psum[:, s % BANKS_A, :]
                act.wait_ge(sem["proj"], s + 1)
                if kind == "qk":
                    half = tb // 2
                    if n >= 1 and tb % 2 == 0:
                        act.wait_ge(sem["q_tap"], 9 * (n - 1) + (5 if half == 0 else 9))
                    at = QW - 1 + (tb % 2) * TB
                    nc.scalar.activation(qraw[:, half, at:at + TB], ps, ACT.Copy).then_inc(sem["evac"]["act"], 1)
                    return
                k = (th_uses(s) - 1) % 2
                before = last_th_user(s)
                if before is not None:
                    if SLOTS[before][0] == "gate":
                        act.wait_ge(sem["evac"]["dve"], evacs(before + 1, "dve"))
                    else:
                        act.wait_ge(sem["th_out"][k], 16 * th_stores(before, k))
                if kind == "gate":
                    nc.scalar.activation(th[:, k, :], ps, ACT.Tanh, scale=0.5).then_inc(sem["evac"]["act"], 1)
                    return
                rows = slice(0, 36) if kind == "gates" else slice(0, P)
                nc.scalar.activation(th[rows, k, :], ps[rows], ACT.Tanh if kind == "o" else ACT.Copy,
                                     scale=0.5 if kind == "o" else 1.0).then_inc(sem["evac"]["act"], 1)
                act.wait_ge(sem["evac"]["act"], evacs(s, "act"))
                if kind == "gates":
                    for half in range(2):
                        act.dma_start(dram["gates"][4 * half:4 * half + 4, tb * TB:(tb + 1) * TB],
                                      th[32 * half:32 * half + 4, k, :]).then_inc(sem["th_out"][k], 16)
                else:
                    act.dma_start(dram["v"][tb] if kind == "v" else dram["o"][tb], th[:, k, :]).then_inc(sem["th_out"][k], 16)

            def silu_qk(s):
                _, j, tb = SLOTS[s]
                half = tb // 2
                act.wait_ge(sem["q_tap"], 9 * j + (5 if half == 0 else 9))
                nc.scalar.activation(qout[:], qout[:], ACT.Silu,
                                     bias=par[:, QKC_B + j:QKC_B + j + 1]).then_inc(sem["q_silu"], 1)
                act.wait_ge(sem["q_silu"], 2 * j + half + 1)
                act.dma_start(dram["qk"][j, :, half * HALF:(half + 1) * HALF], qout[:]).then_inc(sem["q_out"], 16)

            nc.scalar.preload_act_table_set(LN_EXP)
            act.wait_ge(sem["par_a"], 16)
            act.wait_ge(sem["eps_a"], 1)
            normalise_x(0)
            split_w(0)
            split_w(1)
            normalise_x(1)
            split_w(2)
            split_w(3)
            nc.scalar.preload_act_table_set(SILU_TANH)
            for s in range(N_SLOTS):
                for t in tiles_split_at(s):
                    if t >= 4:
                        split_w(t)
                evacuate(s)
                if s in (1, 3):
                    nc.scalar.preload_act_table_set(LN_EXP)
                    normalise_x(2 + s // 2)
                    nc.scalar.preload_act_table_set(SILU_TANH)
                for u in units_at(s, AT_SQUARE):
                    act.wait_ge(sem["c_center"], u + 1)
                    if u >= 1:
                        act.wait_ge(sem["c_norm"], u)
                    nc.scalar.activation(rstd[:], c_buf[:, u % 2], ACT.Square).then_inc(sem["c_sq"], 1)
                for u in units_at(s, AT_RSTD):
                    nc.scalar.preload_act_table_set(LN_EXP)
                    act.wait_ge(sem["ln_sum"], 4 * u + 4)
                    nc.scalar.activation(rstd[:], ln_ps, ACT.Ln, scale=1.0 / P, bias=eps[:, 0:1]).then_inc(sem["c_rstd"], 1)
                    act.wait_ge(sem["c_rstd"], 2 * u + 1)
                    nc.scalar.activation(rstd[:], rstd[:], ACT.Exp, scale=-0.5).then_inc(sem["c_rstd"], 1)
                    nc.scalar.preload_act_table_set(SILU_TANH)
                for u in units_at(s, AT_SILU):
                    g, half = u // 2, u % 2
                    act.wait_ge(sem["c_norm"], u + 1)
                    nc.scalar.activation(c_buf[:, u % 2], c_buf[:, u % 2], ACT.Silu, scale=par[:, CN_W + g:CN_W + g + 1],
                                         bias=par[:, CN_B + g:CN_B + g + 1]).then_inc(sem["c_silu"], 1)
                    act.wait_ge(sem["c_silu"], u + 1)
                    act.dma_start(dram["yc"][g, :, half * HALF:(half + 1) * HALF], c_buf[:, u % 2]).then_inc(sem["c_out"][u % 2], 16)
                if s >= 2 and SLOTS[s - 2][0] == "qk" and SLOTS[s - 2][2] % 2 == 1:
                    silu_qk(s - 2)
            for k in range(2):
                act.wait_ge(sem["th_out"][k], 16 * th_stores(N_SLOTS - 1, k))
                act.wait_ge(sem["c_out"][k], 16 * (N_UNITS // 2))
            act.wait_ge(sem["q_out"], 16 * 16)

        @block.vector
        def _(dve):
            self_n = [0]

            def link(ins):
                self_n[0] += 1
                ins.then_inc(sem["dve_a"], 1)
                dve.wait_ge(sem["dve_a"], self_n[0])

            def normalise_x(tb):
                dve.wait_ge(sem["x_rstd"], tb + 1)
                r = rstd[:, (tb % 2) * TB:(tb % 2 + 1) * TB]

                def low(kt):
                    cols = slice(tb * TB, (tb + 1) * TB)
                    dve.wait_ge(sem["h_hi"], KT * tb + kt + 1)
                    nc.vector.tensor_tensor(h_lo[:, kt, cols], x_at(tb, kt), h_hi[:, kt, cols].bitcast(F32),
                                            ALU.subtract).then_inc(sem["h_lo"], 1)

                for kt in range(KT):
                    x = x_at(tb, kt)
                    nc.vector.scalar_tensor_tensor(out=x, in0=x, scalar=par[:, PRE_W + kt:PRE_W + kt + 1], in1=r,
                                                   op0=ALU.mult, op1=ALU.mult).then_inc(sem["h"], 1)
                    if kt >= 1:
                        low(kt - 1)
                low(KT - 1)

            def split_w(t):
                dve.wait_ge(sem["w_hi"], t + 1)
                nc.vector.tensor_tensor(w_lo[:, t % W_RING], w_raw[:, t % W_RING], w_hi[:, t % W_RING].bitcast(F32),
                                        ALU.subtract).then_inc(sem["w_lo"], 1)

            def glu(s):
                _, g, tb = SLOTS[s]
                u = 2 * g + tb // 2
                at = CW - 1 + (tb % 2) * TB
                if tb % 2 == 0 and u >= U_RING:
                    dve.wait_ge(sem["tap"], CW * (u - U_RING + 1))
                if tb == 0:
                    nc.vector.memset(u_buf[:, u % U_RING, 0:CW - 1], 0.0).then_inc(sem["u_head"], 1)
                elif tb == 2:
                    nc.vector.tensor_copy(u_buf[:, u % U_RING, 0:CW - 1],
                                          u_buf[:, (u - 1) % U_RING, HALF:HALF + CW - 1]).then_inc(sem["u_head"], 1)
                dve.wait_ge(sem["proj"], s + 1)
                dve.wait_ge(sem["evac"]["act"], evacs(s - 1, "act"))
                nc.vector.scalar_tensor_tensor(out=u_buf[:, u % U_RING, at:at + TB], in0=th[:, (th_uses(s) - 1) % 2, :],
                                               scalar=1.0, in1=psum[:, s % BANKS_A, :], op0=ALU.add,
                                               op1=ALU.mult).then_inc(sem["evac"]["dve"], 1)

            def tap(n):
                u, k = n // CW, n % CW
                g = u // 2
                out, src = c_buf[:, u % 2], u_buf[:, u % U_RING, k:k + HALF]
                w = par[:, CONV_W + g * CW + k:CONV_W + g * CW + k + 1]
                if k == 0:
                    dve.wait_ge(sem["evac"]["dve"], 2 * (u + 1))
                    dve.wait_ge(sem["u_head"], u + 1)
                    if u >= 2:
                        dve.wait_ge(sem["c_out"][u % 2], 16 * (u // 2))
                    nc.vector.tensor_scalar(out, src, w, par[:, CONV_B + g:CONV_B + g + 1],
                                            ALU.mult, ALU.add).then_inc(sem["tap"], 1)
                else:
                    dve.wait_ge(sem["tap"], n)
                    nc.vector.scalar_tensor_tensor(out=out, in0=src, scalar=w, in1=out, op0=ALU.mult,
                                                   op1=ALU.add).then_inc(sem["tap"], 1)

            def convolve_qk(s):
                _, j, tb = SLOTS[s]
                half = tb // 2
                dve.wait_ge(sem["evac"]["act"], evacs(s, "act"))
                if 2 * j + half >= 1:
                    dve.wait_ge(sem["q_out"], 16 * (2 * j + half))
                for k in range(QW):
                    w = par[:, QKC_W + j * QW + k:QKC_W + j * QW + k + 1]
                    src = qraw[:, half, k:k + HALF]
                    if k == 0:
                        nc.vector.tensor_scalar(qout[:], src, w, None, ALU.mult).then_inc(sem["q_tap"], 1)
                    else:
                        dve.wait_ge(sem["q_tap"], 9 * j + 5 * half + k)
                        nc.vector.scalar_tensor_tensor(out=qout[:], in0=src, scalar=w, in1=qout[:], op0=ALU.mult,
                                                       op1=ALU.add).then_inc(sem["q_tap"], 1)
                if half == 0:
                    nc.vector.tensor_copy(qraw[:, 1, 0:QW - 1], qraw[:, 0, HALF:HALF + QW - 1]).then_inc(sem["q_tap"], 1)

            nc.vector.memset(eps[:], EPS).then_inc(sem["eps_a"], 1)
            dve.wait_ge(sem["par_a"], 16)
            link(nc.vector.tensor_scalar(par[:, CONV_W:CONV_W + H * CW], par[:, CONV_W:CONV_W + H * CW], 0.5, None, ALU.mult))
            normalise_x(0)
            split_w(0)
            split_w(1)
            normalise_x(1)
            split_w(2)
            split_w(3)
            for s in range(N_SLOTS):
                for t in tiles_split_at(s):
                    if t >= 4:
                        split_w(t)
                if SLOTS[s][0] == "val":
                    glu(s)
                if s in (1, 3):
                    normalise_x(2 + s // 2)
                if s == 0:
                    link(nc.vector.memset(qraw[:, 0, 0:QW - 1], 0.0))
                for n in range(TAPS[s - 1] if s else 0, TAPS[s]):
                    tap(n)
                if s >= 1 and SLOTS[s - 1][0] == "qk" and SLOTS[s - 1][2] % 2 == 1:
                    convolve_qk(s - 1)
                for u in units_at(s, AT_CENTER):
                    dve.wait_ge(sem["ln_sum"], 4 * u + 2)
                    nc.vector.scalar_tensor_tensor(out=c_buf[:, u % 2], in0=ln_ps, scalar=-1.0 / P, in1=c_buf[:, u % 2],
                                                   op0=ALU.mult, op1=ALU.add).then_inc(sem["c_center"], 1)
                for u in units_at(s, AT_NORM):
                    dve.wait_ge(sem["c_rstd"], 2 * u + 2)
                    nc.vector.tensor_tensor(c_buf[:, u % 2], c_buf[:, u % 2], rstd[:], ALU.mult).then_inc(sem["c_norm"], 1)


WO_SCALE = 0
PAR_B = 8
COL_A, COL_WK, COL_FLOOR = 0, 1, 2
VW = HD + 1


def phase_b(nc, sem, psum, dram):
    with ExitStack() as ctx:
        def sb(name, shape, dt=F32):
            return ctx.enter_context(nc.sbuf_tensor(name, shape, dt))

        wo_hi = sb("wo_hi", [P, KT, D], F32R)
        with nc.sbuf_tensor("wo_raw", [P, KT, D], F32) as wo_raw:
            pass
        wo_lo = sb("wo_lo", [P, KT, D], F32R)
        par = sb("par_b", [P, PAR_B])
        ident = sb("ident", [P, P])
        mask = sb("mask", [P, P])
        post_w = sb("post_w_sb", [P, D])
        cols = sb("cols", [P, NCH, 4, H])
        decay_b = sb("decay_b", [P, H, NCH])
        state = sb("state", [P, H, VW])
        eps = sb("eps_b", [P, 1])
        with ExitStack() as early:
            def row(name, parts=H):
                return early.enter_context(nc.sbuf_tensor(name, [parts, S], F32))

            gi, gf, t0, t1, t2, keep, step = (row(n) for n in ("gi", "gf", "t0", "t1", "t2", "keep", "step"))
            rows = row("rows", P)
            m_prev = early.enter_context(nc.sbuf_tensor("m_prev", [H, NCH], F32))
            decay = early.enter_context(nc.sbuf_tensor("decay", [H, NCH], F32))
            gate_bias = early.enter_context(nc.sbuf_tensor("gate_bias", [H, 2], F32))
        q_t = sb("q_t", [P, 2, H, P])
        k_t = sb("k_t", [P, 2, H, P])
        v_c = sb("v_c", [P, 2, H, VW])
        o_c = sb("o_c", [P, 2, DH])
        negm_b = sb("negm_b", [P, 2, H, P])
        winter_b = sb("winter_b", [P, 2, H, P])
        yc_c = sb("yc_c", [P, 2, H, P])
        x_c = sb("x_c", [P, 2, D])
        e_c = sb("e_c", [P, H, P])
        p_c = sb("p_c", [P, H, P])
        qs_c = sb("qs_c", [P, H, P])
        wk_c = sb("wk_c", [P, H, P])
        y_c = sb("y_c", [P, DH])
        y_hi = sb("y_hi", [P, 2, KT, P], F32R)
        y_lo = sb("y_lo", [P, 2, KT, P], F32R)
        small = sb("small", [P, 64])
        junk = sb("junk", [P, TB])
        t_post = sb("t_post", [P, D])
        xn = sb("xn", [P, 2, D])
        h2 = sb("h2", [P, D])
        h2_hi = sb("h2_hi", [P, 2, KT, P], F32R)
        h2_lo = sb("h2_lo", [P, 2, KT, P], F32R)
        den, rden, stats, aggr = small[:, 0:4], small[:, 4:8], small[:, 8:32], small[:, 32:40]
        var_h, rs_h, s_h = small[:, 40:44], small[:, 44:48], small[:, 48:52]
        ss, ss2, r1, r2 = small[:, 52:54], small[:, 54:56], small[:, 56:57], small[:, 57:58]

        block = ctx.enter_context(nc.Block())

        def by_head(a):
            return a.rearrange("p (h d) -> p h d", h=H)

        def head_ps(bank, h):
            return psum[:, bank + h // 2, (h % 2) * VW:(h % 2 + 1) * VW]

        @block.sync
        def _(sp):
            sp.dma_start(gi[:], dram["gates"][0:H]).then_inc(sem["gates_in"], 16)
            sp.dma_start(gf[:], dram["gates"][H:2 * H]).then_inc(sem["gates_in"], 16)
            sp.dma_start(gate_bias[:], dram["gate_bias"]).then_inc(sem["gates_in"], 16)
            sp.dma_start(par[:], dram["params_b"]).then_inc(sem["par_b"], 16)
            sp.dma_start(post_w[:], dram["post_w"].partition_broadcast(P)).then_inc(sem["par_b"], 16)
            for kt in range(KT):
                sp.dma_start(wo_raw[:, kt], dram["w_out"][kt]).then_inc(sem["wo_in"][kt], 16)
            sp.wait_ge(sem["rows_done"], 4)
            sp.dma_start(dram["rows"][0], t0[:]).then_inc(sem["rows_out"], 16)
            sp.dma_start(dram["rows"][1], t1[:]).then_inc(sem["rows_out"], 16)
            sp.dma_start(dram["decay"], decay[:]).then_inc(sem["rows_out"], 16)
            sp.wait_ge(sem["rows_out"], 48)
            sp.dma_start(decay_b[:], dram["decay"].partition_broadcast(P)).then_inc(sem["decay_in"], 16)
            sp.wait_ge(sem["cols_done"], 4)

            def load(c):
                b = c % 2
                at = slice(c * P, (c + 1) * P)
                if c >= 2:
                    sp.wait_ge(sem["scores"], c - 1)
                    sp.wait_ge(sem["qs"], c - 1)
                    sp.wait_ge(sem["z"], c - 1)
                    sp.wait_ge(sem["incr"], c - 1)
                    sp.wait_ge(sem["y"], c - 1)
                    sp.wait_ge(sem["yc_lo"], c - 1)
                for buf, src, s in ((q_t, dram["qk"][0:4, :, at], 0), (k_t, dram["qk"][4:8, :, at], 1),
                                    (yc_c, dram["yc"][:, :, at], 2)):
                    sp.dma_start(buf[:, b], src.rearrange("h p t -> p h t")).then_inc(sem["chunk_in"][b], 16)
                sp.dma_start(v_c[:, b, :, 0:HD], by_head(dram["v"][c])).then_inc(sem["chunk_in"][b], 16)
                sp.dma_start(o_c[:, b], dram["o"][c]).then_inc(sem["chunk_in"][b], 16)
                for buf, n in ((negm_b, 0), (winter_b, 1)):
                    sp.dma_start(buf[:, b], dram["rows"][n, :, at].partition_broadcast(P)).then_inc(sem["chunk_in"][b], 16)

            def load_x(c):
                if c >= 2:
                    sp.wait_ge(sem["xn"], c - 1)
                sp.dma_start(x_c[:, c % 2], dram["x"][c * P:(c + 1) * P]).then_inc(sem["xc_in_b"][c % 2], 16)

            load(0)
            for c in range(NCH + 4):
                if c >= 4:
                    sp.wait_ge(sem["h2_lo"], 2 * (c - 3))
                    at = slice((c - 4) * P, (c - 3) * P)
                    for buf, out in ((h2_hi, dram["h2_hi"]), (h2_lo, dram["h2_lo"])):
                        sp.dma_start(out[:, :, at], buf[:, c % 2].bitcast(F32)).then_inc(sem["h2_out"][c % 2], 16)
                if c + 1 < NCH:
                    load(c + 1)
                if c < NCH:
                    load_x(c)
                if 0 <= c - 2 < NCH:
                    sp.wait_ge(sem["xn"], c - 1)
                    sp.dma_start(dram["xn"][c - 2], xn[:, c % 2]).then_inc(sem["xn_out"][c % 2], 16)
            for b in range(2):
                sp.wait_ge(sem["h2_out"][b], 32 * NCH // 2)
                sp.wait_ge(sem["xn_out"][b], 16 * NCH // 2)

        def chunk_here(eng, c):
            eng.wait_ge(sem["chunk_in"][c % 2], 7 * 16 * (c // 2 + 1))

        @block.gpsimd
        def _(pool):
            nc.gpsimd.memset(ident[:], 0.0).then_inc(sem["ident"], 1)
            nc.gpsimd.memset(mask[:], 0.0).then_inc(sem["ident"], 1)
            nc.gpsimd.memset(rows[:], 0.0).then_inc(sem["ident"], 1)
            pool.wait_ge(sem["ident"], 3)
            nc.gpsimd.affine_select(out=ident[:], in_=ident[:], compare_op=ALU.not_equal, fill=1.0, base=0,
                                    pattern=[[-1, P]], channel_multiplier=1).then_inc(sem["ident"], 1)
            nc.gpsimd.affine_select(out=mask[:], in_=mask[:], compare_op=ALU.is_ge, fill=FAR, base=0,
                                    pattern=[[1, P]], channel_multiplier=-1).then_inc(sem["ident"], 1)
            pool.wait_ge(sem["rows_out"], 48)
            pool.wait_ge(sem["cols_done"], 4)
            nc.gpsimd.memset(v_c[:, :, :, HD:VW], 1.0).then_inc(sem["v_ones"], 1)
            for c in range(NCH):
                chunk_here(pool, c)
                if c >= 1:
                    pool.wait_ge(sem["num"], c)
                nc.gpsimd.tensor_tensor(qs_c[:], q_t[:, c % 2], winter_b[:, c % 2], ALU.mult).then_inc(sem["qs"], 1)

        @block.tensor
        def _(pe):
            def scores(c):
                chunk_here(pe, c)
                if c >= 1:
                    pe.wait_ge(sem["p"], c)
                    pe.wait_ge(sem["wk"], c)
                for h in range(H):
                    mm = nc.tensor.matmul(psum[:, 0, h * P:(h + 1) * P], k_t[:, c % 2, h], q_t[:, c % 2, h],
                                          start=True, stop=True)
                for h in range(H):
                    mm = nc.tensor.transpose(psum[:, 1, h * P:(h + 1) * P], k_t[:, c % 2, h], ident[:])
                mm.then_inc(sem["scores"], 1)

            def numerators(c):
                pe.wait_ge(sem["p"], c + 1)
                pe.wait_ge(sem["qs"], c + 1)
                pe.wait_ge(sem["wk"], c + 1)
                if c == 0:
                    pe.wait_ge(sem["v_ones"], 1)
                if c >= 1:
                    pe.wait_ge(sem["y_lo"], c)
                pe.wait_ge(sem["state"], c + 1)
                if c >= 4:
                    pe.wait_ge(sem["h2_lo"], 2 * (c - 3))
                for h in range(H):
                    nc.tensor.matmul(head_ps(2, h), p_c[:, h], v_c[:, c % 2, h], start=True, stop=False)
                    mm = nc.tensor.matmul(head_ps(2, h), qs_c[:, h], state[:, h], start=False, stop=True)
                mm.then_inc(sem["num"], 1)
                for h in range(H):
                    mm = nc.tensor.matmul(head_ps(4, h), wk_c[:, h], v_c[:, c % 2, h], start=True, stop=True)
                mm.then_inc(sem["incr"], 1)

            def transpose_y(c):
                pe.wait_ge(sem["y"], c + 1)
                for h in range(H):
                    mm = nc.tensor.transpose(psum[:, 2, h * P:(h + 1) * P], y_c[:, h * P:(h + 1) * P], ident[:])
                mm.then_inc(sem["y_t"], 1)

            def project(c, half):
                b = c % 2
                if half == 0:
                    pe.wait_ge(sem["y_hi"], c + 1)
                    pe.wait_ge(sem["y_lo"], c + 1)
                    pe.wait_ge(sem["yc_hi"], c + 1)
                    pe.wait_ge(sem["yc_lo"], c + 1)
                if c == 0:
                    pe.wait_ge(sem["wo_lo"], KT)
                    pe.wait_ge(sem["wo_hi"], KT)
                else:
                    pe.wait_ge(sem["t_post"], 2 * (c - 1) + half + 1)
                    pe.wait_ge(sem["ss"], 2 * (c - 1) + half + 1)
                cols_ = slice(half * TB, (half + 1) * TB)
                for kt in range(KT):
                    pairs = [(y_hi[:, b, kt], wo_hi[:, kt, cols_]), (y_hi[:, b, kt], wo_lo[:, kt, cols_]),
                             (y_lo[:, b, kt], wo_hi[:, kt, cols_])]
                    for i, (l, r) in enumerate(pairs):
                        mm = nc.tensor.matmul(psum[:, 6 + half, :], l, r, start=kt == 0 and i == 0,
                                              stop=kt == KT - 1 and i == 2)
                mm.then_inc(sem["out_proj"], 1)

            def transpose_h2(c):
                pe.wait_ge(sem["h2"], c + 1)
                if c >= 1:
                    pe.wait_ge(sem["h2_lo"], 2 * c)
                pe.wait_ge(sem["state"], min(c + 4, NCH) + 1)
                for kt in range(KT):
                    mm = nc.tensor.transpose(psum[:, 4 + kt // 4, (kt % 4) * P:(kt % 4 + 1) * P], h2[:, kt * P:(kt + 1) * P],
                                             ident[:])
                    if kt % 4 == 3:
                        mm.then_inc(sem["h2_t"], 1)

            pe.wait_ge(sem["ident"], 5)
            pe.wait_ge(sem["rows_done"], 4)
            for c in range(NCH):
                nc_bank = c // 4
                mm = nc.tensor.transpose(psum[:, nc_bank, (c % 4) * P:(c % 4 + 1) * P], rows[:, c * P:(c + 1) * P], ident[:])
                if c % 4 == 3:
                    mm.then_inc(sem["cols_t"], 1)
            pe.wait_ge(sem["cols_done"], 4)
            scores(0)
            for c in range(NCH + 3):
                if c < NCH:
                    numerators(c)
                if 1 <= c <= NCH:
                    project(c - 1, 0)
                if c + 1 < NCH:
                    scores(c + 1)
                if c < NCH:
                    transpose_y(c)
                if c >= 3:
                    transpose_h2(c - 3)
                if 1 <= c <= NCH:
                    project(c - 1, 1)

        @block.scalar
        def _(act):
            n_self = [0]

            def link(ins):
                n_self[0] += 1
                ins.then_inc(sem["act_b"], 1)
                act.wait_ge(sem["act_b"], n_self[0])

            def rsqrt(out, in_, scale, signal):
                link(nc.scalar.activation(out, in_, ACT.Ln, scale=scale, bias=eps[:, 0:1]))
                nc.scalar.activation(out, out, ACT.Exp, scale=-0.5).then_inc(signal, 1)

            nc.scalar.preload_act_table_set(LN_EXP)
            act.wait_ge(sem["gates_in"], 48)
            link(nc.scalar.activation(gf[:], gf[:], ACT.Identity, bias=gate_bias[:, 1:2]))
            link(nc.scalar.activation(t0[:], gf[:], ACT.Abs))
            link(nc.scalar.activation(t0[:], t0[:], ACT.Exp, scale=-1.0))
            nc.scalar.activation(t0[:], t0[:], ACT.Ln, bias=1.0).then_inc(sem["softplus"], 1)

            def split_wo(kt):
                act.wait_ge(sem["wo_in"][kt], 16)
                nc.scalar.activation(wo_hi[:, kt], wo_raw[:, kt], ACT.Copy,
                                     scale=par[:, WO_SCALE + kt:WO_SCALE + kt + 1]).then_inc(sem["wo_hi"], 1)

            act.wait_ge(sem["wo_scale"], 1)
            for kt in range(KT):
                split_wo(kt)
            act.wait_ge(sem["ident"], 3)
            act.wait_ge(sem["exps"], 1)
            nc.scalar.activation(t1[:], t1[:], ACT.Exp).then_inc(sem["exps_out"], 1)
            act.wait_ge(sem["exps"], 2)
            nc.scalar.activation(rows[32 * COL_WK:32 * COL_WK + H, :], t2[:], ACT.Exp).then_inc(sem["rows_done"], 1)
            nc.scalar.activation(rows[32 * COL_FLOOR:32 * COL_FLOOR + H, :], gf[:], ACT.Exp).then_inc(sem["rows_done"], 1)
            nc.scalar.activation(decay[:], decay[:], ACT.Exp).then_inc(sem["rows_done"], 1)

            def weights(c):
                act.wait_ge(sem["z"], c + 1)
                if c >= 1:
                    act.wait_ge(sem["p"], c)
                nc.scalar.activation(e_c[:], p_c[:], ACT.Exp).then_inc(sem["e"], 1)

            def wk(c):
                act.wait_ge(sem["scores"], c + 1)
                if c >= 1:
                    act.wait_ge(sem["incr"], c)
                for h in range(H):
                    a = nc.scalar.activation(wk_c[:, h], psum[:, 1, h * P:(h + 1) * P], ACT.Copy,
                                             scale=cols[:, c, COL_WK, h:h + 1])
                a.then_inc(sem["wk"], 1)

            def yc_high(c):
                if c >= 2:
                    act.wait_ge(sem["out_proj"], 2 * (c - 1))
                nc.scalar.activation(y_hi[:, c % 2, H:KT], yc_c[:, c % 2], ACT.Copy).then_inc(sem["yc_hi"], 1)

            def denominators(c):
                act.wait_ge(sem["num"], c + 1)
                if c >= 1:
                    act.wait_ge(sem["y"], c)
                for bank in range(2):
                    a = nc.scalar.activation(den[:, 2 * bank:2 * bank + 2], psum[:, 2 + bank, HD:2 * VW:VW], ACT.Abs)
                a.then_inc(sem["den"], 1)

            def squares(c, half):
                act.wait_ge(sem["out_proj"], 2 * c + half + 1)
                if half:
                    act.wait_ge(sem["ss"], 2 * c + 1)
                elif c >= 1:
                    act.wait_ge(sem["ss_sum"], c)
                    act.wait_ge(sem["ss2"], 2 * c)
                nc.scalar.activation(junk[:], psum[:, 6 + half, :], ACT.Square,
                                     accum_out=ss[:, half:half + 1]).then_inc(sem["ss"], 1)

            def pre_mlp_squares(c):
                act.wait_ge(sem["xn"], c + 1)
                for half in range(2):
                    act.wait_ge(sem["ss"], 2 * c + 2)
                    if half:
                        act.wait_ge(sem["ss2"], 2 * c + 1)
                    nc.scalar.activation(junk[:], xn[:, c % 2, half * TB:(half + 1) * TB], ACT.Square,
                                         accum_out=ss2[:, half:half + 1]).then_inc(sem["ss2"], 1)

            def pre_mlp(c):
                act.wait_ge(sem["ss2_sum"], c + 1)
                rsqrt(r2, r2, 1.0 / D, sem["r2"])
                act.wait_ge(sem["r2"], c + 1)
                if c >= 1:
                    act.wait_ge(sem["h2_t"], 2 * c)
                nc.scalar.activation(h2[:], xn[:, c % 2], ACT.Copy, scale=r2).then_inc(sem["h2"], 1)

            def h2_high(c):
                for b in range(2):
                    act.wait_ge(sem["h2_t"], 2 * c + b + 1)
                    if c >= 2:
                        act.wait_ge(sem["h2_out"][c % 2], 32 * (c // 2))
                    nc.scalar.activation(h2_hi[:, c % 2, 4 * b:4 * b + 4], by_head(psum[:, 4 + b, :]), ACT.Copy).then_inc(sem["h2_hi"], 1)

            act.wait_ge(sem["eps_b"], 1)
            weights(0)
            wk(0)
            yc_high(0)
            for c in range(NCH + 3):
                if c < NCH:
                    denominators(c)
                    act.wait_ge(sem["var_h"], c + 1)
                    rsqrt(rs_h, var_h, 1.0, sem["rs_h"])
                if c + 1 < NCH:
                    weights(c + 1)
                if 2 <= c < NCH + 2:
                    pre_mlp_squares(c - 2)
                if 1 <= c <= NCH:
                    squares(c - 1, 0)
                if c + 1 < NCH:
                    wk(c + 1)
                if c < NCH:
                    act.wait_ge(sem["y_t"], c + 1)
                    nc.scalar.activation(y_hi[:, c % 2, 0:H], by_head(psum[:, 2, :]), ACT.Copy).then_inc(sem["y_hi"], 1)
                if c >= 3:
                    h2_high(c - 3)
                if 2 <= c < NCH + 2:
                    pre_mlp(c - 2)
                if 1 <= c <= NCH:
                    squares(c - 1, 1)
                if c + 1 < NCH:
                    yc_high(c + 1)
                if 1 <= c <= NCH:
                    act.wait_ge(sem["ss_sum"], c)
                    rsqrt(r1, r1, 1.0 / D, sem["r1"])

        @block.vector
        def _(dve):
            n_self = [0]

            def link(ins):
                n_self[0] += 1
                ins.then_inc(sem["dve_b"], 1)
                dve.wait_ge(sem["dve_b"], n_self[0])

            def by_chunk(a):
                return a.rearrange("p (c l) -> p c l", l=P)

            nc.vector.memset(eps[:], EPS).then_inc(sem["eps_b"], 1)
            link(nc.vector.memset(keep[:], 1.0))
            link(nc.vector.memset(by_chunk(keep[:])[:, :, 0:1], 0.0))
            link(nc.vector.memset(step[:], 0.0))
            link(nc.vector.memset(m_prev[:], 0.0))
            nc.vector.memset(state[:], 0.0).then_inc(sem["state"], 1)
            dve.wait_ge(sem["par_b"], 32)
            nc.vector.tensor_scalar(par[:, WO_SCALE:WO_SCALE + H], par[:, WO_SCALE:WO_SCALE + H], 0.5, None,
                                    ALU.mult).then_inc(sem["wo_scale"], 1)
            dve.wait_ge(sem["gates_in"], 48)
            link(nc.vector.tensor_scalar(gi[:], gi[:], gate_bias[:, 0:1], None, ALU.add))
            dve.wait_ge(sem["softplus"], 1)
            link(nc.vector.scalar_tensor_tensor(out=gf[:], in0=gf[:], scalar=0.0, in1=t0[:], op0=ALU.min,
                                                op1=ALU.subtract))
            link(nc.vector.tensor_tensor_scan(t1[:], keep[:], gf[:], 0.0, ALU.mult, ALU.add))
            link(nc.vector.tensor_copy(by_chunk(step[:])[:, 1:NCH, 0:1], by_chunk(t1[:])[:, 0:NCH - 1, P - 1:P]))
            dve.wait_ge(sem["ident"], 3)
            a_row = rows[32 * COL_A:32 * COL_A + H, :]
            link(nc.vector.tensor_tensor(a_row, gi[:], t1[:], ALU.subtract))
            link(nc.vector.tensor_tensor_scan(t2[:], step[:], a_row, 0.0, ALU.add, ALU.max))
            last = by_chunk(t2[:])[:, :, P - 1:P]
            link(nc.vector.tensor_tensor(m_prev[:, 1:NCH].unsqueeze(2), by_chunk(t1[:])[:, 0:NCH - 1, P - 1:P],
                                         last[:, 0:NCH - 1], ALU.add))
            link(nc.vector.tensor_tensor(decay[:].unsqueeze(2), m_prev[:].unsqueeze(2), last, ALU.subtract))
            link(nc.vector.tensor_scalar(t0[:], t2[:], -1.0, None, ALU.mult))
            link(nc.vector.tensor_tensor(gf[:], t0[:], t1[:], ALU.subtract))
            nc.vector.tensor_tensor(by_chunk(t1[:]), by_chunk(t0[:]), m_prev[:].unsqueeze(2).to_broadcast([H, NCH, P]),
                                    ALU.add).then_inc(sem["exps"], 1)
            nc.vector.tensor_copy(gi[:, 0:NCH].unsqueeze(2), last).then_inc(sem["gi_last"], 1)
            dve.wait_ge(sem["gi_last"], 1)
            nc.vector.tensor_tensor(by_chunk(t2[:]), by_chunk(a_row), gi[:, 0:NCH].unsqueeze(2).to_broadcast([H, NCH, P]),
                                    ALU.subtract).then_inc(sem["exps"], 1)
            dve.wait_ge(sem["exps_out"], 1)
            nc.vector.tensor_scalar(t1[:], t1[:], SCALE, None, ALU.mult).then_inc(sem["rows_done"], 1)

            for kt in range(KT):
                dve.wait_ge(sem["wo_hi"], kt + 1)
                nc.vector.scalar_tensor_tensor(out=wo_lo[:, kt], in0=wo_raw[:, kt],
                                               scalar=par[:, WO_SCALE + kt:WO_SCALE + kt + 1],
                                               in1=wo_hi[:, kt].bitcast(F32), op0=ALU.mult,
                                               op1=ALU.subtract).then_inc(sem["wo_lo"], 1)
            for b in range(4):
                dve.wait_ge(sem["cols_t"], b + 1)
                for q in range(3):
                    i = nc.vector.tensor_copy(cols[:, 4 * b:4 * b + 4, q, :],
                                              by_chunk(psum[:, b, :])[:, :, 32 * q:32 * q + H])
                i.then_inc(sem["cols_done"], 1)
            dve.wait_ge(sem["decay_in"], 16)
            dve.wait_ge(sem["cols_done"], 4)

            def exponents(c):
                chunk_here(dve, c)
                if c >= 1:
                    dve.wait_ge(sem["num"], c)
                for h in range(H):
                    i = nc.vector.scalar_tensor_tensor(out=p_c[:, h], in0=negm_b[:, c % 2, h],
                                                       scalar=cols[:, c, COL_A, h:h + 1], in1=mask[:], op0=ALU.add,
                                                       op1=ALU.min)
                i.then_inc(sem["z"], 1)

            def weigh(c):
                dve.wait_ge(sem["e"], c + 1)
                dve.wait_ge(sem["scores"], c + 1)
                nc.vector.scalar_tensor_tensor(out=p_c[:], in0=by_head(psum[:, 0, :]), scalar=SCALE, in1=e_c[:],
                                               op0=ALU.mult, op1=ALU.mult).then_inc(sem["p"], 1)

            def yc_low(c):
                dve.wait_ge(sem["yc_hi"], c + 1)
                nc.vector.tensor_tensor(y_lo[:, c % 2, H:KT], yc_c[:, c % 2], y_hi[:, c % 2, H:KT].bitcast(F32),
                                        ALU.subtract).then_inc(sem["yc_lo"], 1)

            def update_state(c):
                dve.wait_ge(sem["incr"], c + 1)
                for h in range(H):
                    i = nc.vector.scalar_tensor_tensor(out=state[:, h], in0=state[:, h], scalar=decay_b[:, h, c:c + 1],
                                                       in1=head_ps(4, h), op0=ALU.mult, op1=ALU.add)
                i.then_inc(sem["state"], 1)

            def normalise_heads(c):
                dve.wait_ge(sem["den"], c + 1)
                for h in range(H):
                    i = nc.vector.bn_stats(stats[:, 6 * h:6 * h + 6], head_ps(2, h)[:, 0:HD])
                link(i)
                for h in range(H):
                    i = nc.vector.bn_aggr(aggr[:, 2 * h:2 * h + 2], stats[:, 6 * h:6 * h + 6])
                link(i)
                link(nc.vector.tensor_tensor(den, den, cols[:, c, COL_FLOOR, :], ALU.max))
                link(nc.vector.reciprocal(rden, den))
                link(nc.vector.tensor_tensor(var_h, aggr[:, 1:8:2], rden, ALU.mult))
                nc.vector.tensor_tensor(var_h, var_h, rden, ALU.mult).then_inc(sem["var_h"], 1)
                dve.wait_ge(sem["rs_h"], c + 1)
                link(nc.vector.tensor_tensor(s_h, rs_h, rden, ALU.mult))
                if c >= 1:
                    dve.wait_ge(sem["y_t"], c)
                for h in range(H):
                    i = nc.vector.tensor_scalar(y_c[:, h * P:(h + 1) * P], head_ps(2, h)[:, 0:HD],
                                                aggr[:, 2 * h:2 * h + 1], s_h[:, h:h + 1], ALU.subtract, ALU.mult)
                link(i)
                nc.vector.scalar_tensor_tensor(out=y_c[:], in0=o_c[:, c % 2], scalar=1.0, in1=y_c[:], op0=ALU.add,
                                               op1=ALU.mult).then_inc(sem["y"], 1)

            def y_low(c):
                dve.wait_ge(sem["y_hi"], c + 1)
                nc.vector.tensor_tensor(y_lo[:, c % 2, 0:H], by_head(psum[:, 2, :]), y_hi[:, c % 2, 0:H].bitcast(F32),
                                        ALU.subtract).then_inc(sem["y_lo"], 1)

            def post_scale(c, half):
                at = slice(half * TB, (half + 1) * TB)
                dve.wait_ge(sem["ss"], 2 * c + half + 1)
                if c >= 1:
                    dve.wait_ge(sem["xn"], c)
                if half == 1:
                    nc.vector.tensor_tensor(r1, ss[:, 0:1], ss[:, 1:2], ALU.add).then_inc(sem["ss_sum"], 1)
                nc.vector.tensor_tensor(t_post[:, at], psum[:, 6 + half, :], post_w[:, at],
                                        ALU.mult).then_inc(sem["t_post"], 1)

            def residual(c):
                dve.wait_ge(sem["r1"], c + 1)
                dve.wait_ge(sem["t_post"], 2 * c + 2)
                dve.wait_ge(sem["xc_in_b"][c % 2], 16 * (c // 2 + 1))
                if c >= 2:
                    dve.wait_ge(sem["h2"], c - 1)
                    dve.wait_ge(sem["xn_out"][c % 2], 16 * (c // 2))
                nc.vector.scalar_tensor_tensor(out=xn[:, c % 2], in0=t_post[:], scalar=r1, in1=x_c[:, c % 2],
                                               op0=ALU.mult, op1=ALU.add).then_inc(sem["xn"], 1)

            def sum_squares(c):
                dve.wait_ge(sem["ss2"], 2 * c + 2)
                if c >= 1:
                    dve.wait_ge(sem["h2"], c)
                nc.vector.tensor_tensor(r2, ss2[:, 0:1], ss2[:, 1:2], ALU.add).then_inc(sem["ss2_sum"], 1)

            def h2_low(c):
                for b in range(2):
                    dve.wait_ge(sem["h2_hi"], 2 * c + b + 1)
                    if c >= 2:
                        dve.wait_ge(sem["h2_out"][c % 2], 32 * (c // 2))
                    nc.vector.tensor_tensor(h2_lo[:, c % 2, 4 * b:4 * b + 4], by_head(psum[:, 4 + b, :]),
                                            h2_hi[:, c % 2, 4 * b:4 * b + 4].bitcast(F32), ALU.subtract).then_inc(sem["h2_lo"], 1)

            exponents(0)
            weigh(0)
            yc_low(0)
            for c in range(NCH + 3):
                if c < NCH:
                    update_state(c)
                    normalise_heads(c)
                if c + 1 < NCH:
                    exponents(c + 1)
                if 2 <= c < NCH + 2:
                    residual(c - 2)
                if c + 1 < NCH:
                    weigh(c + 1)
                if c < NCH:
                    y_low(c)
                if c >= 3:
                    h2_low(c - 3)
                if 2 <= c < NCH + 2:
                    sum_squares(c - 2)
                if 1 <= c <= NCH:
                    post_scale(c - 1, 0)
                    post_scale(c - 1, 1)
                if c + 1 < NCH:
                    yc_low(c + 1)


BLOCK = 1024
NBLOCK = S // BLOCK
NT = BLOCK // P
CHUNK_F = 256
NSTEP = FF // CHUNK_F
PRE_MLP = 0


def phase_c(nc, sem, psum, dram):
    with ExitStack() as ctx:
        def sb(name, shape, dt=F32):
            return ctx.enter_context(nc.sbuf_tensor(name, shape, dt))

        x_hi = sb("x_hi", [P, KT, BLOCK], F32R)
        x_lo = sb("x_lo", [P, KT, BLOCK], F32R)
        acc = sb("acc", [P, NT, D])
        hid_hi = sb("hid_hi", [P, 2, 2, BLOCK], F32R)
        hid_lo = sb("hid_lo", [P, 2, 2, BLOCK], F32R)
        w1_hi = sb("w1_hi", [P, 2, KT, P], F32R)
        w1_lo = sb("w1_lo", [P, 2, KT, P], F32R)
        w2_hi = sb("w2_hi", [P, 2, D], F32R)
        w2_lo = sb("w2_lo", [P, 2, D], F32R)
        w1_raw = sb("w1_raw", [P, 2, KT, P])
        w2_raw = sb("w2_raw", [P, 2, D])
        relu = sb("relu", [P, 2, TB])
        sq = sb("sq", [P, 2, TB])
        par = sb("par_c", [P, KT])
        wpost = sb("wpost_c", [P, D])
        eps = sb("eps_c", [P, 1])
        ss = sb("ss_c", [P, NT])
        rs = sb("rs_c", [P, NT])
        xn = sb("xn_c", [P, D])
        junk = sb("junk_c", [P, D])

        block = ctx.enter_context(nc.Block())

        @block.sync
        def _(sp):
            def load_w1(n, m):
                for f in range(2):
                    if n >= 1:
                        sp.wait_ge(sem["w1_hi"], 2 * n + f - 1)
                        sp.wait_ge(sem["w1_lo"], 2 * n + f - 1)
                    sp.dma_start(w1_raw[:, f], dram["w1"][2 * m + f]).then_inc(sem["w1_in"][f], 16)

            def load_w2(n, m):
                for f in range(2):
                    if n >= 1:
                        sp.wait_ge(sem["w2_hi"], 2 * n + f - 1)
                        sp.wait_ge(sem["w2_lo"], 2 * n + f - 1)
                    sp.dma_start(w2_raw[:, f], dram["w2"][2 * m + f]).then_inc(sem["w2_in"][f], 16)

            def load_x(b):
                for tb in range(BLOCK // TB):
                    for buf, src in ((x_hi, dram["h2_hi"]), (x_lo, dram["h2_lo"])):
                        at = slice(b * BLOCK + tb * TB, b * BLOCK + (tb + 1) * TB)
                        sp.dma_start(buf[:, :, tb * TB:(tb + 1) * TB].bitcast(F32), src[:, :, at]).then_inc(sem["xc_in"][tb], 16)

            def final(b):
                for t in range(NT):
                    i = NT * b + t
                    if i >= 1:
                        sp.wait_ge(sem["fin"], i)
                    sp.dma_start(xn[:], dram["xn"][i]).then_inc(sem["xnc_in"], 16)
                    sp.wait_ge(sem["fin"], i + 1)
                    sp.dma_start(dram["out"][i], acc[:, t, :]).then_inc(sem["out"], 16)

            sp.dma_start(par[:], dram["params_c"]).then_inc(sem["par_c"], 16)
            load_w1(0, 0)
            load_x(0)
            load_w2(0, 0)
            sp.dma_start(wpost[:], dram["post_mlp_w"].partition_broadcast(P)).then_inc(sem["par_c"], 16)
            for b in range(NBLOCK):
                for m in range(NSTEP):
                    n = NSTEP * b + m
                    if n + 1 < NBLOCK * NSTEP:
                        load_w1(n + 1, (m + 1) % NSTEP)
                    if n >= 1:
                        load_w2(n, m)
                    if m == NSTEP - 1 and b + 1 < NBLOCK:
                        sp.wait_ge(sem["ff1"], 4 * NSTEP * (b + 1))
                        load_x(b + 1)
                    if m == 0 and b >= 1:
                        final(b - 1)
            final(NBLOCK - 1)
            sp.wait_ge(sem["out"], 16 * S // P)

        @block.tensor
        def _(pe):
            def first(n, x_wait=None):
                for f in range(2):
                    pe.wait_ge(sem["w1_hi"], 2 * n + f + 1)
                    pe.wait_ge(sem["w1_lo"], 2 * n + f + 1)
                    for tb in range(2):
                        if x_wait is not None and f == 0:
                            pe.wait_ge(sem["xc_in"][tb], x_wait)
                        g = 4 * n + 2 * f + tb
                        if g >= 2 if isinstance(g, int) else True:
                            pe.wait_ge(sem["relu"], g - 1)
                        for kt in range(KT):
                            cols = slice(tb * TB, (tb + 1) * TB)
                            pairs = [(w1_hi[:, f, kt], x_hi[:, kt, cols]), (w1_hi[:, f, kt], x_lo[:, kt, cols]),
                                     (w1_lo[:, f, kt], x_hi[:, kt, cols])]
                            for i, (l, r) in enumerate(pairs):
                                mm = nc.tensor.matmul(psum[:, tb, :], l, r, start=kt == 0 and i == 0,
                                                      stop=kt == KT - 1 and i == 2)
                        mm.then_inc(sem["ff1"], 1)

            def second(n, par_):
                pe.wait_ge(sem["w2_hi"], 2 * n + 2)
                pe.wait_ge(sem["w2_lo"], 2 * n + 2)
                pe.wait_ge(sem["hid_lo"], 4 * n + 4)
                for t in range(NT):
                    for half in range(2):
                        g = 16 * n + 2 * t + half
                        bank = 2 + (2 * t + half) % 4
                        if g >= 4 if isinstance(g, int) else True:
                            pe.wait_ge(sem["acc"], g - 3)
                        cols = slice(half * TB, (half + 1) * TB)
                        tok = slice(t * P, (t + 1) * P)
                        for f in range(2):
                            pairs = [(hid_hi[:, par_, f, tok], w2_hi[:, f, cols]), (hid_hi[:, par_, f, tok], w2_lo[:, f, cols]),
                                     (hid_lo[:, par_, f, tok], w2_hi[:, f, cols])]
                            for i, (l, r) in enumerate(pairs):
                                mm = nc.tensor.matmul(psum[:, bank, :], l, r, start=f == 0 and i == 0, stop=f == 1 and i == 2)
                        mm.then_inc(sem["ff2"], 1)

            for n in range(NBLOCK * NSTEP + 1):
                if n < NBLOCK * NSTEP:
                    first(n, 32 * (n // NSTEP + 1) if n % NSTEP == 0 else None)
                if n >= 1:
                    second(n - 1, (n - 1) % 2)

        @block.scalar
        def _(act):
            def split_w1(n, f):
                u = 2 * n + f
                act.wait_ge(sem["w1_in"][f], 16 * (n + 1))
                if n >= 1 if isinstance(n, int) else True:
                    act.wait_ge(sem["ff1"], 4 * (n - 1) + 2 * f + 2)
                for kt in range(KT):
                    i = nc.scalar.activation(w1_hi[:, f, kt], w1_raw[:, f, kt], ACT.Copy, scale=par[:, kt:kt + 1])
                i.then_inc(sem["w1_hi"], 1)

            def split_w2(n, f):
                act.wait_ge(sem["w2_in"][f], 16 * (n + 1))
                if n >= 1 if isinstance(n, int) else True:
                    act.wait_ge(sem["ff2"], 16 * n)
                nc.scalar.activation(w2_hi[:, f], w2_raw[:, f], ACT.Copy).then_inc(sem["w2_hi"], 1)

            def hidden(n, f, tb, par_):
                g = 4 * n + 2 * f + tb
                act.wait_ge(sem["ff1"], g + 1)
                if g >= 2 if isinstance(g, int) else True:
                    act.wait_ge(sem["sq"], g - 1)
                nc.scalar.activation(relu[:, tb], psum[:, tb, :], ACT.Relu).then_inc(sem["relu"], 1)
                act.wait_ge(sem["relu"], g + 1)
                if n >= 2 if isinstance(n, int) else True:
                    act.wait_ge(sem["ff2"], 16 * (n - 1))
                nc.scalar.activation(hid_hi[:, par_, f, tb * TB:(tb + 1) * TB], relu[:, tb], ACT.Square).then_inc(sem["hid_hi"], 1)

            def final_squares(b):
                for t in range(NT):
                    i = NT * b + t
                    act.wait_ge(sem["acc"], 16 * NSTEP * (b + 1) - 16 + 2 * t + 2)
                    if i >= 1:
                        act.wait_ge(sem["fss"], i)
                    nc.scalar.activation(junk_c, acc[:, t, :], ACT.Square, accum_out=ss[:, t:t + 1]).then_inc(sem["fss"], 1)
                act.wait_ge(sem["fss"], NT * (b + 1))
                nc.scalar.activation(rs[:], ss[:], ACT.Ln, scale=1.0 / D, bias=eps[:, 0:1]).then_inc(sem["fln"], 1)
                act.wait_ge(sem["fln"], b + 1)
                nc.scalar.activation(rs[:], rs[:], ACT.Exp, scale=-0.5).then_inc(sem["frs"], 1)

            junk_c = junk[:]
            nc.scalar.preload_act_table_set(LN_EXP)
            act.wait_ge(sem["par_c"], 32)
            act.wait_ge(sem["eps_c"], 1)
            split_w1(0, 0)
            split_w1(0, 1)
            for n in range(NBLOCK * NSTEP + 1):
                last = n == NBLOCK * NSTEP
                if n >= 1:
                    split_w2(n - 1, 0)
                    split_w2(n - 1, 1)
                if not last:
                    for f in range(2):
                        for tb in range(2):
                            hidden(n, f, tb, n % 2)
                        if n + 1 < NBLOCK * NSTEP:
                            split_w1(n + 1, f)
                if n >= 1 and n % NSTEP == 0:
                    final_squares(n // NSTEP - 1)

        @block.vector
        def _(dve):
            def split_w1(n, f):
                dve.wait_ge(sem["w1_hi"], 2 * n + f + 1)
                for kt in range(KT):
                    i = nc.vector.scalar_tensor_tensor(out=w1_lo[:, f, kt], in0=w1_raw[:, f, kt], scalar=par[:, kt:kt + 1],
                                                       in1=w1_hi[:, f, kt].bitcast(F32), op0=ALU.mult, op1=ALU.subtract)
                i.then_inc(sem["w1_lo"], 1)

            def split_w2(n, f):
                dve.wait_ge(sem["w2_hi"], 2 * n + f + 1)
                nc.vector.tensor_tensor(w2_lo[:, f], w2_raw[:, f], w2_hi[:, f].bitcast(F32),
                                        ALU.subtract).then_inc(sem["w2_lo"], 1)

            def hidden(n, f, tb, par_):
                g = 4 * n + 2 * f + tb
                dve.wait_ge(sem["relu"], g + 1)
                if g >= 2 if isinstance(g, int) else True:
                    dve.wait_ge(sem["hid_lo"], g - 1)
                nc.vector.tensor_tensor(sq[:, tb], relu[:, tb], relu[:, tb], ALU.mult).then_inc(sem["sq"], 1)
                dve.wait_ge(sem["sq"], g + 1)
                dve.wait_ge(sem["hid_hi"], g + 1)
                at = slice(tb * TB, (tb + 1) * TB)
                nc.vector.tensor_tensor(hid_lo[:, par_, f, at], sq[:, tb], hid_hi[:, par_, f, at].bitcast(F32),
                                        ALU.subtract).then_inc(sem["hid_lo"], 1)

            def accumulate(n, first):
                for t in range(NT):
                    for half in range(2):
                        j = 2 * t + half
                        dve.wait_ge(sem["ff2"], 16 * n + j + 1)
                        out = acc[:, t, half * TB:(half + 1) * TB]
                        ps = psum[:, 2 + j % 4, :]
                        if first:
                            if n >= NSTEP:
                                dve.wait_ge(sem["out"], 16 * (n // NSTEP * NT - NT + t + 1))
                            nc.vector.tensor_copy(out, ps).then_inc(sem["acc"], 1)
                        else:
                            dve.wait_ge(sem["acc"], 16 * n + j - 15)
                            nc.vector.tensor_tensor(out, out, ps, ALU.add).then_inc(sem["acc"], 1)

            def final(b):
                dve.wait_ge(sem["frs"], b + 1)
                for t in range(NT):
                    i = NT * b + t
                    nc.vector.scalar_tensor_tensor(out=acc[:, t], in0=acc[:, t], scalar=rs[:, t:t + 1], in1=wpost[:],
                                                   op0=ALU.mult, op1=ALU.mult).then_inc(sem["fmul"], 1)
                    dve.wait_ge(sem["fmul"], i + 1)
                    dve.wait_ge(sem["xnc_in"], 16 * (i + 1))
                    nc.vector.tensor_tensor(acc[:, t], acc[:, t], xn[:], ALU.add).then_inc(sem["fin"], 1)

            nc.vector.memset(eps[:], EPS).then_inc(sem["eps_c"], 1)
            dve.wait_ge(sem["par_c"], 32)
            split_w1(0, 0)
            split_w1(0, 1)
            for n in range(NBLOCK * NSTEP + 1):
                last = n == NBLOCK * NSTEP
                if n >= 1:
                    split_w2(n - 1, 0)
                    split_w2(n - 1, 1)
                if not last:
                    for f in range(2):
                        for tb in range(2):
                            hidden(n, f, tb, n % 2)
                        if n + 1 < NBLOCK * NSTEP:
                            split_w1(n + 1, f)
                if n >= 1:
                    accumulate(n - 1, (n - 1) % NSTEP == 0)
                if n >= 1 and n % NSTEP == 0:
                    final(n // NSTEP - 1)


SEM_NAMES = ["par_a", "eps_a", "ones_a", "x_sq", "x_sum", "x_ln", "x_rstd", "h", "h_hi", "h_lo", "w_hi", "w_lo", "proj",
             "tap", "u_head", "ln_sum", "c_center", "c_sq", "c_rstd", "c_norm", "c_silu", "q_tap", "q_silu", "q_out",
             "dve_a",
             "gates_in", "par_b", "rows_done", "rows_out", "decay_in", "cols_done", "scores", "qs", "z", "incr", "y", "yc_lo",
             "xn", "ident", "v_ones", "num", "p", "wk", "h2_lo", "y_lo", "state", "y_t", "y_hi", "yc_hi",
             "wo_lo", "wo_hi", "t_post", "ss", "out_proj", "h2", "h2_t", "cols_t", "act_b", "softplus", "exps", "exps_out",
             "e", "den", "r1", "r2", "ss2", "ss2_sum", "ss_sum", "h2_hi", "var_h", "rs_h", "dve_b", "eps_b", "gi_last",
             "wo_scale",
             "w1_hi", "w1_lo", "w2_hi", "w2_lo", "par_c", "eps_c", "ff1", "ff2", "relu", "sq", "hid_hi", "hid_lo", "acc",
             "fss", "fln", "frs", "fmul", "fin", "xnc_in", "out"]
SEM_LISTS = {"w_raw": W_RING, "x_in": 2 * NTB, "th_out": 2, "c_out": 2, "chunk_in": 2, "xc_in_b": 2, "xn_out": 2, "h2_out": 2, "wo_in": KT, "w1_in": 2, "w2_in": 2, "xc_in": 2}


def semaphores(nc, ctx):
    named = {name: ctx.enter_context(nc.semaphore(name)) for name in SEM_NAMES}
    for name, n in SEM_LISTS.items():
        named[name] = [ctx.enter_context(nc.semaphore(f"{name}{i}")) for i in range(n)]
    named["evac"] = {e: ctx.enter_context(nc.semaphore(f"evac_{e}")) for e in ("act", "dve")}
    return named


def layouts(x, pre_mix_norm_w, w_in, qk_conv_w, qk_conv_b, gate_bias, mlstm_norm_w, conv_w, conv_b, conv_norm_w,
            conv_norm_b, w_out, post_mix_norm_w, pre_mlp_norm_w, w_ff1, w_ff2, post_mlp_norm_w):
    def by_channel(a):
        return a.reshape(a.shape[0], -1, P).transpose(2, 1, 0)

    w = w_in[0]
    qk, v, o, gates, val, gate = np.split(w, [2 * DH, 3 * DH, 4 * DH, 4 * DH + 2 * H, 5 * DH + 2 * H], axis=1)

    def tile(a, n):
        return a[:, n * P:(n + 1) * P]

    gate_tile = np.zeros((D, P), w.dtype)
    gate_tile[:, 0:H] = gates[:, 0:H]
    gate_tile[:, 32:32 + H] = gates[:, H:]
    tiles = []
    for g in range(H):
        tiles += [tile(gate, g), tile(val, g), tile(qk, 2 * g), tile(qk, 2 * g + 1)]
    tiles += [gate_tile] + [tile(v, h) for h in VO_HEADS] + [tile(o, h) for h in VO_HEADS]
    params_a = np.concatenate([
        pre_mix_norm_w[0].reshape(KT, P).T,
        by_channel(conv_w[0]).reshape(P, -1),
        conv_b[0].reshape(H, P).T, conv_norm_w[0].reshape(H, P).T, conv_norm_b[0].reshape(H, P).T,
        by_channel(qk_conv_w[0]).reshape(P, -1), qk_conv_b[0].reshape(8, P).T,
    ], axis=1)
    return {
        "xt": np.ascontiguousarray(x[0].T.reshape(KT, P, S).transpose(1, 0, 2)),
        "w_in": np.ascontiguousarray(np.stack(tiles).reshape(N_TILES, KT, P, P).transpose(0, 2, 1, 3)),
        "params_a": np.ascontiguousarray(params_a),
        "x": x[0],
        "w_out": w_out[0].reshape(KT, P, D),
        "params_b": np.ascontiguousarray(np.concatenate([mlstm_norm_w[0].reshape(H, P).T, np.ones((P, H), w.dtype)], axis=1)),
        "gate_bias": np.ascontiguousarray(gate_bias[0].reshape(2, H).T),
        "post_w": post_mix_norm_w[0],
        "w1": np.ascontiguousarray(w_ff1[0].reshape(KT, P, FF // P, P).transpose(2, 1, 0, 3)),
        "w2": w_ff2[0].reshape(FF // P, P, D),
        "params_c": np.ascontiguousarray(pre_mlp_norm_w[0].reshape(KT, P).T),
        "post_mlp_w": post_mlp_norm_w[0],
    }


INPUTS = ["xt", "w_in", "params_a", "x", "w_out", "params_b", "gate_bias", "post_w", "w1", "w2", "params_c", "post_mlp_w"]
SCRATCH = {
    "qk": ([8, P, S], F32), "v": ([NCH, P, DH], F32), "o": ([NCH, P, DH], F32), "yc": ([H, P, S], F32),
    "gates": ([2 * H, S], F32), "rows": ([2, H, S], F32), "decay": ([H, NCH], F32), "xn": ([NCH, P, D], F32),
    "h2_hi": ([P, KT, S], F32), "h2_lo": ([P, KT, S], F32),
}


def build(nc, arrays, out):
    scratch = {name: nc.dram_tensor("scratch_" + name, shape, dt).ap() for name, (shape, dt) in SCRATCH.items()}
    dram = {**arrays, **scratch, "out": out.rearrange("a (n p) d -> (a n) p d", p=P)}
    with ExitStack() as ctx:
        sem = semaphores(nc, ctx)
        psum = ctx.enter_context(nc.psum_tensor("psum", [P, 8, TB], F32))
        phase_a(nc, sem, psum, dram)
        phase_b(nc, sem, psum, dram)
        phase_c(nc, sem, psum, dram)


def kernel(**inputs):
    import concourse.bacc as bacc
    from concourse.bass_utils import run_bass_kernel_spmd as run

    nc = bacc.Bacc("TRN2", target_bir_lowering=False, num_devices=1)
    arrays, args = {}, {}
    for name, a in layouts(**{k: np.asarray(v) for k, v in inputs.items()}).items():
        a = np.ascontiguousarray(a)
        arrays[f"in_{name}"] = a
        args[name] = nc.dram_tensor(f"in_{name}", a.shape, mybir.dt.from_np(a.dtype), kind="ExternalInput").ap()
    out = nc.dram_tensor("out_0", (1, S, D), F32, kind="ExternalOutput").ap()
    build(nc, args, out)
    r = run(nc, [arrays], core_ids=[0])
    return r.results[0]["out_0"]
```

```python
from contextlib import ExitStack

import numpy as np
import concourse.bass as bass
from concourse import mybir
from concourse.alu_op_type import AluOpType as ALU

ACT = mybir.ActivationFunctionType
F32 = mybir.dt.float32
F32R = mybir.dt.float32r

P = 128
S = 2048
D = 1024
KT = D // P
DH = 512
H = 4
HD = 128
FF = 4096
CW = 31
QW = 4
TB = 512
NTB = S // TB
HALF = 1024
NCH = S // P
EPS = 1e-6
SCALE = float(HD) ** -0.5
LN_EXP = "natural_log_exp_and_others"
SILU_TANH = "silu_and_others"
FAR = -1e30

PRE_W, CONV_W, CONV_B, CN_W, CN_B = 0, 8, 8 + H * CW, 8 + H * CW + 4, 8 + H * CW + 8
QKC_W = CN_B + 4
QKC_B = QKC_W + 8 * QW
PAR_A = QKC_B + 8

SLOTS = []
for _g in range(H):
    for _tb in range(NTB):
        SLOTS += [("gate", _g, _tb), ("val", _g, _tb)]
    for _j in (2 * _g, 2 * _g + 1):
        SLOTS += [("qk", _j, _tb) for _tb in range(NTB)]
SLOTS += [("gates", 0, _tb) for _tb in range(NTB)]
SLOTS += [("v", 0, _m) for _m in range(NCH)] + [("o", 0, _m) for _m in range(NCH)]
N_SLOTS = len(SLOTS)
N_TILES = 25
W_RING = 4
VO_HEADS = [1, 2, 3, 0]
BANKS_A = 6
N_UNITS = 2 * H
U_RING = 3


def tile_of(slot):
    kind, n, _ = slot
    return {"gate": 4 * n, "val": 4 * n + 1, "qk": 4 * (n // 2) + 2 + n % 2, "gates": 16, "v": 17, "o": 21}[kind]


def first_use(tile):
    base = tile if tile < 17 else 17 + 4 * ((tile - 17) // 4)
    return min(i for i, s in enumerate(SLOTS) if tile_of(s) == base)


def last_use(tile):
    base = tile if tile < 17 else 17 + 4 * ((tile - 17) // 4)
    return max(i for i, s in enumerate(SLOTS) if tile_of(s) == base)


def split_slot(tile):
    if tile < 4:
        return 0
    return max(first_use(tile) - 5, last_use(tile - W_RING) + 1)


def tiles_split_at(s):
    return [t for t in range(N_TILES) if split_slot(t) == s]


def evacs(s, engine):
    return sum((k == "val") == (engine == "dve") for k, _, _ in SLOTS[: s + 1])


def glu_slot(u):
    return SLOTS.index(("val", u // 2, 2 * (u % 2)))


def tap_plan():
    out = []
    for s in range(N_SLOTS):
        n = max(0, 3 * (s - 3))
        for u in range(U_RING, N_UNITS):
            if s + 1 >= glu_slot(u):
                n = max(n, CW * (u - U_RING + 1))
        out.append(min(n, CW * N_UNITS))
    return out


TAPS = tap_plan()
CONV_END = [min(s for s in range(N_SLOTS) if TAPS[s] >= CW * (u + 1)) for u in range(N_UNITS)]
AT_MEAN, AT_CENTER, AT_SQUARE, AT_VAR, AT_RSTD, AT_NORM, AT_SILU = 1, 2, 3, 4, 5, 6, 7


def units_at(s, step):
    return [u for u in range(N_UNITS) if CONV_END[u] + step == s]


def th_uses(s):
    return sum(k in ("gate", "gates", "v", "o") for k, _, _ in SLOTS[: s + 1])


def th_stores(s, parity):
    n = 0
    for i in range(s + 1):
        k = SLOTS[i][0]
        if k in ("gates", "v", "o") and (th_uses(i) - 1) % 2 == parity:
            n += 2 if k == "gates" else 1
    return n


def last_th_user(s):
    n = th_uses(s) - 1
    for i in range(s):
        if SLOTS[i][0] in ("gate", "gates", "v", "o") and th_uses(i) - 1 == n - 2:
            return i
    return None


def phase_a(nc, sem, psum, dram):
    with ExitStack() as ctx:
        def sb(name, shape, dt=F32):
            return ctx.enter_context(nc.sbuf_tensor(name, shape, dt))

        h_hi = sb("h_hi", [P, KT, S], F32R)
        with nc.sbuf_tensor("x_raw", [P, KT, S], F32) as x_raw:
            pass
        h_lo = sb("h_lo", [P, KT, S], F32R)
        w_hi = sb("w_hi", [P, W_RING, KT, P], F32R)
        with nc.sbuf_tensor("w_raw", [P, W_RING, KT, P], F32) as w_raw:
            pass
        w_lo = sb("w_lo", [P, W_RING, KT, P], F32R)
        par = sb("par_a", [P, PAR_A])
        ones = sb("ones_a", [P, P])
        eps = sb("eps_a", [P, 1])
        th = sb("th", [P, 2, TB])
        qout = sb("qout", [P, HALF])
        rstd = sb("rstd_a", [P, HALF])
        qraw = sb("qraw", [P, 2, QW - 1 + HALF])
        u_buf = sb("u_buf", [P, U_RING, CW - 1 + HALF])
        c_buf = sb("c_buf", [P, 2, HALF])
        ln_ps = psum[:, 6:8, :].rearrange("p a b -> p (a b)")

        def x_sq(n):
            return c_buf[:, n % 4 // 2, n % 2 * TB:(n % 2 + 1) * TB]

        def x_adds(n):
            return (KT - 1) * (n // KT - 1) + max(n % KT, 1)

        def x_at(tb, kt):
            return x_raw[:, kt, tb * TB:(tb + 1) * TB]

        block = ctx.enter_context(nc.Block())

        @block.sync
        def _(sp):
            def load_w(t):
                if t >= W_RING:
                    sp.wait_ge(sem["proj"], last_use(t - W_RING) + 1)
                sp.dma_start(w_raw[:, t % W_RING], dram["w_in"][t]).then_inc(sem["w_raw"][t % W_RING], 16)

            def load_x(tb):
                for half in range(2):
                    kt = slice(half * KT // 2, (half + 1) * KT // 2)
                    cols = slice(tb * TB, (tb + 1) * TB)
                    sp.dma_start(x_raw[:, kt, cols], dram["xt"][:, kt, cols]).then_inc(sem["x_in"][2 * tb + half], 16)

            sp.dma_start(par[:], dram["params_a"]).then_inc(sem["par_a"], 16)
            load_x(0)
            load_w(0)
            load_w(1)
            for tb in range(1, NTB):
                load_x(tb)
            load_w(2)
            load_w(3)
            for t in range(4, N_TILES):
                load_w(t)

        @block.gpsimd
        def _(pool):
            nc.gpsimd.memset(ones[:], 1.0).then_inc(sem["ones_a"], 1)
            for tb in range(1, NTB):
                total = qout[:, (tb % 2) * TB:(tb % 2 + 1) * TB]
                for kt in range(1, KT):
                    n = KT * tb + kt
                    pool.wait_ge(sem["x_sq"], n + 1)
                    if kt == 1:
                        if tb == 3:
                            pool.wait_ge(sem["x_sum"], KT + 1)
                        a = x_sq(n - 1)
                    else:
                        pool.wait_ge(sem["x_add"], x_adds(n - 1))
                        a = total
                    nc.gpsimd.tensor_tensor(total, a, x_sq(n), ALU.add).then_inc(sem["x_add"], 1)

        @block.tensor
        def _(pe):
            def sum_squares(tb):
                if tb == 0:
                    pe.wait_ge(sem["ones_a"], 1)
                if tb >= 2:
                    pe.wait_ge(sem["x_rstd"], tb - 1)
                if tb == 0:
                    for kt in range(KT):
                        pe.wait_ge(sem["x_sq"], kt + 1)
                        nc.tensor.matmul(psum[:, 6, :], ones[:], x_sq(kt), start=kt == 0,
                                         stop=kt == KT - 1).then_inc(sem["x_sum"], 1)
                else:
                    pe.wait_ge(sem["x_add"], x_adds(KT * tb + KT - 1))
                    nc.tensor.matmul(psum[:, 6 + tb % 2, :], ones[:], qout[:, (tb % 2) * TB:(tb % 2 + 1) * TB],
                                     start=True, stop=True).then_inc(sem["x_sum"], 1)

            def slot(s):
                kind, n, tb = SLOTS[s]
                tile = tile_of(SLOTS[s])
                out = psum[:, s % BANKS_A, :]
                pe.wait_ge(sem["w_hi"], tile + 1 if tile < 17 else tile + 4)
                pe.wait_ge(sem["w_lo"], tile + 1 if tile < 17 else tile + 4)
                if s >= BANKS_A:
                    by = "dve" if SLOTS[s - BANKS_A][0] == "val" else "act"
                    pe.wait_ge(sem["evac"][by], evacs(s - BANKS_A, by))
                for kt in range(KT):
                    if kind == "gate" and n == 0:
                        pe.wait_ge(sem["h_hi"], KT * tb + kt + 1)
                        pe.wait_ge(sem["h_lo"], KT * tb + kt + 1)
                    if kind in ("v", "o"):
                        cols = slice(tb * P, (tb + 1) * P)
                        o = out.rearrange("p (a b) -> p a b", a=H)
                        pairs = [(h_hi[:, kt, cols], w_hi[:, :, kt, :]), (h_hi[:, kt, cols], w_lo[:, :, kt, :]),
                                 (h_lo[:, kt, cols], w_hi[:, :, kt, :])]
                    else:
                        cols = slice(tb * TB, (tb + 1) * TB)
                        o, r = out, tile % W_RING
                        pairs = [(w_hi[:, r, kt, :], h_hi[:, kt, cols]), (w_hi[:, r, kt, :], h_lo[:, kt, cols]),
                                 (w_lo[:, r, kt, :], h_hi[:, kt, cols])]
                    for i, (a, b) in enumerate(pairs):
                        mm = nc.tensor.matmul(o, a, b, start=kt == 0 and i == 0, stop=kt == KT - 1 and i == 2)
                mm.then_inc(sem["proj"], 1)

            def group_sum(src, b):
                nc.tensor.matmul(psum[:, 6 + b, :], ones[:], src[:, b * TB:(b + 1) * TB],
                                 start=True, stop=True).then_inc(sem["ln_sum"], 1)

            sum_squares(0)
            for s in range(N_SLOTS):
                slot(s)
                if s in (0, 2, 4):
                    sum_squares(1 + s // 2)
                for u in units_at(s, AT_MEAN):
                    pe.wait_ge(sem["tap"], CW * (u + 1))
                    if u == 0:
                        pe.wait_ge(sem["x_rstd"], NTB)
                    else:
                        pe.wait_ge(sem["c_rstd"], 2 * u)
                    for b in range(2):
                        group_sum(c_buf[:, u % 2], b)
                for u in units_at(s, AT_VAR):
                    pe.wait_ge(sem["c_sq"], u + 1)
                    for b in range(2):
                        group_sum(rstd, b)

        @block.scalar
        def _(act):
            def square_x(n):
                act.wait_ge(sem["x_in"][n // (KT // 2)], 16)
                if n >= 4:
                    if n - 4 < KT:
                        act.wait_ge(sem["x_sum"], n - 3)
                    else:
                        act.wait_ge(sem["x_add"], x_adds(n - 4))
                nc.scalar.activation(x_sq(n), x_at(n // KT, n % KT), ACT.Square).then_inc(sem["x_sq"], 1)

            def rstd_x(tb):
                r = rstd[:, (tb % 2) * TB:(tb % 2 + 1) * TB]
                act.wait_ge(sem["x_sum"], KT + tb)
                if tb >= 2:
                    act.wait_ge(sem["h"], KT * (tb - 1))
                nc.scalar.activation(r, psum[:, 6 + tb % 2, :], ACT.Ln, scale=1.0 / D, bias=eps[:, 0:1]).then_inc(sem["x_ln"], 1)
                act.wait_ge(sem["x_ln"], tb + 1)
                nc.scalar.activation(r, r, ACT.Exp, scale=-0.5).then_inc(sem["x_rstd"], 1)

            def high_x(n):
                tb, kt = n // KT, n % KT
                act.wait_ge(sem["h"], n + 1)
                nc.scalar.activation(h_hi[:, kt, tb * TB:(tb + 1) * TB], x_at(tb, kt),
                                     ACT.Copy).then_inc(sem["h_hi"], 1)
                for i in range(KT + n + min(n, 3), KT + n + 1 + min(n + 1, 3)):
                    if i < KT * NTB:
                        square_x(i)

            def split_w(t):
                act.wait_ge(sem["w_raw"][t % W_RING], 16 * (t // W_RING + 1))
                nc.scalar.activation(w_hi[:, t % W_RING], w_raw[:, t % W_RING], ACT.Copy).then_inc(sem["w_hi"], 1)

            def evacuate(s):
                kind, n, tb = SLOTS[s]
                if kind == "val":
                    return
                ps = psum[:, s % BANKS_A, :]
                act.wait_ge(sem["proj"], s + 1)
                if kind == "qk":
                    half = tb // 2
                    if n >= 1 and tb % 2 == 0:
                        act.wait_ge(sem["q_tap"], 9 * (n - 1) + (5 if half == 0 else 9))
                    at = QW - 1 + (tb % 2) * TB
                    nc.scalar.activation(qraw[:, half, at:at + TB], ps, ACT.Copy).then_inc(sem["evac"]["act"], 1)
                    return
                k = (th_uses(s) - 1) % 2
                before = last_th_user(s)
                if before is not None:
                    if SLOTS[before][0] == "gate":
                        act.wait_ge(sem["evac"]["dve"], evacs(before + 1, "dve"))
                    else:
                        act.wait_ge(sem["th_out"][k], 16 * th_stores(before, k))
                if kind == "gate":
                    nc.scalar.activation(th[:, k, :], ps, ACT.Tanh, scale=0.5).then_inc(sem["evac"]["act"], 1)
                    return
                rows = slice(0, 36) if kind == "gates" else slice(0, P)
                nc.scalar.activation(th[rows, k, :], ps[rows], ACT.Tanh if kind == "o" else ACT.Copy,
                                     scale=0.5 if kind == "o" else 1.0).then_inc(sem["evac"]["act"], 1)
                act.wait_ge(sem["evac"]["act"], evacs(s, "act"))
                if kind == "gates":
                    for half in range(2):
                        act.dma_start(dram["gates"][4 * half:4 * half + 4, tb * TB:(tb + 1) * TB],
                                      th[32 * half:32 * half + 4, k, :]).then_inc(sem["th_out"][k], 16)
                else:
                    act.dma_start(dram["v"][tb] if kind == "v" else dram["o"][tb], th[:, k, :]).then_inc(sem["th_out"][k], 16)

            def silu_qk(s):
                _, j, tb = SLOTS[s]
                half = tb // 2
                act.wait_ge(sem["q_tap"], 9 * j + (5 if half == 0 else 9))
                nc.scalar.activation(qout[:], qout[:], ACT.Silu,
                                     bias=par[:, QKC_B + j:QKC_B + j + 1]).then_inc(sem["q_silu"], 1)
                act.wait_ge(sem["q_silu"], 2 * j + half + 1)
                act.dma_start(dram["qk"][j, :, half * HALF:(half + 1) * HALF], qout[:]).then_inc(sem["q_out"], 16)

            nc.scalar.preload_act_table_set(LN_EXP)
            act.wait_ge(sem["par_a"], 16)
            act.wait_ge(sem["eps_a"], 1)
            for n in range(KT):
                square_x(n)
            split_w(0)
            split_w(1)
            for tb in range(NTB):
                rstd_x(tb)
                if tb == NTB - 1:
                    nc.scalar.preload_act_table_set(SILU_TANH)
                    evacuate(0)
                for kt in range(KT):
                    high_x(KT * tb + kt)
            split_w(2)
            split_w(3)
            for s in range(N_SLOTS):
                for t in tiles_split_at(s):
                    if t >= 4:
                        split_w(t)
                if s >= 1:
                    evacuate(s)
                for u in units_at(s, AT_SQUARE):
                    act.wait_ge(sem["c_center"], u + 1)
                    if u >= 1:
                        act.wait_ge(sem["c_norm"], u)
                    nc.scalar.activation(rstd[:], c_buf[:, u % 2], ACT.Square).then_inc(sem["c_sq"], 1)
                for u in units_at(s, AT_RSTD):
                    nc.scalar.preload_act_table_set(LN_EXP)
                    act.wait_ge(sem["ln_sum"], 4 * u + 4)
                    nc.scalar.activation(rstd[:], ln_ps, ACT.Ln, scale=1.0 / P, bias=eps[:, 0:1]).then_inc(sem["c_rstd"], 1)
                    act.wait_ge(sem["c_rstd"], 2 * u + 1)
                    nc.scalar.activation(rstd[:], rstd[:], ACT.Exp, scale=-0.5).then_inc(sem["c_rstd"], 1)
                    nc.scalar.preload_act_table_set(SILU_TANH)
                for u in units_at(s, AT_SILU):
                    g, half = u // 2, u % 2
                    act.wait_ge(sem["c_norm"], u + 1)
                    nc.scalar.activation(c_buf[:, u % 2], c_buf[:, u % 2], ACT.Silu, scale=par[:, CN_W + g:CN_W + g + 1],
                                         bias=par[:, CN_B + g:CN_B + g + 1]).then_inc(sem["c_silu"], 1)
                    act.wait_ge(sem["c_silu"], u + 1)
                    act.dma_start(dram["yc"][g, :, half * HALF:(half + 1) * HALF], c_buf[:, u % 2]).then_inc(sem["c_out"][u % 2], 16)
                if s >= 2 and SLOTS[s - 2][0] == "qk" and SLOTS[s - 2][2] % 2 == 1:
                    silu_qk(s - 2)
            for k in range(2):
                act.wait_ge(sem["th_out"][k], 16 * th_stores(N_SLOTS - 1, k))
                act.wait_ge(sem["c_out"][k], 16 * (N_UNITS // 2))
            act.wait_ge(sem["q_out"], 16 * 16)

        @block.vector
        def _(dve):
            self_n = [0]

            def link(ins):
                self_n[0] += 1
                ins.then_inc(sem["dve_a"], 1)
                dve.wait_ge(sem["dve_a"], self_n[0])

            def normalise_x(tb):
                dve.wait_ge(sem["x_rstd"], tb + 1)
                r = rstd[:, (tb % 2) * TB:(tb % 2 + 1) * TB]

                def low(kt):
                    cols = slice(tb * TB, (tb + 1) * TB)
                    dve.wait_ge(sem["h_hi"], KT * tb + kt + 1)
                    nc.vector.tensor_tensor(h_lo[:, kt, cols], x_at(tb, kt), h_hi[:, kt, cols].bitcast(F32),
                                            ALU.subtract).then_inc(sem["h_lo"], 1)

                for kt in range(KT):
                    x = x_at(tb, kt)
                    nc.vector.scalar_tensor_tensor(out=x, in0=x, scalar=par[:, PRE_W + kt:PRE_W + kt + 1], in1=r,
                                                   op0=ALU.mult, op1=ALU.mult).then_inc(sem["h"], 1)
                    if kt >= 1:
                        low(kt - 1)
                    if tb == NTB - 1 and kt == 2:
                        glu(1)
                low(KT - 1)

            def split_w(t):
                dve.wait_ge(sem["w_hi"], t + 1)
                nc.vector.tensor_tensor(w_lo[:, t % W_RING], w_raw[:, t % W_RING], w_hi[:, t % W_RING].bitcast(F32),
                                        ALU.subtract).then_inc(sem["w_lo"], 1)

            def glu(s):
                _, g, tb = SLOTS[s]
                u = 2 * g + tb // 2
                at = CW - 1 + (tb % 2) * TB
                if tb % 2 == 0 and u >= U_RING:
                    dve.wait_ge(sem["tap"], CW * (u - U_RING + 1))
                if tb == 0:
                    nc.vector.memset(u_buf[:, u % U_RING, 0:CW - 1], 0.0).then_inc(sem["u_head"], 1)
                elif tb == 2:
                    nc.vector.tensor_copy(u_buf[:, u % U_RING, 0:CW - 1],
                                          u_buf[:, (u - 1) % U_RING, HALF:HALF + CW - 1]).then_inc(sem["u_head"], 1)
                dve.wait_ge(sem["proj"], s + 1)
                dve.wait_ge(sem["evac"]["act"], evacs(s - 1, "act"))
                nc.vector.scalar_tensor_tensor(out=u_buf[:, u % U_RING, at:at + TB], in0=th[:, (th_uses(s) - 1) % 2, :],
                                               scalar=1.0, in1=psum[:, s % BANKS_A, :], op0=ALU.add,
                                               op1=ALU.mult).then_inc(sem["evac"]["dve"], 1)

            def tap(n):
                u, k = n // CW, n % CW
                g = u // 2
                out, src = c_buf[:, u % 2], u_buf[:, u % U_RING, k:k + HALF]
                w = par[:, CONV_W + g * CW + k:CONV_W + g * CW + k + 1]
                if k == 0:
                    dve.wait_ge(sem["evac"]["dve"], 2 * (u + 1))
                    dve.wait_ge(sem["u_head"], u + 1)
                    if u >= 2:
                        dve.wait_ge(sem["c_out"][u % 2], 16 * (u // 2))
                    nc.vector.tensor_scalar(out, src, w, par[:, CONV_B + g:CONV_B + g + 1],
                                            ALU.mult, ALU.add).then_inc(sem["tap"], 1)
                else:
                    dve.wait_ge(sem["tap"], n)
                    nc.vector.scalar_tensor_tensor(out=out, in0=src, scalar=w, in1=out, op0=ALU.mult,
                                                   op1=ALU.add).then_inc(sem["tap"], 1)

            def convolve_qk(s):
                _, j, tb = SLOTS[s]
                half = tb // 2
                dve.wait_ge(sem["evac"]["act"], evacs(s, "act"))
                if 2 * j + half >= 1:
                    dve.wait_ge(sem["q_out"], 16 * (2 * j + half))
                for k in range(QW):
                    w = par[:, QKC_W + j * QW + k:QKC_W + j * QW + k + 1]
                    src = qraw[:, half, k:k + HALF]
                    if k == 0:
                        nc.vector.tensor_scalar(qout[:], src, w, None, ALU.mult).then_inc(sem["q_tap"], 1)
                    else:
                        dve.wait_ge(sem["q_tap"], 9 * j + 5 * half + k)
                        nc.vector.scalar_tensor_tensor(out=qout[:], in0=src, scalar=w, in1=qout[:], op0=ALU.mult,
                                                       op1=ALU.add).then_inc(sem["q_tap"], 1)
                if half == 0:
                    nc.vector.tensor_copy(qraw[:, 1, 0:QW - 1], qraw[:, 0, HALF:HALF + QW - 1]).then_inc(sem["q_tap"], 1)

            nc.vector.memset(eps[:], EPS).then_inc(sem["eps_a"], 1)
            dve.wait_ge(sem["par_a"], 16)
            link(nc.vector.tensor_scalar(par[:, CONV_W:CONV_W + H * CW], par[:, CONV_W:CONV_W + H * CW], 0.5, None, ALU.mult))
            split_w(0)
            split_w(1)
            for tb in range(NTB):
                normalise_x(tb)
            split_w(2)
            split_w(3)
            for s in range(N_SLOTS):
                for t in tiles_split_at(s):
                    if t >= 4:
                        split_w(t)
                if SLOTS[s][0] == "val" and s > 1:
                    glu(s)
                if s == 0:
                    link(nc.vector.memset(qraw[:, 0, 0:QW - 1], 0.0))
                for n in range(TAPS[s - 1] if s else 0, TAPS[s]):
                    tap(n)
                if s >= 1 and SLOTS[s - 1][0] == "qk" and SLOTS[s - 1][2] % 2 == 1:
                    convolve_qk(s - 1)
                for u in units_at(s, AT_CENTER):
                    dve.wait_ge(sem["ln_sum"], 4 * u + 2)
                    nc.vector.scalar_tensor_tensor(out=c_buf[:, u % 2], in0=ln_ps, scalar=-1.0 / P, in1=c_buf[:, u % 2],
                                                   op0=ALU.mult, op1=ALU.add).then_inc(sem["c_center"], 1)
                for u in units_at(s, AT_NORM):
                    dve.wait_ge(sem["c_rstd"], 2 * u + 2)
                    nc.vector.tensor_tensor(c_buf[:, u % 2], c_buf[:, u % 2], rstd[:], ALU.mult).then_inc(sem["c_norm"], 1)


WO_SCALE = 0
PAR_B = 8
COL_A, COL_WK, COL_FLOOR = 0, 1, 2
VW = HD + 1


def phase_b(nc, sem, psum, dram):
    with ExitStack() as ctx:
        def sb(name, shape, dt=F32):
            return ctx.enter_context(nc.sbuf_tensor(name, shape, dt))

        wo_hi = sb("wo_hi", [P, KT, D], F32R)
        with nc.sbuf_tensor("wo_raw", [P, KT, D], F32) as wo_raw:
            pass
        wo_lo = sb("wo_lo", [P, KT, D], F32R)
        par = sb("par_b", [P, PAR_B])
        ident = sb("ident", [P, P])
        mask = sb("mask", [P, P])
        post_w = sb("post_w_sb", [P, D])
        cols = sb("cols", [P, NCH, 4, H])
        decay_b = sb("decay_b", [P, H, NCH])
        state = sb("state", [P, H, VW])
        eps = sb("eps_b", [P, 1])
        with ExitStack() as early:
            def row(name, parts=H):
                return early.enter_context(nc.sbuf_tensor(name, [parts, S], F32))

            gi, gf, t0, t1, t2, keep, step = (row(n) for n in ("gi", "gf", "t0", "t1", "t2", "keep", "step"))
            rows = row("rows", P)
            m_prev = early.enter_context(nc.sbuf_tensor("m_prev", [H, NCH], F32))
            decay = early.enter_context(nc.sbuf_tensor("decay", [H, NCH], F32))
            gate_bias = early.enter_context(nc.sbuf_tensor("gate_bias", [H, 2], F32))
        q_t = sb("q_t", [P, 2, H, P])
        k_t = sb("k_t", [P, 2, H, P])
        v_c = sb("v_c", [P, 2, H, VW])
        o_c = sb("o_c", [P, 2, DH])
        negm_b = sb("negm_b", [P, 2, H, P])
        winter_b = sb("winter_b", [P, 2, H, P])
        yc_c = sb("yc_c", [P, 2, H, P])
        x_c = sb("x_c", [P, 2, D])
        e_c = sb("e_c", [P, H, P])
        p_c = sb("p_c", [P, H, P])
        qs_c = sb("qs_c", [P, H, P])
        wk_c = sb("wk_c", [P, H, P])
        y_c = sb("y_c", [P, DH])
        y_hi = sb("y_hi", [P, 2, KT, P], F32R)
        y_lo = sb("y_lo", [P, 2, KT, P], F32R)
        small = sb("small", [P, 64])
        junk = sb("junk", [P, TB])
        t_post = sb("t_post", [P, D])
        xn = sb("xn", [P, 2, D])
        h2 = sb("h2", [P, D])
        h2_hi = sb("h2_hi", [P, 2, KT, P], F32R)
        h2_lo = sb("h2_lo", [P, 2, KT, P], F32R)
        den, rden, stats, aggr = small[:, 0:4], small[:, 4:8], small[:, 8:32], small[:, 32:40]
        var_h, rs_h, s_h = small[:, 40:44], small[:, 44:48], small[:, 48:52]
        ss, ss2, r1, r2 = small[:, 52:54], small[:, 54:56], small[:, 56:57], small[:, 57:58]

        block = ctx.enter_context(nc.Block())

        def by_head(a):
            return a.rearrange("p (h d) -> p h d", h=H)

        def head_ps(bank, h):
            return psum[:, bank + h // 2, (h % 2) * VW:(h % 2 + 1) * VW]

        @block.sync
        def _(sp):
            sp.dma_start(gi[:], dram["gates"][0:H]).then_inc(sem["gates_in"], 16)
            sp.dma_start(gf[:], dram["gates"][H:2 * H]).then_inc(sem["gates_in"], 16)
            sp.dma_start(gate_bias[:], dram["gate_bias"]).then_inc(sem["gates_in"], 16)
            sp.dma_start(par[:], dram["params_b"]).then_inc(sem["par_b"], 16)
            sp.dma_start(post_w[:], dram["post_w"].partition_broadcast(P)).then_inc(sem["par_b"], 16)
            for kt in range(KT):
                sp.dma_start(wo_raw[:, kt], dram["w_out"][kt]).then_inc(sem["wo_in"][kt], 16)
            sp.wait_ge(sem["rows_done"], 4)
            sp.dma_start(dram["rows"][0], t0[:]).then_inc(sem["rows_out"], 16)
            sp.dma_start(dram["rows"][1], t1[:]).then_inc(sem["rows_out"], 16)
            sp.dma_start(dram["decay"], decay[:]).then_inc(sem["rows_out"], 16)
            sp.wait_ge(sem["rows_out"], 48)
            sp.dma_start(decay_b[:], dram["decay"].partition_broadcast(P)).then_inc(sem["decay_in"], 16)
            sp.wait_ge(sem["cols_done"], 4)

            def load(c):
                b = c % 2
                at = slice(c * P, (c + 1) * P)
                if c >= 2:
                    sp.wait_ge(sem["scores"], c - 1)
                    sp.wait_ge(sem["qs"], c - 1)
                    sp.wait_ge(sem["z"], c - 1)
                    sp.wait_ge(sem["incr"], c - 1)
                    sp.wait_ge(sem["y"], c - 1)
                    sp.wait_ge(sem["yc_lo"], c - 1)
                for buf, src, s in ((q_t, dram["qk"][0:4, :, at], 0), (k_t, dram["qk"][4:8, :, at], 1),
                                    (yc_c, dram["yc"][:, :, at], 2)):
                    sp.dma_start(buf[:, b], src.rearrange("h p t -> p h t")).then_inc(sem["chunk_in"][b], 16)
                sp.dma_start(v_c[:, b, :, 0:HD], by_head(dram["v"][c])).then_inc(sem["chunk_in"][b], 16)
                sp.dma_start(o_c[:, b], dram["o"][c]).then_inc(sem["chunk_in"][b], 16)
                for buf, n in ((negm_b, 0), (winter_b, 1)):
                    sp.dma_start(buf[:, b], dram["rows"][n, :, at].partition_broadcast(P)).then_inc(sem["chunk_in"][b], 16)

            def load_x(c):
                if c >= 2:
                    sp.wait_ge(sem["xn"], c - 1)
                sp.dma_start(x_c[:, c % 2], dram["x"][c * P:(c + 1) * P]).then_inc(sem["xc_in_b"][c % 2], 16)

            load(0)
            for c in range(NCH + 4):
                if c >= 4:
                    sp.wait_ge(sem["h2_lo"], 2 * (c - 3))
                    at = slice((c - 4) * P, (c - 3) * P)
                    for buf, out in ((h2_hi, dram["h2_hi"]), (h2_lo, dram["h2_lo"])):
                        sp.dma_start(out[:, :, at], buf[:, c % 2].bitcast(F32)).then_inc(sem["h2_out"][c % 2], 16)
                if c + 1 < NCH:
                    load(c + 1)
                if c < NCH:
                    load_x(c)
                if 0 <= c - 2 < NCH:
                    sp.wait_ge(sem["xn"], c - 1)
                    sp.dma_start(dram["xn"][c - 2], xn[:, c % 2]).then_inc(sem["xn_out"][c % 2], 16)
            for b in range(2):
                sp.wait_ge(sem["h2_out"][b], 32 * NCH // 2)
                sp.wait_ge(sem["xn_out"][b], 16 * NCH // 2)

        def chunk_here(eng, c):
            eng.wait_ge(sem["chunk_in"][c % 2], 7 * 16 * (c // 2 + 1))

        @block.gpsimd
        def _(pool):
            nc.gpsimd.memset(ident[:], 0.0).then_inc(sem["ident"], 1)
            nc.gpsimd.memset(mask[:], 0.0).then_inc(sem["ident"], 1)
            nc.gpsimd.memset(rows[:], 0.0).then_inc(sem["ident"], 1)
            pool.wait_ge(sem["ident"], 3)
            nc.gpsimd.affine_select(out=ident[:], in_=ident[:], compare_op=ALU.not_equal, fill=1.0, base=0,
                                    pattern=[[-1, P]], channel_multiplier=1).then_inc(sem["ident"], 1)
            nc.gpsimd.affine_select(out=mask[:], in_=mask[:], compare_op=ALU.is_ge, fill=FAR, base=0,
                                    pattern=[[1, P]], channel_multiplier=-1).then_inc(sem["ident"], 1)
            pool.wait_ge(sem["rows_out"], 48)
            pool.wait_ge(sem["cols_done"], 4)
            nc.gpsimd.memset(v_c[:, :, :, HD:VW], 1.0).then_inc(sem["v_ones"], 1)
            for c in range(NCH):
                chunk_here(pool, c)
                if c >= 1:
                    pool.wait_ge(sem["num"], c)
                nc.gpsimd.tensor_tensor(qs_c[:], q_t[:, c % 2], winter_b[:, c % 2], ALU.mult).then_inc(sem["qs"], 1)

        @block.tensor
        def _(pe):
            def scores(c):
                chunk_here(pe, c)
                if c >= 1:
                    pe.wait_ge(sem["p"], c)
                    pe.wait_ge(sem["wk"], c)
                for h in range(H):
                    mm = nc.tensor.matmul(psum[:, 0, h * P:(h + 1) * P], k_t[:, c % 2, h], q_t[:, c % 2, h],
                                          start=True, stop=True)
                for h in range(H):
                    mm = nc.tensor.transpose(psum[:, 1, h * P:(h + 1) * P], k_t[:, c % 2, h], ident[:])
                mm.then_inc(sem["scores"], 1)

            def numerators(c):
                pe.wait_ge(sem["p"], c + 1)
                pe.wait_ge(sem["qs"], c + 1)
                pe.wait_ge(sem["wk"], c + 1)
                if c == 0:
                    pe.wait_ge(sem["v_ones"], 1)
                if c >= 1:
                    pe.wait_ge(sem["y_lo"], c)
                pe.wait_ge(sem["state"], c + 1)
                if c >= 4:
                    pe.wait_ge(sem["h2_lo"], 2 * (c - 3))
                for h in range(H):
                    nc.tensor.matmul(head_ps(2, h), p_c[:, h], v_c[:, c % 2, h], start=True, stop=False)
                    mm = nc.tensor.matmul(head_ps(2, h), qs_c[:, h], state[:, h], start=False, stop=True)
                mm.then_inc(sem["num"], 1)
                for h in range(H):
                    mm = nc.tensor.matmul(head_ps(4, h), wk_c[:, h], v_c[:, c % 2, h], start=True, stop=True)
                mm.then_inc(sem["incr"], 1)

            def transpose_y(c):
                pe.wait_ge(sem["y"], c + 1)
                for h in range(H):
                    mm = nc.tensor.transpose(psum[:, 2, h * P:(h + 1) * P], y_c[:, h * P:(h + 1) * P], ident[:])
                mm.then_inc(sem["y_t"], 1)

            def project(c, half):
                b = c % 2
                if half == 0:
                    pe.wait_ge(sem["y_hi"], c + 1)
                    pe.wait_ge(sem["y_lo"], c + 1)
                    pe.wait_ge(sem["yc_hi"], c + 1)
                    pe.wait_ge(sem["yc_lo"], c + 1)
                if c == 0:
                    pe.wait_ge(sem["wo_lo"], KT)
                    pe.wait_ge(sem["wo_hi"], KT)
                else:
                    pe.wait_ge(sem["t_post"], 2 * (c - 1) + half + 1)
                    pe.wait_ge(sem["ss"], 2 * (c - 1) + half + 1)
                cols_ = slice(half * TB, (half + 1) * TB)
                for kt in range(KT):
                    pairs = [(y_hi[:, b, kt], wo_hi[:, kt, cols_]), (y_hi[:, b, kt], wo_lo[:, kt, cols_]),
                             (y_lo[:, b, kt], wo_hi[:, kt, cols_])]
                    for i, (l, r) in enumerate(pairs):
                        mm = nc.tensor.matmul(psum[:, 6 + half, :], l, r, start=kt == 0 and i == 0,
                                              stop=kt == KT - 1 and i == 2)
                mm.then_inc(sem["out_proj"], 1)

            def transpose_h2(c):
                pe.wait_ge(sem["h2"], c + 1)
                if c >= 1:
                    pe.wait_ge(sem["h2_lo"], 2 * c)
                pe.wait_ge(sem["state"], min(c + 4, NCH) + 1)
                for kt in range(KT):
                    mm = nc.tensor.transpose(psum[:, 4 + kt // 4, (kt % 4) * P:(kt % 4 + 1) * P], h2[:, kt * P:(kt + 1) * P],
                                             ident[:])
                    if kt % 4 == 3:
                        mm.then_inc(sem["h2_t"], 1)

            pe.wait_ge(sem["ident"], 5)
            pe.wait_ge(sem["rows_done"], 4)
            for c in range(NCH):
                nc_bank = c // 4
                mm = nc.tensor.transpose(psum[:, nc_bank, (c % 4) * P:(c % 4 + 1) * P], rows[:, c * P:(c + 1) * P], ident[:])
                if c % 4 == 3:
                    mm.then_inc(sem["cols_t"], 1)
            pe.wait_ge(sem["cols_done"], 4)
            scores(0)
            for c in range(NCH + 3):
                if c < NCH:
                    numerators(c)
                if 1 <= c <= NCH:
                    project(c - 1, 0)
                if c + 1 < NCH:
                    scores(c + 1)
                if c < NCH:
                    transpose_y(c)
                if c >= 3:
                    transpose_h2(c - 3)
                if 1 <= c <= NCH:
                    project(c - 1, 1)

        @block.scalar
        def _(act):
            n_self = [0]

            def link(ins):
                n_self[0] += 1
                ins.then_inc(sem["act_b"], 1)
                act.wait_ge(sem["act_b"], n_self[0])

            def rsqrt(out, in_, scale, signal):
                link(nc.scalar.activation(out, in_, ACT.Ln, scale=scale, bias=eps[:, 0:1]))
                nc.scalar.activation(out, out, ACT.Exp, scale=-0.5).then_inc(signal, 1)

            nc.scalar.preload_act_table_set(LN_EXP)
            act.wait_ge(sem["gates_in"], 48)
            link(nc.scalar.activation(gf[:], gf[:], ACT.Identity, bias=gate_bias[:, 1:2]))
            link(nc.scalar.activation(t0[:], gf[:], ACT.Abs))
            link(nc.scalar.activation(t0[:], t0[:], ACT.Exp, scale=-1.0))
            nc.scalar.activation(t0[:], t0[:], ACT.Ln, bias=1.0).then_inc(sem["softplus"], 1)

            def split_wo(kt):
                act.wait_ge(sem["wo_in"][kt], 16)
                nc.scalar.activation(wo_hi[:, kt], wo_raw[:, kt], ACT.Copy,
                                     scale=par[:, WO_SCALE + kt:WO_SCALE + kt + 1]).then_inc(sem["wo_hi"], 1)

            act.wait_ge(sem["wo_scale"], 1)
            for kt in range(KT):
                split_wo(kt)
            act.wait_ge(sem["ident"], 3)
            act.wait_ge(sem["exps"], 1)
            nc.scalar.activation(t1[:], t1[:], ACT.Exp).then_inc(sem["exps_out"], 1)
            act.wait_ge(sem["exps"], 2)
            nc.scalar.activation(rows[32 * COL_WK:32 * COL_WK + H, :], t2[:], ACT.Exp).then_inc(sem["rows_done"], 1)
            nc.scalar.activation(rows[32 * COL_FLOOR:32 * COL_FLOOR + H, :], gf[:], ACT.Exp).then_inc(sem["rows_done"], 1)
            nc.scalar.activation(decay[:], decay[:], ACT.Exp).then_inc(sem["rows_done"], 1)

            def weights(c):
                act.wait_ge(sem["z"], c + 1)
                if c >= 1:
                    act.wait_ge(sem["p"], c)
                nc.scalar.activation(e_c[:], p_c[:], ACT.Exp).then_inc(sem["e"], 1)

            def wk(c):
                act.wait_ge(sem["scores"], c + 1)
                if c >= 1:
                    act.wait_ge(sem["incr"], c)
                for h in range(H):
                    a = nc.scalar.activation(wk_c[:, h], psum[:, 1, h * P:(h + 1) * P], ACT.Copy,
                                             scale=cols[:, c, COL_WK, h:h + 1])
                a.then_inc(sem["wk"], 1)

            def yc_high(c):
                if c >= 2:
                    act.wait_ge(sem["out_proj"], 2 * (c - 1))
                nc.scalar.activation(y_hi[:, c % 2, H:KT], yc_c[:, c % 2], ACT.Copy).then_inc(sem["yc_hi"], 1)

            def denominators(c):
                act.wait_ge(sem["num"], c + 1)
                if c >= 1:
                    act.wait_ge(sem["y"], c)
                for bank in range(2):
                    a = nc.scalar.activation(den[:, 2 * bank:2 * bank + 2], psum[:, 2 + bank, HD:2 * VW:VW], ACT.Abs)
                a.then_inc(sem["den"], 1)

            def squares(c, half):
                act.wait_ge(sem["out_proj"], 2 * c + half + 1)
                if half:
                    act.wait_ge(sem["ss"], 2 * c + 1)
                elif c >= 1:
                    act.wait_ge(sem["ss_sum"], c)
                    act.wait_ge(sem["ss2"], 2 * c)
                nc.scalar.activation(junk[:], psum[:, 6 + half, :], ACT.Square,
                                     accum_out=ss[:, half:half + 1]).then_inc(sem["ss"], 1)

            def pre_mlp_squares(c):
                act.wait_ge(sem["xn"], c + 1)
                for half in range(2):
                    act.wait_ge(sem["ss"], 2 * c + 2)
                    if half:
                        act.wait_ge(sem["ss2"], 2 * c + 1)
                    nc.scalar.activation(junk[:], xn[:, c % 2, half * TB:(half + 1) * TB], ACT.Square,
                                         accum_out=ss2[:, half:half + 1]).then_inc(sem["ss2"], 1)

            def pre_mlp(c):
                act.wait_ge(sem["ss2_sum"], c + 1)
                rsqrt(r2, r2, 1.0 / D, sem["r2"])
                act.wait_ge(sem["r2"], c + 1)
                if c >= 1:
                    act.wait_ge(sem["h2_t"], 2 * c)
                nc.scalar.activation(h2[:], xn[:, c % 2], ACT.Copy, scale=r2).then_inc(sem["h2"], 1)

            def h2_high(c):
                for b in range(2):
                    act.wait_ge(sem["h2_t"], 2 * c + b + 1)
                    if c >= 2:
                        act.wait_ge(sem["h2_out"][c % 2], 32 * (c // 2))
                    nc.scalar.activation(h2_hi[:, c % 2, 4 * b:4 * b + 4], by_head(psum[:, 4 + b, :]), ACT.Copy).then_inc(sem["h2_hi"], 1)

            act.wait_ge(sem["eps_b"], 1)
            weights(0)
            wk(0)
            yc_high(0)
            for c in range(NCH + 3):
                if c < NCH:
                    denominators(c)
                    act.wait_ge(sem["var_h"], c + 1)
                    rsqrt(rs_h, var_h, 1.0, sem["rs_h"])
                if c + 1 < NCH:
                    weights(c + 1)
                if 2 <= c < NCH + 2:
                    pre_mlp_squares(c - 2)
                if 1 <= c <= NCH:
                    squares(c - 1, 0)
                if c + 1 < NCH:
                    wk(c + 1)
                if c < NCH:
                    act.wait_ge(sem["y_t"], c + 1)
                    nc.scalar.activation(y_hi[:, c % 2, 0:H], by_head(psum[:, 2, :]), ACT.Copy).then_inc(sem["y_hi"], 1)
                if c >= 3:
                    h2_high(c - 3)
                if 2 <= c < NCH + 2:
                    pre_mlp(c - 2)
                if 1 <= c <= NCH:
                    squares(c - 1, 1)
                if c + 1 < NCH:
                    yc_high(c + 1)
                if 1 <= c <= NCH:
                    act.wait_ge(sem["ss_sum"], c)
                    rsqrt(r1, r1, 1.0 / D, sem["r1"])

        @block.vector
        def _(dve):
            n_self = [0]

            def link(ins):
                n_self[0] += 1
                ins.then_inc(sem["dve_b"], 1)
                dve.wait_ge(sem["dve_b"], n_self[0])

            def by_chunk(a):
                return a.rearrange("p (c l) -> p c l", l=P)

            nc.vector.memset(eps[:], EPS).then_inc(sem["eps_b"], 1)
            link(nc.vector.memset(keep[:], 1.0))
            link(nc.vector.memset(by_chunk(keep[:])[:, :, 0:1], 0.0))
            link(nc.vector.memset(step[:], 0.0))
            link(nc.vector.memset(m_prev[:], 0.0))
            nc.vector.memset(state[:], 0.0).then_inc(sem["state"], 1)
            dve.wait_ge(sem["par_b"], 32)
            nc.vector.tensor_scalar(par[:, WO_SCALE:WO_SCALE + H], par[:, WO_SCALE:WO_SCALE + H], 0.5, None,
                                    ALU.mult).then_inc(sem["wo_scale"], 1)
            dve.wait_ge(sem["gates_in"], 48)
            link(nc.vector.tensor_scalar(gi[:], gi[:], gate_bias[:, 0:1], None, ALU.add))
            dve.wait_ge(sem["softplus"], 1)
            link(nc.vector.scalar_tensor_tensor(out=gf[:], in0=gf[:], scalar=0.0, in1=t0[:], op0=ALU.min,
                                                op1=ALU.subtract))
            link(nc.vector.tensor_tensor_scan(t1[:], keep[:], gf[:], 0.0, ALU.mult, ALU.add))
            link(nc.vector.tensor_copy(by_chunk(step[:])[:, 1:NCH, 0:1], by_chunk(t1[:])[:, 0:NCH - 1, P - 1:P]))
            dve.wait_ge(sem["ident"], 3)
            a_row = rows[32 * COL_A:32 * COL_A + H, :]
            link(nc.vector.tensor_tensor(a_row, gi[:], t1[:], ALU.subtract))
            link(nc.vector.tensor_tensor_scan(t2[:], step[:], a_row, 0.0, ALU.add, ALU.max))
            last = by_chunk(t2[:])[:, :, P - 1:P]
            link(nc.vector.tensor_tensor(m_prev[:, 1:NCH].unsqueeze(2), by_chunk(t1[:])[:, 0:NCH - 1, P - 1:P],
                                         last[:, 0:NCH - 1], ALU.add))
            link(nc.vector.tensor_tensor(decay[:].unsqueeze(2), m_prev[:].unsqueeze(2), last, ALU.subtract))
            link(nc.vector.tensor_scalar(t0[:], t2[:], -1.0, None, ALU.mult))
            link(nc.vector.tensor_tensor(gf[:], t0[:], t1[:], ALU.subtract))
            nc.vector.tensor_tensor(by_chunk(t1[:]), by_chunk(t0[:]), m_prev[:].unsqueeze(2).to_broadcast([H, NCH, P]),
                                    ALU.add).then_inc(sem["exps"], 1)
            nc.vector.tensor_copy(gi[:, 0:NCH].unsqueeze(2), last).then_inc(sem["gi_last"], 1)
            dve.wait_ge(sem["gi_last"], 1)
            nc.vector.tensor_tensor(by_chunk(t2[:]), by_chunk(a_row), gi[:, 0:NCH].unsqueeze(2).to_broadcast([H, NCH, P]),
                                    ALU.subtract).then_inc(sem["exps"], 1)
            dve.wait_ge(sem["exps_out"], 1)
            nc.vector.tensor_scalar(t1[:], t1[:], SCALE, None, ALU.mult).then_inc(sem["rows_done"], 1)

            for kt in range(KT):
                dve.wait_ge(sem["wo_hi"], kt + 1)
                nc.vector.scalar_tensor_tensor(out=wo_lo[:, kt], in0=wo_raw[:, kt],
                                               scalar=par[:, WO_SCALE + kt:WO_SCALE + kt + 1],
                                               in1=wo_hi[:, kt].bitcast(F32), op0=ALU.mult,
                                               op1=ALU.subtract).then_inc(sem["wo_lo"], 1)
            for b in range(4):
                dve.wait_ge(sem["cols_t"], b + 1)
                for q in range(3):
                    i = nc.vector.tensor_copy(cols[:, 4 * b:4 * b + 4, q, :],
                                              by_chunk(psum[:, b, :])[:, :, 32 * q:32 * q + H])
                i.then_inc(sem["cols_done"], 1)
            dve.wait_ge(sem["decay_in"], 16)
            dve.wait_ge(sem["cols_done"], 4)

            def exponents(c):
                chunk_here(dve, c)
                if c >= 1:
                    dve.wait_ge(sem["num"], c)
                for h in range(H):
                    i = nc.vector.scalar_tensor_tensor(out=p_c[:, h], in0=negm_b[:, c % 2, h],
                                                       scalar=cols[:, c, COL_A, h:h + 1], in1=mask[:], op0=ALU.add,
                                                       op1=ALU.min)
                i.then_inc(sem["z"], 1)

            def weigh(c):
                dve.wait_ge(sem["e"], c + 1)
                dve.wait_ge(sem["scores"], c + 1)
                nc.vector.scalar_tensor_tensor(out=p_c[:], in0=by_head(psum[:, 0, :]), scalar=SCALE, in1=e_c[:],
                                               op0=ALU.mult, op1=ALU.mult).then_inc(sem["p"], 1)

            def yc_low(c):
                dve.wait_ge(sem["yc_hi"], c + 1)
                nc.vector.tensor_tensor(y_lo[:, c % 2, H:KT], yc_c[:, c % 2], y_hi[:, c % 2, H:KT].bitcast(F32),
                                        ALU.subtract).then_inc(sem["yc_lo"], 1)

            def update_state(c):
                dve.wait_ge(sem["incr"], c + 1)
                for h in range(H):
                    i = nc.vector.scalar_tensor_tensor(out=state[:, h], in0=state[:, h], scalar=decay_b[:, h, c:c + 1],
                                                       in1=head_ps(4, h), op0=ALU.mult, op1=ALU.add)
                i.then_inc(sem["state"], 1)

            def normalise_heads(c):
                dve.wait_ge(sem["den"], c + 1)
                for h in range(H):
                    i = nc.vector.bn_stats(stats[:, 6 * h:6 * h + 6], head_ps(2, h)[:, 0:HD])
                link(i)
                for h in range(H):
                    i = nc.vector.bn_aggr(aggr[:, 2 * h:2 * h + 2], stats[:, 6 * h:6 * h + 6])
                link(i)
                link(nc.vector.tensor_tensor(den, den, cols[:, c, COL_FLOOR, :], ALU.max))
                link(nc.vector.reciprocal(rden, den))
                link(nc.vector.tensor_tensor(var_h, aggr[:, 1:8:2], rden, ALU.mult))
                nc.vector.tensor_tensor(var_h, var_h, rden, ALU.mult).then_inc(sem["var_h"], 1)
                dve.wait_ge(sem["rs_h"], c + 1)
                link(nc.vector.tensor_tensor(s_h, rs_h, rden, ALU.mult))
                if c >= 1:
                    dve.wait_ge(sem["y_t"], c)
                for h in range(H):
                    i = nc.vector.tensor_scalar(y_c[:, h * P:(h + 1) * P], head_ps(2, h)[:, 0:HD],
                                                aggr[:, 2 * h:2 * h + 1], s_h[:, h:h + 1], ALU.subtract, ALU.mult)
                link(i)
                nc.vector.scalar_tensor_tensor(out=y_c[:], in0=o_c[:, c % 2], scalar=1.0, in1=y_c[:], op0=ALU.add,
                                               op1=ALU.mult).then_inc(sem["y"], 1)

            def y_low(c):
                dve.wait_ge(sem["y_hi"], c + 1)
                nc.vector.tensor_tensor(y_lo[:, c % 2, 0:H], by_head(psum[:, 2, :]), y_hi[:, c % 2, 0:H].bitcast(F32),
                                        ALU.subtract).then_inc(sem["y_lo"], 1)

            def post_scale(c, half):
                at = slice(half * TB, (half + 1) * TB)
                dve.wait_ge(sem["ss"], 2 * c + half + 1)
                if c >= 1:
                    dve.wait_ge(sem["xn"], c)
                if half == 1:
                    nc.vector.tensor_tensor(r1, ss[:, 0:1], ss[:, 1:2], ALU.add).then_inc(sem["ss_sum"], 1)
                nc.vector.tensor_tensor(t_post[:, at], psum[:, 6 + half, :], post_w[:, at],
                                        ALU.mult).then_inc(sem["t_post"], 1)

            def residual(c):
                dve.wait_ge(sem["r1"], c + 1)
                dve.wait_ge(sem["t_post"], 2 * c + 2)
                dve.wait_ge(sem["xc_in_b"][c % 2], 16 * (c // 2 + 1))
                if c >= 2:
                    dve.wait_ge(sem["h2"], c - 1)
                    dve.wait_ge(sem["xn_out"][c % 2], 16 * (c // 2))
                nc.vector.scalar_tensor_tensor(out=xn[:, c % 2], in0=t_post[:], scalar=r1, in1=x_c[:, c % 2],
                                               op0=ALU.mult, op1=ALU.add).then_inc(sem["xn"], 1)

            def sum_squares(c):
                dve.wait_ge(sem["ss2"], 2 * c + 2)
                if c >= 1:
                    dve.wait_ge(sem["h2"], c)
                nc.vector.tensor_tensor(r2, ss2[:, 0:1], ss2[:, 1:2], ALU.add).then_inc(sem["ss2_sum"], 1)

            def h2_low(c):
                for b in range(2):
                    dve.wait_ge(sem["h2_hi"], 2 * c + b + 1)
                    if c >= 2:
                        dve.wait_ge(sem["h2_out"][c % 2], 32 * (c // 2))
                    nc.vector.tensor_tensor(h2_lo[:, c % 2, 4 * b:4 * b + 4], by_head(psum[:, 4 + b, :]),
                                            h2_hi[:, c % 2, 4 * b:4 * b + 4].bitcast(F32), ALU.subtract).then_inc(sem["h2_lo"], 1)

            exponents(0)
            weigh(0)
            yc_low(0)
            for c in range(NCH + 3):
                if c < NCH:
                    update_state(c)
                    normalise_heads(c)
                if c + 1 < NCH:
                    exponents(c + 1)
                if 2 <= c < NCH + 2:
                    residual(c - 2)
                if c + 1 < NCH:
                    weigh(c + 1)
                if c < NCH:
                    y_low(c)
                if c >= 3:
                    h2_low(c - 3)
                if 2 <= c < NCH + 2:
                    sum_squares(c - 2)
                if 1 <= c <= NCH:
                    post_scale(c - 1, 0)
                    post_scale(c - 1, 1)
                if c + 1 < NCH:
                    yc_low(c + 1)


BLOCK = 1024
NBLOCK = S // BLOCK
NT = BLOCK // P
CHUNK_F = 256
NSTEP = FF // CHUNK_F
LAST = NBLOCK * NSTEP - 1
Q_RING = 3


def phase_c(nc, sem, psum, dram):
    with ExitStack() as ctx:
        def sb(name, shape, dt=F32):
            return ctx.enter_context(nc.sbuf_tensor(name, shape, dt))

        x_hi = sb("x_hi", [P, KT, BLOCK], F32R)
        x_lo = sb("x_lo", [P, KT, BLOCK], F32R)
        acc = sb("acc", [P, NT, D])
        hid_hi = sb("hid_hi", [P, 2, 2, BLOCK], F32R)
        hid_lo = sb("hid_lo", [P, 2, 2, BLOCK], F32R)
        w1_hi = sb("w1_hi", [P, 2, KT, P], F32R)
        w1_lo = sb("w1_lo", [P, 2, KT, P], F32R)
        w2_hi = sb("w2_hi", [P, 2, D], F32R)
        w2_lo = sb("w2_lo", [P, 2, D], F32R)
        w1_raw = sb("w1_raw", [P, 2, KT, P])
        w2_raw = sb("w2_raw", [P, 2, D])
        relu = sb("relu", [P, 2, TB])
        sq = sb("sq", [P, 2, TB])
        par = sb("par_c", [P, KT])
        wpost = sb("wpost_c", [P, D])
        eps = sb("eps_c", [P, 1])
        ss = sb("ss_c", [P, NT])
        rs = sb("rs_c", [P, NT])
        xn = sb("xn_c", [P, Q_RING, D])
        junk = sb("junk_c", [P, D])

        block = ctx.enter_context(nc.Block())

        @block.sync
        def _(sp):
            def load_w1(n, m, fresh=False):
                for f in range(2):
                    if not fresh:
                        sp.wait_ge(sem["w1_hi"], 2 * n + f - 1)
                        sp.wait_ge(sem["w1_lo"], 2 * n + f - 1)
                    sp.dma_start(w1_raw[:, f], dram["w1"][bass.ds(2 * m + f, 1)]
                                 .rearrange("a p k c -> (a p) k c")).then_inc(sem["w1_in"][f], 16)

            def load_w2(n, m, fresh=False):
                for f in range(2):
                    if not fresh:
                        sp.wait_ge(sem["w2_hi"], 2 * n + f - 1)
                        sp.wait_ge(sem["w2_lo"], 2 * n + f - 1)
                    sp.dma_start(w2_raw[:, f], dram["w2"][bass.ds(2 * m + f, 1)]
                                 .rearrange("a p c -> (a p) c")).then_inc(sem["w2_in"][f], 16)

            def load_x(b):
                for tb in range(BLOCK // TB):
                    for buf, src in ((x_hi, dram["h2_hi"]), (x_lo, dram["h2_lo"])):
                        at = slice(b * BLOCK + tb * TB, b * BLOCK + (tb + 1) * TB)
                        sp.dma_start(buf[:, :, tb * TB:(tb + 1) * TB].bitcast(F32), src[:, :, at]).then_inc(sem["xc_in"][tb], 16)

            def load_residual(i):
                if i >= Q_RING:
                    sp.wait_ge(sem["fin"], i - Q_RING + 1)
                sp.dma_start(xn[:, i % Q_RING], dram["xn"][i]).then_inc(sem["xnc_in"][i % Q_RING], 16)

            sp.dma_start(par[:], dram["params_c"]).then_inc(sem["par_c"], 16)
            load_w1(0, 0, fresh=True)
            load_x(0)
            sp.dma_start(wpost[:], dram["post_mlp_w"].partition_broadcast(P)).then_inc(sem["par_c"], 16)
            load_w1(1, 1)
            load_w2(0, 0, fresh=True)
            for i in range(Q_RING):
                load_residual(i)
            for b in range(NBLOCK):
                n0 = NSTEP * b
                with sp.Fori(1, NSTEP - 1) as m:
                    load_w1(n0 + m + 1, m + 1)
                    load_w2(n0 + m, m)
                if b + 1 < NBLOCK:
                    load_w1(n0 + NSTEP, 0)
                load_w2(n0 + NSTEP - 1, NSTEP - 1)
                if b + 1 < NBLOCK:
                    sp.wait_ge(sem["ff1"], 4 * NSTEP * (b + 1))
                    load_x(b + 1)
                    load_w1(n0 + NSTEP + 1, 1)
                    load_w2(n0 + NSTEP, 0)
                for i in range(NT * b, NT * (b + 1)):
                    sp.wait_ge(sem["fin"], i + 1)
                    sp.dma_start(dram["out"][i], acc[:, i % NT, :]).then_inc(sem["out"], 16)
                    if i + Q_RING < NT * NBLOCK:
                        load_residual(i + Q_RING)
            sp.wait_ge(sem["out"], 16 * S // P)

        @block.gpsimd
        def _(pool):
            for i in range(NT * NBLOCK):
                pool.wait_ge(sem["fmul"], i + 1)
                pool.wait_ge(sem["xnc_in"][i % Q_RING], 16 * (i // Q_RING + 1))
                nc.gpsimd.tensor_tensor(acc[:, i % NT], acc[:, i % NT], xn[:, i % Q_RING], ALU.add).then_inc(sem["fin"], 1)

        @block.tensor
        def _(pe):
            def first(n, x_wait=None, fresh=False):
                for f in range(2):
                    pe.wait_ge(sem["w1_hi"], 2 * n + f + 1)
                    pe.wait_ge(sem["w1_lo"], 2 * n + f + 1)
                    for tb in range(2):
                        if x_wait is not None and f == 0:
                            pe.wait_ge(sem["xc_in"][tb], x_wait)
                        if not fresh or f == 1:
                            pe.wait_ge(sem["relu"], 4 * n + 2 * f + tb - 1)
                        for kt in range(KT):
                            cols = slice(tb * TB, (tb + 1) * TB)
                            pairs = [(w1_hi[:, f, kt], x_hi[:, kt, cols]), (w1_hi[:, f, kt], x_lo[:, kt, cols]),
                                     (w1_lo[:, f, kt], x_hi[:, kt, cols])]
                            for i, (l, r) in enumerate(pairs):
                                mm = nc.tensor.matmul(psum[:, tb, :], l, r, start=kt == 0 and i == 0,
                                                      stop=kt == KT - 1 and i == 2)
                        mm.then_inc(sem["ff1"], 1)

            def second(n, par_, fresh=False):
                pe.wait_ge(sem["w2_hi"], 2 * n + 2)
                pe.wait_ge(sem["w2_lo"], 2 * n + 2)
                pe.wait_ge(sem["hid_lo"], 4 * n + 4)
                for t in range(NT):
                    for half in range(2):
                        j = 2 * t + half
                        if not fresh or j >= 4:
                            pe.wait_ge(sem["acc"], 16 * n + j - 3)
                        cols = slice(half * TB, (half + 1) * TB)
                        tok = slice(t * P, (t + 1) * P)
                        for f in range(2):
                            pairs = [(hid_hi[:, par_, f, tok], w2_hi[:, f, cols]), (hid_hi[:, par_, f, tok], w2_lo[:, f, cols]),
                                     (hid_lo[:, par_, f, tok], w2_hi[:, f, cols])]
                            for i, (l, r) in enumerate(pairs):
                                mm = nc.tensor.matmul(psum[:, 2 + j % 4, :], l, r, start=f == 0 and i == 0, stop=f == 1 and i == 2)
                        mm.then_inc(sem["ff2"], 1)

            for b in range(NBLOCK):
                n0 = NSTEP * b
                first(n0, x_wait=32 * (b + 1), fresh=b == 0)
                first(n0 + 1)
                second(n0, 0, fresh=b == 0)
                with pe.Fori(n0 + 2, n0 + NSTEP, 2) as n:
                    first(n)
                    second(n - 1, 1)
                    first(n + 1)
                    second(n, 0)
                second(n0 + NSTEP - 1, 1)

        @block.scalar
        def _(act):
            def split_w1(n, f, fresh=False):
                act.wait_ge(sem["w1_in"][f], 16 * n + 16)
                if not fresh:
                    act.wait_ge(sem["ff1"], 4 * n + 2 * f - 2)
                for kt in range(KT):
                    i = nc.scalar.activation(w1_hi[:, f, kt], w1_raw[:, f, kt], ACT.Copy, scale=par[:, kt:kt + 1])
                i.then_inc(sem["w1_hi"], 1)

            def split_w2(n, fresh=False):
                for f in range(2):
                    act.wait_ge(sem["w2_in"][f], 16 * n + 16)
                    if not fresh:
                        act.wait_ge(sem["ff2"], 16 * n)
                    nc.scalar.activation(w2_hi[:, f], w2_raw[:, f], ACT.Copy).then_inc(sem["w2_hi"], 1)

            def hidden(n, f, tb, par_, early=0):
                g = 4 * n + 2 * f + tb
                act.wait_ge(sem["ff1"], g + 1)
                if early != 1 or f == 1:
                    act.wait_ge(sem["sq"], g - 1)
                nc.scalar.activation(relu[:, tb], psum[:, tb, :], ACT.Relu).then_inc(sem["relu"], 1)
                act.wait_ge(sem["relu"], g + 1)
                if not early:
                    act.wait_ge(sem["ff2"], 16 * n - 16)
                nc.scalar.activation(hid_hi[:, par_, f, tb * TB:(tb + 1) * TB], relu[:, tb], ACT.Square).then_inc(sem["hid_hi"], 1)

            def step(n, par_, early=0, more=True):
                for f in range(2):
                    for tb in range(2):
                        hidden(n, f, tb, par_, early)
                    if more:
                        split_w1(n + 1, f)

            def final_norm(b):
                for t in range(NT):
                    i = NT * b + t
                    act.wait_ge(sem["acc"], 16 * NSTEP * (b + 1) - 16 + 2 * t + 2)
                    if i >= 1:
                        act.wait_ge(sem["fss"], i)
                    nc.scalar.activation(junk[:], acc[:, t, :], ACT.Square, accum_out=ss[:, t:t + 1]).then_inc(sem["fss"], 1)
                    act.wait_ge(sem["fss"], i + 1)
                    if b >= 1:
                        act.wait_ge(sem["fmul"], i - NT + 1)
                    nc.scalar.activation(rs[:, t:t + 1], ss[:, t:t + 1], ACT.Ln, scale=1.0 / D,
                                         bias=eps[:, 0:1]).then_inc(sem["fln"], 1)
                    act.wait_ge(sem["fln"], i + 1)
                    nc.scalar.activation(rs[:, t:t + 1], rs[:, t:t + 1], ACT.Exp, scale=-0.5).then_inc(sem["frs"], 1)

            nc.scalar.preload_act_table_set(LN_EXP)
            act.wait_ge(sem["par_c"], 16)
            act.wait_ge(sem["eps_c"], 1)
            split_w1(0, 0, fresh=True)
            split_w1(0, 1, fresh=True)
            for b in range(NBLOCK):
                n0 = NSTEP * b
                step(n0, 0, early=1 if b == 0 else 0)
                split_w2(n0, fresh=b == 0)
                step(n0 + 1, 1, early=2 if b == 0 else 0)
                with act.Fori(n0 + 2, n0 + NSTEP - 2, 2) as n:
                    split_w2(n - 1)
                    step(n, 0)
                    split_w2(n)
                    step(n + 1, 1)
                n = n0 + NSTEP - 2
                split_w2(n - 1)
                step(n, 0)
                split_w2(n)
                step(n + 1, 1, more=b + 1 < NBLOCK)
                split_w2(n + 1)
                final_norm(b)

        @block.vector
        def _(dve):
            def split_w1(n, f):
                dve.wait_ge(sem["w1_hi"], 2 * n + f + 1)
                for kt in range(KT):
                    i = nc.vector.scalar_tensor_tensor(out=w1_lo[:, f, kt], in0=w1_raw[:, f, kt], scalar=par[:, kt:kt + 1],
                                                       in1=w1_hi[:, f, kt].bitcast(F32), op0=ALU.mult, op1=ALU.subtract)
                i.then_inc(sem["w1_lo"], 1)

            def split_w2(n):
                for f in range(2):
                    dve.wait_ge(sem["w2_hi"], 2 * n + f + 1)
                    nc.vector.tensor_tensor(w2_lo[:, f], w2_raw[:, f], w2_hi[:, f].bitcast(F32),
                                            ALU.subtract).then_inc(sem["w2_lo"], 1)

            def hidden(n, f, tb, par_, fresh=False):
                g = 4 * n + 2 * f + tb
                dve.wait_ge(sem["relu"], g + 1)
                if not fresh or f == 1:
                    dve.wait_ge(sem["hid_lo"], g - 1)
                nc.vector.tensor_tensor(sq[:, tb], relu[:, tb], relu[:, tb], ALU.mult).then_inc(sem["sq"], 1)
                dve.wait_ge(sem["sq"], g + 1)
                dve.wait_ge(sem["hid_hi"], g + 1)
                at = slice(tb * TB, (tb + 1) * TB)
                nc.vector.tensor_tensor(hid_lo[:, par_, f, at], sq[:, tb], hid_hi[:, par_, f, at].bitcast(F32),
                                        ALU.subtract).then_inc(sem["hid_lo"], 1)

            def add(n, j):
                dve.wait_ge(sem["ff2"], 16 * n + j + 1)
                dve.wait_ge(sem["acc"], 16 * n + j - 15)
                out = acc[:, j // 2, j % 2 * TB:(j % 2 + 1) * TB]
                nc.vector.tensor_tensor(out, out, psum[:, 2 + j % 4, :], ALU.add).then_inc(sem["acc"], 1)

            def step(n, par_, fresh=False):
                for f in range(2):
                    for tb in range(2):
                        hidden(n, f, tb, par_, fresh)
                    if f == 0:
                        split_w1(n + 1, 0)

            def turn(n, par_, first=None):
                split_w2(n - 1)
                step(n, par_)
                for j in range(2 * NT):
                    if first is None:
                        add(n - 1, j)
                    else:
                        dve.wait_ge(sem["ff2"], 16 * (n - 1) + j + 1)
                        if first >= 1 and j == 0:
                            dve.wait_ge(sem["out"], 16 * NT * first)
                        nc.vector.tensor_copy(acc[:, j // 2, j % 2 * TB:(j % 2 + 1) * TB],
                                              psum[:, 2 + j % 4, :]).then_inc(sem["acc"], 1)
                    if j == 3:
                        split_w1(n + 1, 1)

            def scale_out(b, t):
                i = NT * b + t
                dve.wait_ge(sem["frs"], i + 1)
                nc.vector.scalar_tensor_tensor(out=acc[:, t], in0=acc[:, t], scalar=rs[:, t:t + 1], in1=wpost[:],
                                               op0=ALU.mult, op1=ALU.mult).then_inc(sem["fmul"], 1)

            nc.vector.memset(eps[:], EPS).then_inc(sem["eps_c"], 1)
            dve.wait_ge(sem["par_c"], 32)
            split_w1(0, 0)
            split_w1(0, 1)
            for b in range(NBLOCK):
                n0 = NSTEP * b
                step(n0, 0, fresh=b == 0)
                split_w1(n0 + 1, 1)
                turn(n0 + 1, 1, first=b)
                with dve.Fori(n0 + 2, n0 + NSTEP - 2, 2) as n:
                    turn(n, 0)
                    turn(n + 1, 1)
                turn(n0 + NSTEP - 2, 0)
                n = n0 + NSTEP - 1
                split_w2(n - 1)
                for f in range(2):
                    for tb in range(2):
                        hidden(n, f, tb, 1)
                    if b + 1 < NBLOCK and f == 0:
                        split_w1(n + 1, 0)
                for j in range(2 * NT):
                    add(n - 1, j)
                    if b + 1 < NBLOCK and j == 3:
                        split_w1(n + 1, 1)
                split_w2(n)
                for t in range(NT):
                    add(n, 2 * t)
                    add(n, 2 * t + 1)
                    if t >= 1:
                        scale_out(b, t - 1)
                scale_out(b, NT - 1)


SEM_NAMES = ["par_a", "eps_a", "ones_a", "x_sq", "x_sum", "x_add", "x_ln", "x_rstd", "h", "h_hi", "h_lo", "w_hi", "w_lo", "proj",
             "tap", "u_head", "ln_sum", "c_center", "c_sq", "c_rstd", "c_norm", "c_silu", "q_tap", "q_silu", "q_out",
             "dve_a",
             "gates_in", "par_b", "rows_done", "rows_out", "decay_in", "cols_done", "scores", "qs", "z", "incr", "y", "yc_lo",
             "xn", "ident", "v_ones", "num", "p", "wk", "h2_lo", "y_lo", "state", "y_t", "y_hi", "yc_hi",
             "wo_lo", "wo_hi", "t_post", "ss", "out_proj", "h2", "h2_t", "cols_t", "act_b", "softplus", "exps", "exps_out",
             "e", "den", "r1", "r2", "ss2", "ss2_sum", "ss_sum", "h2_hi", "var_h", "rs_h", "dve_b", "eps_b", "gi_last",
             "wo_scale",
             "w1_hi", "w1_lo", "w2_hi", "w2_lo", "par_c", "eps_c", "ff1", "ff2", "relu", "sq", "hid_hi", "hid_lo", "acc",
             "fss", "fln", "frs", "fmul", "fin", "out"]
SEM_LISTS = {"w_raw": W_RING, "x_in": 2 * NTB, "th_out": 2, "c_out": 2, "chunk_in": 2, "xc_in_b": 2, "xn_out": 2, "h2_out": 2, "wo_in": KT, "w1_in": 2, "w2_in": 2, "xc_in": 2,
             "xnc_in": 3}


def semaphores(nc, ctx):
    named = {name: ctx.enter_context(nc.semaphore(name)) for name in SEM_NAMES}
    for name, n in SEM_LISTS.items():
        named[name] = [ctx.enter_context(nc.semaphore(f"{name}{i}")) for i in range(n)]
    named["evac"] = {e: ctx.enter_context(nc.semaphore(f"evac_{e}")) for e in ("act", "dve")}
    return named


def layouts(x, pre_mix_norm_w, w_in, qk_conv_w, qk_conv_b, gate_bias, mlstm_norm_w, conv_w, conv_b, conv_norm_w,
            conv_norm_b, w_out, post_mix_norm_w, pre_mlp_norm_w, w_ff1, w_ff2, post_mlp_norm_w):
    def by_channel(a):
        return a.reshape(a.shape[0], -1, P).transpose(2, 1, 0)

    w = w_in[0]
    qk, v, o, gates, val, gate = np.split(w, [2 * DH, 3 * DH, 4 * DH, 4 * DH + 2 * H, 5 * DH + 2 * H], axis=1)

    def tile(a, n):
        return a[:, n * P:(n + 1) * P]

    gate_tile = np.zeros((D, P), w.dtype)
    gate_tile[:, 0:H] = gates[:, 0:H]
    gate_tile[:, 32:32 + H] = gates[:, H:]
    tiles = []
    for g in range(H):
        tiles += [tile(gate, g), tile(val, g), tile(qk, 2 * g), tile(qk, 2 * g + 1)]
    tiles += [gate_tile] + [tile(v, h) for h in VO_HEADS] + [tile(o, h) for h in VO_HEADS]
    params_a = np.concatenate([
        pre_mix_norm_w[0].reshape(KT, P).T,
        by_channel(conv_w[0]).reshape(P, -1),
        conv_b[0].reshape(H, P).T, conv_norm_w[0].reshape(H, P).T, conv_norm_b[0].reshape(H, P).T,
        by_channel(qk_conv_w[0]).reshape(P, -1), qk_conv_b[0].reshape(8, P).T,
    ], axis=1)
    return {
        "xt": np.ascontiguousarray(x[0].T.reshape(KT, P, S).transpose(1, 0, 2)),
        "w_in": np.ascontiguousarray(np.stack(tiles).reshape(N_TILES, KT, P, P).transpose(0, 2, 1, 3)),
        "params_a": np.ascontiguousarray(params_a),
        "x": x[0],
        "w_out": w_out[0].reshape(KT, P, D),
        "params_b": np.ascontiguousarray(np.concatenate([mlstm_norm_w[0].reshape(H, P).T, np.ones((P, H), w.dtype)], axis=1)),
        "gate_bias": np.ascontiguousarray(gate_bias[0].reshape(2, H).T),
        "post_w": post_mix_norm_w[0],
        "w1": np.ascontiguousarray(w_ff1[0].reshape(KT, P, FF // P, P).transpose(2, 1, 0, 3)),
        "w2": w_ff2[0].reshape(FF // P, P, D),
        "params_c": np.ascontiguousarray(pre_mlp_norm_w[0].reshape(KT, P).T),
        "post_mlp_w": post_mlp_norm_w[0],
    }


INPUTS = ["xt", "w_in", "params_a", "x", "w_out", "params_b", "gate_bias", "post_w", "w1", "w2", "params_c", "post_mlp_w"]
SCRATCH = {
    "qk": ([8, P, S], F32), "v": ([NCH, P, DH], F32), "o": ([NCH, P, DH], F32), "yc": ([H, P, S], F32),
    "gates": ([2 * H, S], F32), "rows": ([2, H, S], F32), "decay": ([H, NCH], F32), "xn": ([NCH, P, D], F32),
    "h2_hi": ([P, KT, S], F32), "h2_lo": ([P, KT, S], F32),
}


def build(nc, arrays, out):
    scratch = {name: nc.dram_tensor("scratch_" + name, shape, dt).ap() for name, (shape, dt) in SCRATCH.items()}
    dram = {**arrays, **scratch, "out": out.rearrange("a (n p) d -> (a n) p d", p=P)}
    with ExitStack() as ctx:
        sem = semaphores(nc, ctx)
        psum = ctx.enter_context(nc.psum_tensor("psum", [P, 8, TB], F32))
        phase_a(nc, sem, psum, dram)
        phase_b(nc, sem, psum, dram)
        phase_c(nc, sem, psum, dram)


def kernel(**inputs):
    import concourse.bacc as bacc
    from concourse.bass_utils import run_bass_kernel_spmd as run

    nc = bacc.Bacc("TRN2", target_bir_lowering=False, num_devices=1)
    arrays, args = {}, {}
    for name, a in layouts(**{k: np.asarray(v) for k, v in inputs.items()}).items():
        a = np.ascontiguousarray(a)
        arrays[f"in_{name}"] = a
        args[name] = nc.dram_tensor(f"in_{name}", a.shape, mybir.dt.from_np(a.dtype), kind="ExternalInput").ap()
    out = nc.dram_tensor("out_0", (1, S, D), F32, kind="ExternalOutput").ap()
    build(nc, args, out)
    r = run(nc, [arrays], core_ids=[0])
    return r.results[0]["out_0"]
```

```python
from contextlib import ExitStack

import numpy as np
import concourse.bass as bass
from concourse import mybir
from concourse.alu_op_type import AluOpType as ALU

ACT = mybir.ActivationFunctionType
F32 = mybir.dt.float32
F32R = mybir.dt.float32r

P = 128
S = 2048
D = 1024
KT = D // P
DH = 512
H = 4
HD = 128
FF = 4096
CW = 31
QW = 4
TB = 512
NTB = S // TB
HALF = 1024
NCH = S // P
EPS = 1e-6
SCALE = float(HD) ** -0.5
LN_EXP = "natural_log_exp_and_others"
SILU_TANH = "silu_and_others"
FAR = -1e30

PRE_W, CONV_W, CONV_B, CN_W, CN_B = 0, 8, 8 + H * CW, 8 + H * CW + 4, 8 + H * CW + 8
QKC_W = CN_B + 4
QKC_B = QKC_W + 8 * QW
PAR_A = QKC_B + 8

def group_slots(g):
    out = []
    for tb in range(NTB):
        out += [("gate", g, tb), ("val", g, tb)]
    return out + [("qk", j, tb) for j in (2 * g, 2 * g + 1) for tb in range(NTB)]


def pair_slots(kind, pair):
    return [(kind, pair, m) for m in range(NCH // 2)]


SLOTS = (group_slots(0) + group_slots(1) + pair_slots("v", 0) + group_slots(2) + pair_slots("v", 1) + group_slots(3)
         + [("gates", 0, tb) for tb in range(NTB)] + pair_slots("o", 0) + pair_slots("o", 1))
N_SLOTS = len(SLOTS)
TILES = []
for _kind, _n, _ in SLOTS:
    for _tile in [(_kind, 2 * _n), (_kind, 2 * _n + 1)] if _kind in ("v", "o") else [(_kind, _n)]:
        if _tile not in TILES:
            TILES.append(_tile)
N_TILES = len(TILES)
RING = [0, 1, 2, 3] + [0, 1, 2, 3] + [0, 1] + [2, 3, 0, 1] + [2, 3] + [0, 1, 2, 3] + [2] + [0, 1] + [2, 3]
W_RING = 4
BANKS_A = 6
N_UNITS = 2 * H
U_RING = 3
DVE_TAPS = CW - 1


def tiles_of(slot):
    kind, n, _ = slot
    return [TILES.index(t) for t in ([(kind, 2 * n), (kind, 2 * n + 1)] if kind in ("v", "o") else [(kind, n)])]


def first_use(tile):
    return min(i for i, s in enumerate(SLOTS) if tile in tiles_of(s))


def last_use(tile):
    return max(i for i, s in enumerate(SLOTS) if tile in tiles_of(s))


def before_in_ring(tile):
    return max((t for t in range(tile) if RING[t] == RING[tile]), default=None)


def nth_in_ring(tile):
    return sum(RING[t] == RING[tile] for t in range(tile))


def split_slot(tile):
    if tile < 4:
        return 0
    return max(first_use(tile) - 5, last_use(before_in_ring(tile)) + 1, split_slot(tile - 1))


def tiles_split_at(s):
    return [t for t in range(N_TILES) if split_slot(t) == s]


def evacs(s, engine):
    return sum((k == "val") == (engine == "dve") for k, _, _ in SLOTS[: s + 1])


def glu_slot(u):
    return SLOTS.index(("val", u // 2, 2 * (u % 2)))


def tap_plan():
    out, n, room = [], 0, 0
    for s in range(N_SLOTS):
        ready = DVE_TAPS * sum(SLOTS.index(("val", u // 2, 2 * (u % 2) + 1)) <= s for u in range(N_UNITS))
        if s >= 2 * NTB:
            room += 100 - 13 * (SLOTS[s][0] == "val")
        if s and SLOTS[s - 1][0] == "qk" and SLOTS[s - 1][2] % 2 == 1:
            room -= 78
        more = max(0, min(ready - n, room // 26))
        for u in range(U_RING, N_UNITS):
            if s + 1 >= glu_slot(u):
                more = max(more, DVE_TAPS * (u - U_RING + 1) - n)
        n += more
        room = min(room - 26 * more, 26)
        out.append(n)
    return out


TAPS = tap_plan()
FIRST_TAP = [max(min(s for s in range(N_SLOTS) if TAPS[s] > DVE_TAPS * u) - 1, glu_slot(u) + 2) for u in range(N_UNITS)]
CONV_END = [min(s for s in range(N_SLOTS) if TAPS[s] >= DVE_TAPS * (u + 1)) for u in range(N_UNITS)]
AT_MEAN, AT_CENTER, AT_SQUARE, AT_VAR, AT_RSTD, AT_NORM, AT_SILU = 1, 2, 3, 4, 5, 6, 7


TAIL_SLOT = N_SLOTS - 6


def units_at(s, step):
    return [u for u in range(N_UNITS) if CONV_END[u] + step == s]


def q_taps(j, half):
    return (2 * QW - 1) * j + QW * half - (half == 2)


def th_uses(s):
    return sum(k in ("gate", "gates", "v", "o") for k, _, _ in SLOTS[: s + 1])


def th_stores(s, parity):
    n = 0
    for i in range(s + 1):
        k = SLOTS[i][0]
        if k in ("gates", "v", "o") and (th_uses(i) - 1) % 2 == parity:
            n += 2 if k == "gates" else 1
    return n


def last_th_user(s):
    n = th_uses(s) - 1
    for i in range(s):
        if SLOTS[i][0] in ("gate", "gates", "v", "o") and th_uses(i) - 1 == n - 2:
            return i
    return None


def phase_a(nc, sem, psum, dram, big, keep, tail):
    with ExitStack() as ctx:
        def sb(name, shape, dt=F32):
            return ctx.enter_context(nc.sbuf_tensor(name, shape, dt))

        h_hi, h_lo = [big["hi"]], [big["lo"]]
        qout = sb("qout", [P, HALF])
        rstd = sb("rstd_a", [P, HALF])
        qraw = sb("qraw", [P, 2, QW - 1 + HALF])
        u_buf = sb("u_buf", [P, U_RING, CW - 1 + HALF])
        c_buf = sb("c_buf", [P, 2, HALF])
        th = sb("th", [P, 2, TB])
        w_hi = sb("w_hi", [P, W_RING, KT, P], F32R)
        with nc.sbuf_tensor("w_raw", [P, W_RING, KT, P], F32) as w_raw:
            pass
        w_lo = sb("w_lo", [P, W_RING, KT, P], F32R)
        h_hi.append(sb("h_hi1", [P, KT, HALF], F32R))
        with nc.sbuf_tensor("x_raw1", [P, KT, HALF], F32) as x_raw1:
            pass
        h_lo.append(sb("h_lo1", [P, KT, HALF], F32R))
        par = sb("par_a", [P, PAR_A])
        ones, eps = keep["ones"], keep["eps"]
        ln_ps = psum[:, 6:8, :].rearrange("p a b -> p (a b)")

        def x_sq(n):
            return c_buf[:, n % 4 // 2, n % 2 * TB:(n % 2 + 1) * TB]

        def x_adds(n):
            return (KT - 1) * (n // KT - 1) + max(n % KT, 1)

        def tokens(a, kt, at, n):
            return a[at // HALF][:, kt, at % HALF:at % HALF + n]

        def x_at(tb, kt):
            return tokens([big["raw"], x_raw1], kt, tb * TB, TB)

        def sync(sp):
            def load_w(t):
                if t >= W_RING:
                    sp.wait_ge(sem["proj"], last_use(before_in_ring(t)) + 1)
                sp.dma_start(w_raw[:, RING[t]], dram["w_in"][t]).then_inc(sem["w_raw"][RING[t]], 16)

            def load_x(tb):
                for half in range(2):
                    kt = slice(half * KT // 2, (half + 1) * KT // 2)
                    sp.dma_start(x_at(tb, kt), dram["xt"][:, kt, tb * TB:(tb + 1) * TB]).then_inc(sem["x_in"][2 * tb + half], 16)

            sp.dma_start(par[:], dram["params_a"]).then_inc(sem["par_a"], 16)
            load_x(0)
            load_w(0)
            load_w(1)
            for tb in range(1, NTB):
                load_x(tb)
            load_w(2)
            load_w(3)
            tail["parameters"](sp)
            for t in range(4, N_TILES):
                load_w(t)
            tail["w_out"](sp)

        def gpsimd(pool):
            def split_w(t):
                pool.wait_ge(sem["w_hi"], t + 1)
                nc.gpsimd.tensor_tensor(w_lo[:, RING[t]], w_raw[:, RING[t]], w_hi[:, RING[t]].bitcast(F32),
                                        ALU.subtract).then_inc(sem["w_lo"], 1)

            nc.gpsimd.memset(ones[:], 1.0).then_inc(sem["ones_a"], 1)
            for tb in range(1, NTB):
                total = qout[:, (tb % 2) * TB:(tb % 2 + 1) * TB]
                for kt in range(1, KT):
                    n = KT * tb + kt
                    pool.wait_ge(sem["x_sq"], n + 1)
                    if kt == 1:
                        if tb == 3:
                            pool.wait_ge(sem["x_sum"], KT + 1)
                        a = x_sq(n - 1)
                    else:
                        pool.wait_ge(sem["x_add"], x_adds(n - 1))
                        a = total
                    nc.gpsimd.tensor_tensor(total, a, x_sq(n), ALU.add).then_inc(sem["x_add"], 1)
            tail["masks"](pool)
            for s in range(N_SLOTS):
                for t in tiles_split_at(s):
                    if t >= 4:
                        split_w(t)
                for u in units_at(s, AT_NORM):
                    pool.wait_ge(sem["c_rstd"], 2 * u + 2)
                    nc.gpsimd.tensor_tensor(c_buf[:, u % 2], c_buf[:, u % 2], rstd[:], ALU.mult).then_inc(sem["c_norm"], 1)
            for b in range(2):
                pool.wait_ge(sem["c_out"][b], 16 * (N_UNITS // 2))
            pool.wait_ge(sem["q_out"], 16 * 16)
            tail["load_gates"](pool)

        def tensor(pe):
            def sum_squares(tb):
                if tb == 0:
                    pe.wait_ge(sem["ones_a"], 1)
                if tb >= 2:
                    pe.wait_ge(sem["x_rstd"], tb - 1)
                if tb == 0:
                    for kt in range(KT):
                        pe.wait_ge(sem["x_sq"], kt + 1)
                        nc.tensor.matmul(psum[:, 6, :], ones[:], x_sq(kt), start=kt == 0,
                                         stop=kt == KT - 1).then_inc(sem["x_sum"], 1)
                else:
                    pe.wait_ge(sem["x_add"], x_adds(KT * tb + KT - 1))
                    nc.tensor.matmul(psum[:, 6 + tb % 2, :], ones[:], qout[:, (tb % 2) * TB:(tb % 2 + 1) * TB],
                                     start=True, stop=True).then_inc(sem["x_sum"], 1)

            def slot(s):
                kind, n, tb = SLOTS[s]
                tile = tiles_of(SLOTS[s])
                out = psum[:, s % BANKS_A, :]
                pe.wait_ge(sem["w_hi"], tile[-1] + 1)
                pe.wait_ge(sem["w_lo"], tile[-1] + 1)
                if s >= BANKS_A:
                    by = "dve" if SLOTS[s - BANKS_A][0] == "val" else "act"
                    pe.wait_ge(sem["evac"][by], evacs(s - BANKS_A, by))
                r = RING[tile[0]]
                if kind in ("v", "o"):
                    for k in range(2):
                        o = out[:, 2 * k * P:2 * (k + 1) * P].rearrange("p (a b) -> p a b", a=2)
                        for kt in range(KT):
                            hi, lo = tokens(h_hi, kt, (2 * tb + k) * P, P), tokens(h_lo, kt, (2 * tb + k) * P, P)
                            pairs = [(hi, w_hi[:, r:r + 2, kt, :]), (hi, w_lo[:, r:r + 2, kt, :]), (lo, w_hi[:, r:r + 2, kt, :])]
                            for i, (a, b) in enumerate(pairs):
                                mm = nc.tensor.matmul(o, a, b, start=kt == 0 and i == 0, stop=kt == KT - 1 and i == 2)
                else:
                    for kt in range(KT):
                        if kind == "gate" and n == 0:
                            pe.wait_ge(sem["h_hi"], KT * tb + kt + 1)
                            pe.wait_ge(sem["h_lo"], KT * tb + kt + 1)
                        hi, lo = tokens(h_hi, kt, tb * TB, TB), tokens(h_lo, kt, tb * TB, TB)
                        pairs = [(w_hi[:, r, kt, :], hi), (w_hi[:, r, kt, :], lo), (w_lo[:, r, kt, :], hi)]
                        for i, (a, b) in enumerate(pairs):
                            mm = nc.tensor.matmul(out, a, b, start=kt == 0 and i == 0, stop=kt == KT - 1 and i == 2)
                mm.then_inc(sem["proj"], 1)

            def group_sum(src, b):
                nc.tensor.matmul(psum[:, 6 + b, :], ones[:], src[:, b * TB:(b + 1) * TB],
                                 start=True, stop=True).then_inc(sem["ln_sum"], 1)

            sum_squares(0)
            for s in range(N_SLOTS):
                slot(s)
                if s in (0, 2, 4):
                    sum_squares(1 + s // 2)
                for u in units_at(s, AT_MEAN):
                    pe.wait_ge(sem["tap"], DVE_TAPS * (u + 1))
                    if u == 0:
                        pe.wait_ge(sem["x_rstd"], NTB)
                    else:
                        pe.wait_ge(sem["c_rstd"], 2 * u)
                    for b in range(2):
                        group_sum(c_buf[:, u % 2], b)
                for u in units_at(s, AT_VAR):
                    pe.wait_ge(sem["c_sq"], u + 1)
                    for b in range(2):
                        group_sum(rstd, b)
                if s == TAIL_SLOT + 1:
                    pe.wait_ge(sem["c_rstd"], 2 * N_UNITS)
                    tail["carry_in"](pe)
                if s == TAIL_SLOT + 2:
                    tail["carry_out"](pe)
                if s == TAIL_SLOT + 3:
                    tail["columns"](pe)

        def scalar(act):
            def square_x(n):
                act.wait_ge(sem["x_in"][n // (KT // 2)], 16)
                if n >= 4:
                    if n - 4 < KT:
                        act.wait_ge(sem["x_sum"], n - 3)
                    else:
                        act.wait_ge(sem["x_add"], x_adds(n - 4))
                nc.scalar.activation(x_sq(n), x_at(n // KT, n % KT), ACT.Square).then_inc(sem["x_sq"], 1)

            def rstd_x(tb):
                r = rstd[:, (tb % 2) * TB:(tb % 2 + 1) * TB]
                act.wait_ge(sem["x_sum"], KT + tb)
                if tb >= 2:
                    act.wait_ge(sem["h"], KT * (tb - 1))
                nc.scalar.activation(r, psum[:, 6 + tb % 2, :], ACT.Ln, scale=1.0 / D, bias=eps[:, 0:1]).then_inc(sem["x_ln"], 1)
                act.wait_ge(sem["x_ln"], tb + 1)
                nc.scalar.activation(r, r, ACT.Exp, scale=-0.5).then_inc(sem["x_rstd"], 1)

            def high_x(n):
                tb, kt = n // KT, n % KT
                act.wait_ge(sem["h"], n + 1)
                nc.scalar.activation(tokens(h_hi, kt, tb * TB, TB), x_at(tb, kt), ACT.Copy).then_inc(sem["h_hi"], 1)
                for i in range(KT + n + min(n, 3), KT + n + 1 + min(n + 1, 3)):
                    if i < KT * NTB:
                        square_x(i)

            def split_w(t):
                act.wait_ge(sem["w_raw"][RING[t]], 16 * (nth_in_ring(t) + 1))
                nc.scalar.activation(w_hi[:, RING[t]], w_raw[:, RING[t]], ACT.Copy).then_inc(sem["w_hi"], 1)

            def evacuate(s):
                kind, n, tb = SLOTS[s]
                if kind == "val":
                    return
                ps = psum[:, s % BANKS_A, :]
                act.wait_ge(sem["proj"], s + 1)
                if kind == "qk":
                    half = tb // 2
                    if n >= 1 and tb % 2 == 0:
                        act.wait_ge(sem["q_tap"], q_taps(n - 1, half + 1))
                    at = QW - 1 + (tb % 2) * TB
                    nc.scalar.activation(qraw[:, half, at:at + TB], ps, ACT.Copy).then_inc(sem["evac"]["act"], 1)
                    return
                k = (th_uses(s) - 1) % 2
                before = last_th_user(s)
                if before is not None:
                    if SLOTS[before][0] == "gate":
                        act.wait_ge(sem["evac"]["dve"], evacs(before + 1, "dve"))
                    else:
                        act.wait_ge(sem["th_out"][k], 16 * th_stores(before, k))
                if kind == "gate":
                    nc.scalar.activation(th[:, k, :], ps, ACT.Tanh, scale=0.5).then_inc(sem["evac"]["act"], 1)
                    return
                rows = slice(0, 36) if kind == "gates" else slice(0, P)
                nc.scalar.activation(th[rows, k, :], ps[rows], ACT.Tanh if kind == "o" else ACT.Copy,
                                     scale=0.5 if kind == "o" else 1.0).then_inc(sem["evac"]["act"], 1)
                act.wait_ge(sem["evac"]["act"], evacs(s, "act"))
                if kind == "gates":
                    for half in range(2):
                        act.dma_start(dram["gates"][4 * half:4 * half + 4, tb * TB:(tb + 1) * TB],
                                      th[32 * half:32 * half + 4, k, :]).then_inc(sem["th_out"][k], 16)
                else:
                    act.dma_start(dram[kind][2 * tb:2 * tb + 2, :, 2 * n * P:2 * (n + 1) * P].rearrange("c p d -> p c d"),
                                  th[:, k, :].rearrange("p (c d) -> p c d", c=2)).then_inc(sem["th_out"][k], 16)

            def first_tap(u):
                g = u // 2
                act.wait_ge(sem["evac"]["dve"], 2 * (u + 1))
                act.wait_ge(sem["u_head"], u + 1)
                if u >= 2:
                    act.wait_ge(sem["c_out"][u % 2], 16 * (u // 2))
                nc.scalar.activation(c_buf[:, u % 2], u_buf[:, u % U_RING, 0:HALF], ACT.Identity,
                                     scale=par[:, CONV_W + g * CW:CONV_W + g * CW + 1],
                                     bias=par[:, CONV_B + g:CONV_B + g + 1]).then_inc(sem["tap0"], 1)

            def first_tap_qk(s):
                _, j, tb = SLOTS[s]
                half = tb // 2
                act.wait_ge(sem["evac"]["act"], evacs(s, "act"))
                act.wait_ge(sem["q_head"], 1)
                if half == 1:
                    act.wait_ge(sem["q_tap"], q_taps(j, 1))
                if 2 * j + half >= 1:
                    act.wait_ge(sem["q_out"], 16 * (2 * j + half))
                nc.scalar.activation(qout[:], qraw[:, half, 0:HALF], ACT.Copy,
                                     scale=par[:, QKC_W + j * QW:QKC_W + j * QW + 1]).then_inc(sem["q_tap0"], 1)

            def silu_qk(s):
                _, j, tb = SLOTS[s]
                half = tb // 2
                act.wait_ge(sem["q_tap"], q_taps(j, half + 1))
                nc.scalar.activation(qout[:], qout[:], ACT.Silu,
                                     bias=par[:, QKC_B + j:QKC_B + j + 1]).then_inc(sem["q_silu"], 1)
                act.wait_ge(sem["q_silu"], 2 * j + half + 1)
                act.dma_start(dram["qk"][j, :, half * HALF:(half + 1) * HALF], qout[:]).then_inc(sem["q_out"], 16)

            nc.scalar.preload_act_table_set(LN_EXP)
            act.wait_ge(sem["par_a"], 16)
            act.wait_ge(sem["eps_a"], 1)
            for n in range(KT):
                square_x(n)
            split_w(0)
            split_w(1)
            for tb in range(NTB):
                rstd_x(tb)
                if tb == NTB - 1:
                    nc.scalar.preload_act_table_set(SILU_TANH)
                    evacuate(0)
                for kt in range(KT):
                    high_x(KT * tb + kt)
            split_w(2)
            split_w(3)
            for s in range(N_SLOTS):
                for t in tiles_split_at(s):
                    if t >= 4:
                        split_w(t)
                if s >= 1:
                    evacuate(s)
                for u in units_at(s, AT_SQUARE):
                    act.wait_ge(sem["c_center"], u + 1)
                    if u >= 1:
                        act.wait_ge(sem["c_norm"], u)
                    nc.scalar.activation(rstd[:], c_buf[:, u % 2], ACT.Square).then_inc(sem["c_sq"], 1)
                for u in units_at(s, AT_RSTD):
                    nc.scalar.preload_act_table_set(LN_EXP)
                    act.wait_ge(sem["ln_sum"], 4 * u + 4)
                    nc.scalar.activation(rstd[:], ln_ps, ACT.Ln, scale=1.0 / P, bias=eps[:, 0:1]).then_inc(sem["c_rstd"], 1)
                    act.wait_ge(sem["c_rstd"], 2 * u + 1)
                    nc.scalar.activation(rstd[:], rstd[:], ACT.Exp, scale=-0.5).then_inc(sem["c_rstd"], 1)
                    nc.scalar.preload_act_table_set(SILU_TANH)
                for u in units_at(s, AT_SILU):
                    g, half = u // 2, u % 2
                    act.wait_ge(sem["c_norm"], u + 1)
                    nc.scalar.activation(c_buf[:, u % 2], c_buf[:, u % 2], ACT.Silu, scale=par[:, CN_W + g:CN_W + g + 1],
                                         bias=par[:, CN_B + g:CN_B + g + 1]).then_inc(sem["c_silu"], 1)
                    act.wait_ge(sem["c_silu"], u + 1)
                    act.dma_start(dram["yc"][g, :, half * HALF:(half + 1) * HALF], c_buf[:, u % 2]).then_inc(sem["c_out"][u % 2], 16)
                if s >= 2 and SLOTS[s - 2][0] == "qk" and SLOTS[s - 2][2] % 2 == 1:
                    silu_qk(s - 2)
                if SLOTS[s][0] == "qk" and SLOTS[s][2] % 2 == 1:
                    first_tap_qk(s)
                for u in range(N_UNITS):
                    if FIRST_TAP[u] == s:
                        first_tap(u)
                if s == TAIL_SLOT:
                    nc.scalar.preload_act_table_set(LN_EXP)
                    tail["softplus"](act)
                    nc.scalar.preload_act_table_set(SILU_TANH)
                if s == TAIL_SLOT + 1:
                    nc.scalar.preload_act_table_set(LN_EXP)
                    tail["exps"](act)
                    nc.scalar.preload_act_table_set(SILU_TANH)
                if s >= N_SLOTS - 3:
                    if s == N_SLOTS - 1:
                        nc.scalar.preload_act_table_set(LN_EXP)
                        tail["weights"](act, 0)
                    for kt in {N_SLOTS - 3: range(4), N_SLOTS - 2: range(4, 7), N_SLOTS - 1: ()}[s]:
                        tail["split_wo"](act, kt)

        def vector(dve):
            self_n = [0]

            def link(ins):
                self_n[0] += 1
                ins.then_inc(sem["dve_a"], 1)
                dve.wait_ge(sem["dve_a"], self_n[0])

            def normalise_x(tb):
                dve.wait_ge(sem["x_rstd"], tb + 1)
                r = rstd[:, (tb % 2) * TB:(tb % 2 + 1) * TB]

                def low(kt):
                    dve.wait_ge(sem["h_hi"], KT * tb + kt + 1)
                    nc.vector.tensor_tensor(tokens(h_lo, kt, tb * TB, TB), x_at(tb, kt),
                                            tokens(h_hi, kt, tb * TB, TB).bitcast(F32), ALU.subtract).then_inc(sem["h_lo"], 1)

                for kt in range(KT):
                    x = x_at(tb, kt)
                    nc.vector.scalar_tensor_tensor(out=x, in0=x, scalar=par[:, PRE_W + kt:PRE_W + kt + 1], in1=r,
                                                   op0=ALU.mult, op1=ALU.mult).then_inc(sem["h"], 1)
                    if kt >= 1:
                        low(kt - 1)
                    if tb == NTB - 1 and kt == 2:
                        glu(1)
                low(KT - 1)

            def split_w(t):
                dve.wait_ge(sem["w_hi"], t + 1)
                nc.vector.tensor_tensor(w_lo[:, RING[t]], w_raw[:, RING[t]], w_hi[:, RING[t]].bitcast(F32),
                                        ALU.subtract).then_inc(sem["w_lo"], 1)

            def glu(s):
                _, g, tb = SLOTS[s]
                u = 2 * g + tb // 2
                at = CW - 1 + (tb % 2) * TB
                if tb % 2 == 0 and u >= U_RING:
                    dve.wait_ge(sem["tap"], DVE_TAPS * (u - U_RING + 1))
                if tb == 0:
                    nc.vector.memset(u_buf[:, u % U_RING, 0:CW - 1], 0.0).then_inc(sem["u_head"], 1)
                elif tb == 2:
                    dve.wait_ge(sem["evac"]["dve"], evacs(s - 1, "dve"))
                    nc.vector.tensor_copy(u_buf[:, u % U_RING, 0:CW - 1],
                                          u_buf[:, (u - 1) % U_RING, HALF:HALF + CW - 1]).then_inc(sem["u_head"], 1)
                dve.wait_ge(sem["proj"], s + 1)
                dve.wait_ge(sem["evac"]["act"], evacs(s - 1, "act"))
                nc.vector.scalar_tensor_tensor(out=u_buf[:, u % U_RING, at:at + TB], in0=th[:, (th_uses(s) - 1) % 2, :],
                                               scalar=1.0, in1=psum[:, s % BANKS_A, :], op0=ALU.add,
                                               op1=ALU.mult).then_inc(sem["evac"]["dve"], 1)

            def tap(n):
                u, k = n // DVE_TAPS, n % DVE_TAPS + 1
                g = u // 2
                out, src = c_buf[:, u % 2], u_buf[:, u % U_RING, k:k + HALF]
                if k == 1:
                    dve.wait_ge(sem["tap0"], u + 1)
                else:
                    dve.wait_ge(sem["tap"], n)
                nc.vector.scalar_tensor_tensor(out=out, in0=src, scalar=par[:, CONV_W + g * CW + k:CONV_W + g * CW + k + 1],
                                               in1=out, op0=ALU.mult, op1=ALU.add).then_inc(sem["tap"], 1)

            def convolve_qk(s):
                _, j, tb = SLOTS[s]
                half = tb // 2
                dve.wait_ge(sem["q_tap0"], 2 * j + half + 1)
                for k in range(1, QW):
                    w = par[:, QKC_W + j * QW + k:QKC_W + j * QW + k + 1]
                    if k > 1:
                        dve.wait_ge(sem["q_tap"], q_taps(j, half) + k - 1)
                    nc.vector.scalar_tensor_tensor(out=qout[:], in0=qraw[:, half, k:k + HALF], scalar=w, in1=qout[:],
                                                   op0=ALU.mult, op1=ALU.add).then_inc(sem["q_tap"], 1)
                if half == 0:
                    nc.vector.tensor_copy(qraw[:, 1, 0:QW - 1], qraw[:, 0, HALF:HALF + QW - 1]).then_inc(sem["q_tap"], 1)

            nc.vector.memset(eps[:], EPS).then_inc(sem["eps_a"], 1)
            dve.wait_ge(sem["par_a"], 16)
            link(nc.vector.tensor_scalar(par[:, CONV_W:CONV_W + H * CW], par[:, CONV_W:CONV_W + H * CW], 0.5, None, ALU.mult))
            split_w(0)
            split_w(1)
            for tb in range(NTB):
                normalise_x(tb)
            split_w(2)
            split_w(3)
            for s in range(N_SLOTS):
                if SLOTS[s][0] == "val" and s > 1:
                    glu(s)
                if s == 0:
                    nc.vector.memset(qraw[:, 0, 0:QW - 1], 0.0).then_inc(sem["q_head"], 1)
                for n in range(TAPS[s - 1] if s else 0, TAPS[s]):
                    tap(n)
                if s >= 1 and SLOTS[s - 1][0] == "qk" and SLOTS[s - 1][2] % 2 == 1:
                    convolve_qk(s - 1)
                for u in units_at(s, AT_CENTER):
                    dve.wait_ge(sem["ln_sum"], 4 * u + 2)
                    nc.vector.scalar_tensor_tensor(out=c_buf[:, u % 2], in0=ln_ps, scalar=-1.0 / P, in1=c_buf[:, u % 2],
                                                   op0=ALU.mult, op1=ALU.add).then_inc(sem["c_center"], 1)
            tail["rows"](dve)
            tail["wo_low"](dve, range(KT - 1))
            tail["exponents"](dve)

        return {"sync": sync, "gpsimd": gpsimd, "tensor": tensor, "scalar": scalar, "vector": vector}


WO_SCALE = 0
PAR_B = 8
COL_A, COL_WK, COL_FLOOR = 0, 1, 2
NG = H * NCH
VW = HD + 1


def phase_b(nc, sem, psum, dram, big, keep, prefetch):
    with ExitStack() as ctx:
        def sb(name, shape, dt=F32):
            return ctx.enter_context(nc.sbuf_tensor(name, shape, dt))

        wo_hi, wo_lo = big["hi"], big["lo"]
        wo_raw = big["raw"]
        ident, mask, ones, eps = keep["ident"], keep["mask"], keep["ones"], keep["eps"]
        par, gate_bias = keep["par_b"], keep["gate_bias"]
        cols, decay_b, state, small = keep["cols"], keep["decay_b"], keep["state"], keep["small"]
        q_t = sb("q_t", [P, 2, H, P])
        k_t = sb("k_t", [P, 2, H, P])
        v_c = sb("v_c", [P, 2, H, VW])
        o_c = sb("o_c", [P, 2, DH])
        negm_b = sb("negm_b", [P, 2, H, P])
        winter_b = sb("winter_b", [P, 2, H, P])
        yc_c = sb("yc_c", [P, 2, H, P])
        with ExitStack() as early:
            def row(name, shape=(NG, P)):
                return early.enter_context(nc.sbuf_tensor(name, list(shape), F32))

            gi, gf, soft, b_row, a_max, neg_m, inter, wk_row, floor = (
                row(n) for n in ("gi", "gf", "soft", "b_row", "a_max", "neg_m", "inter", "wk_row", "floor"))
            last, m_in, m_last, decay = (row(n, (1, k)) for n, k in (("last", 2 * NG), ("m_in", NG), ("m_last", NG), ("decay", NG)))
            carry = row("carry", (NG, 2))
        e_c = sb("e_c", [P, H, P])
        p_c = sb("p_c", [P, H, P])
        qs_c = sb("qs_c", [P, H, P])
        wk_c = sb("wk_c", [P, H, P])
        x_c = sb("x_c", [P, 2, D])
        post_w = sb("post_w_sb", [P, D])
        y_c = sb("y_c", [P, DH])
        y_hi = sb("y_hi", [P, 2, KT, P], F32R)
        y_lo = sb("y_lo", [P, 2, KT, P], F32R)
        junk = sb("junk", [P, TB])
        t_post = sb("t_post", [P, D])
        h2 = sb("h2", [P, D])
        xn = sb("xn", [P, 2, D])
        h2_hi = sb("h2_hi", [P, 2, KT, P], F32R)
        h2_lo = sb("h2_lo", [P, 2, KT, P], F32R)
        den, rden, stats, aggr = small[:, 0:4], small[:, 4:8], small[:, 8:32], small[:, 32:40]
        var_h, rs_h, s_h = small[:, 40:44], small[:, 44:48], small[:, 48:52]
        ss, ss2, r1, r2 = small[:, 52:54], small[:, 54:56], small[:, 56:57], small[:, 57:58]


        def by_head(a):
            return a.rearrange("p (h d) -> p h d", h=H)

        def column(c, q):
            return cols[:, q * NG + c:(q + 1) * NG:NCH]

        def chunk_decay(c, h):
            return decay_b[:, h * NCH + c:h * NCH + c + 1]

        def load_parameters(sp):
            sp.dma_start(gate_bias[:], dram["gate_bias"]).then_inc(sem["par_b"], 16)
            sp.dma_start(par[:], dram["params_b"]).then_inc(sem["par_b"], 16)

        def load_w_out(sp):
            sp.wait_ge(sem["proj"], SLOTS.index(("o", 1, NCH // 4 - 1)) + 1)
            for kt in range(KT):
                sp.dma_start(wo_raw[:, kt], dram["w_out"][kt]).then_inc(sem["wo_in"][kt], 16)

        def make_masks(pool):
            nc.gpsimd.memset(ident[:], 0.0).then_inc(sem["ident"], 1)
            nc.gpsimd.memset(mask[:], 0.0).then_inc(sem["ident"], 1)
            pool.wait_ge(sem["ident"], 2)
            nc.gpsimd.affine_select(out=ident[:], in_=ident[:], compare_op=ALU.not_equal, fill=1.0, base=0,
                                    pattern=[[-1, P]], channel_multiplier=1).then_inc(sem["ident"], 1)
            nc.gpsimd.affine_select(out=mask[:], in_=mask[:], compare_op=ALU.is_ge, fill=FAR, base=0,
                                    pattern=[[1, P]], channel_multiplier=-1).then_inc(sem["ident"], 1)

        def load_gates(pool):
            for k in range(2):
                pool.wait_ge(sem["th_out"][k], 16 * th_stores(SLOTS.index(("gates", 0, NTB - 1)), k))
            for buf, n in ((gi, 0), (gf, 1)):
                pool.dma_start(buf[:], dram["gates"][n * H:(n + 1) * H].rearrange("h (c l) -> (h c) l", l=P)) \
                    .then_inc(sem["gates_in"], 16)
            pool.wait_ge(sem["rows_done"], 2)
            for buf, n in ((neg_m, 0), (inter, 1)):
                pool.dma_start(dram["rows"][n].rearrange("h (c l) -> (h c) l", l=P), buf[:]).then_inc(sem["rows_out"], 16)

        def softplus(act):
            def link(ins, n):
                ins.then_inc(sem["softplus"], 1)
                act.wait_ge(sem["softplus"], n)

            act.wait_ge(sem["gates_in"], 32)
            act.wait_ge(sem["par_b"], 32)
            link(nc.scalar.activation(gf[:], gf[:], ACT.Identity, bias=gate_bias[:, 1:2]), 1)
            link(nc.scalar.activation(soft[:], gf[:], ACT.Abs), 2)
            link(nc.scalar.activation(soft[:], soft[:], ACT.Exp, scale=-1.0), 3)
            nc.scalar.activation(soft[:], soft[:], ACT.Ln, bias=1.0).then_inc(sem["softplus"], 1)

        def carry_in(pe):
            pe.wait_ge(sem["ident"], 4)
            pe.wait_ge(sem["a_max"], 1)
            nc.tensor.transpose(psum[0:1, 6, 0:NG], a_max[:, P - 1:P], ident[0:NG, 0:NG])
            nc.tensor.transpose(psum[0:1, 6, NG:2 * NG], b_row[:, P - 1:P], ident[0:NG, 0:NG]).then_inc(sem["carry"], 1)

        def carry_out(pe):
            pe.wait_ge(sem["m_in"], 2)
            nc.tensor.matmul(psum[0:NG, 7, 0:1], m_in[:], ones[0:1, 0:1], start=True, stop=True)
            nc.tensor.matmul(psum[0:NG, 7, 1:2], m_last[:], ones[0:1, 0:1], start=True, stop=True).then_inc(sem["carry"], 1)
            pe.wait_ge(sem["exps_out"], 1)
            nc.tensor.matmul(psum[:, 6, 0:NG], ones[0:1, :], decay[:], start=True, stop=True).then_inc(sem["carry"], 1)

        def columns(pe):
            pe.wait_ge(sem["exps_out"], 4)
            pe.wait_ge(sem["rows_done"], 1)
            for q, src in ((COL_A, gi), (COL_WK, wk_row), (COL_FLOOR, floor)):
                mm = nc.tensor.transpose(psum[:, 7, q * NG:(q + 1) * NG], src[:], ident[0:NG, 0:NG])
            mm.then_inc(sem["cols_t"], 1)

        def exps(act):
            act.wait_ge(sem["m_in"], 3)
            nc.scalar.activation(decay[:], decay[:], ACT.Exp).then_inc(sem["exps_out"], 1)
            act.wait_ge(sem["exps"], 2)
            nc.scalar.activation(inter[:], neg_m[:], ACT.Exp, bias=carry[:, 0:1]).then_inc(sem["exps_out"], 1)
            nc.scalar.activation(wk_row[:], gi[:], ACT.Exp, bias=carry[:, 1:2]).then_inc(sem["exps_out"], 1)
            nc.scalar.activation(floor[:], floor[:], ACT.Exp).then_inc(sem["exps_out"], 1)

        def rows(dve):
            n_self = [0]

            def link(ins):
                n_self[0] += 1
                ins.then_inc(sem["dve_rows"], 1)
                dve.wait_ge(sem["dve_rows"], n_self[0])

            nc.vector.memset(state[:], 0.0).then_inc(sem["state"], 1)
            dve.wait_ge(sem["par_b"], 32)
            dve.wait_ge(sem["ones_a"], 1)
            nc.vector.tensor_scalar(par[:, WO_SCALE:WO_SCALE + H], par[:, WO_SCALE:WO_SCALE + H], 0.5, None,
                                    ALU.mult).then_inc(sem["wo_scale"], 1)
            dve.wait_ge(sem["gates_in"], 32)
            nc.vector.memset(m_in[:], 0.0).then_inc(sem["m_in"], 1)
            nc.vector.tensor_scalar(gi[:], gi[:], gate_bias[:, 0:1], None, ALU.add).then_inc(sem["dve_rows"], 1)
            n_self[0] += 1
            dve.wait_ge(sem["softplus"], 4)
            link(nc.vector.scalar_tensor_tensor(out=gf[:], in0=gf[:], scalar=0.0, in1=soft[:], op0=ALU.min,
                                                op1=ALU.subtract))
            link(nc.vector.tensor_tensor_scan(b_row[:], ones[0:NG], gf[:], 0.0, ALU.mult, ALU.add))
            link(nc.vector.tensor_tensor(gi[:], gi[:], b_row[:], ALU.subtract))
            nc.vector.tensor_tensor_scan(a_max[:], ones[0:NG], gi[:], FAR, ALU.mult, ALU.max).then_inc(sem["a_max"], 1)
            dve.wait_ge(sem["carry"], 1)
            link(nc.vector.tensor_copy(last[:], psum[0:1, 6, 0:2 * NG]))
            dve.wait_ge(sem["m_in"], 1)
            for h in range(H):
                at = h * NCH
                i = nc.vector.tensor_tensor_scan(m_in[:, at + 1:at + NCH], last[:, at:at + NCH - 1],
                                                 last[:, NG + at:NG + at + NCH - 1], 0.0, ALU.max, ALU.add)
            link(i)
            nc.vector.tensor_tensor(m_last[:], m_in[:], last[:, 0:NG], ALU.max).then_inc(sem["m_in"], 1)
            dve.wait_ge(sem["m_in"], 2)
            nc.vector.tensor_tensor(decay[:], m_in[:], m_last[:], ALU.subtract).then_inc(sem["m_in"], 1)
            dve.wait_ge(sem["carry"], 2)
            nc.vector.tensor_copy(carry[:, 0:1], psum[0:NG, 7, 0:1]).then_inc(sem["exps"], 1)
            link(nc.vector.tensor_scalar(carry[:, 1:2], psum[0:NG, 7, 1:2], -1.0, None, ALU.mult))
            dve.wait_ge(sem["a_max"], 1)
            nc.vector.tensor_scalar(neg_m[:], a_max[:], carry[:, 0:1], -1.0, ALU.max, ALU.mult).then_inc(sem["rows_done"], 1)
            dve.wait_ge(sem["rows_done"], 1)
            nc.vector.tensor_tensor(floor[:], neg_m[:], b_row[:], ALU.subtract).then_inc(sem["exps"], 1)
            dve.wait_ge(sem["exps_out"], 2)
            nc.vector.tensor_scalar(inter[:], inter[:], SCALE, None, ALU.mult).then_inc(sem["rows_done"], 1)
            dve.wait_ge(sem["carry"], 3)
            nc.vector.tensor_copy(decay_b[:], psum[:, 6, 0:NG]).then_inc(sem["cols_done"], 1)
            dve.wait_ge(sem["cols_t"], 1)
            nc.vector.tensor_copy(cols[:], psum[:, 7, 0:3 * NG]).then_inc(sem["cols_done"], 1)

        def split_wo(act, kt):
            act.wait_ge(sem["wo_scale"], 1)
            act.wait_ge(sem["wo_in"][kt], 16)
            nc.scalar.activation(wo_hi[:, kt], wo_raw[:, kt], ACT.Copy,
                                 scale=par[:, WO_SCALE + kt:WO_SCALE + kt + 1]).then_inc(sem["wo_hi"], 1)

        def wo_low(dve, kts):
            for kt in kts:
                dve.wait_ge(sem["wo_hi"], kt + 1)
                nc.vector.scalar_tensor_tensor(out=wo_lo[:, kt], in0=wo_raw[:, kt],
                                               scalar=par[:, WO_SCALE + kt:WO_SCALE + kt + 1],
                                               in1=wo_hi[:, kt].bitcast(F32), op0=ALU.mult,
                                               op1=ALU.subtract).then_inc(sem["wo_lo"], 1)

        def chunk_here(eng, c):
            eng.wait_ge(sem["chunk_in"][c % 2], 7 * 16 * (c // 2 + 1))

        def exponents(dve, c):
            chunk_here(dve, c)
            if c >= 1:
                dve.wait_ge(sem["num"], c)
            for h in range(H):
                i = nc.vector.scalar_tensor_tensor(out=p_c[:, h], in0=negm_b[:, c % 2, h],
                                                   scalar=column(c, COL_A)[:, h:h + 1], in1=mask[:], op0=ALU.add,
                                                   op1=ALU.min)
            i.then_inc(sem["z"], 1)

        def weights(act, c):
            act.wait_ge(sem["z"], c + 1)
            if c >= 1:
                act.wait_ge(sem["p"], c)
            nc.scalar.activation(e_c[:], p_c[:], ACT.Exp).then_inc(sem["e"], 1)

        def exponents_0(dve):
            dve.wait_ge(sem["cols_done"], 2)
            dve.wait_ge(sem["ident"], 4)
            exponents(dve, 0)

        def head_ps(bank, h):
            return psum[:, bank + h // 2, (h % 2) * VW:(h % 2 + 1) * VW]

        def sync(sp):
            def load(c):
                b = c % 2
                at = slice(c * P, (c + 1) * P)
                for k in range(2):
                    sp.wait_ge(sem["th_out"][k], 16 * th_stores(SLOTS.index(("o", 1, c // 2)), k))
                if c >= 2:
                    sp.wait_ge(sem["scores"], c - 1)
                    sp.wait_ge(sem["qs"], c - 1)
                    sp.wait_ge(sem["z"], c - 1)
                    sp.wait_ge(sem["incr"], c - 1)
                    sp.wait_ge(sem["y"], c - 1)
                    sp.wait_ge(sem["yc_lo"], c - 1)
                for buf, src, s in ((q_t, dram["qk"][0:4, :, at], 0), (k_t, dram["qk"][4:8, :, at], 1),
                                    (yc_c, dram["yc"][:, :, at], 2)):
                    sp.dma_start(buf[:, b], src.rearrange("h p t -> p h t")).then_inc(sem["chunk_in"][b], 16)
                sp.dma_start(v_c[:, b, :, 0:HD], by_head(dram["v"][c])).then_inc(sem["chunk_in"][b], 16)
                sp.dma_start(o_c[:, b], dram["o"][c]).then_inc(sem["chunk_in"][b], 16)
                for buf, n in ((negm_b, 0), (winter_b, 1)):
                    sp.dma_start(buf[:, b], dram["rows"][n, :, at].partition_broadcast(P)).then_inc(sem["chunk_in"][b], 16)

            def load_x(c):
                if c >= 2:
                    sp.wait_ge(sem["xn"], c - 1)
                sp.dma_start(x_c[:, c % 2], dram["x"][c * P:(c + 1) * P]).then_inc(sem["xc_in_b"][c % 2], 16)

            sp.wait_ge(sem["rows_out"], 32)
            load(0)
            for c in range(NCH + 4):
                if c + 1 < NCH:
                    load(c + 1)
                if c == NCH + 1:
                    sp.wait_ge(sem["out_proj"], 2 * NCH)
                    for b in range(2):
                        sp.wait_ge(sem["h2_out"][b], 32 * ((NCH - 3) // 2 + 1 - b))
                    prefetch["tokens"](sp)
                if c >= 4:
                    sp.wait_ge(sem["h2_lo"], 2 * (c - 3))
                    at = slice((c - 4) * P, (c - 3) * P)
                    for buf, out in ((h2_hi, dram["h2_hi"]), (h2_lo, dram["h2_lo"])):
                        sp.dma_start(out[:, :, at], buf[:, c % 2].bitcast(F32)).then_inc(sem["h2_out"][c % 2], 16)
                if c == 0:
                    sp.wait_ge(sem["proj"], N_SLOTS)
                    for k in range(2):
                        sp.wait_ge(sem["th_out"][k], 16 * th_stores(N_SLOTS - 1, k))
                    sp.dma_start(post_w[:], dram["post_w"].partition_broadcast(P)).then_inc(sem["post_w"], 16)
                if c < NCH:
                    load_x(c)
                if c == NCH // 2:
                    prefetch["weights"](sp)
                if 0 <= c - 2 < NCH:
                    sp.wait_ge(sem["xn"], c - 1)
                    sp.dma_start(dram["xn"][c - 2], xn[:, c % 2]).then_inc(sem["xn_out"][c % 2], 16)
            for b in range(2):
                sp.wait_ge(sem["h2_out"][b], 32 * NCH // 2)
                sp.wait_ge(sem["xn_out"][b], 16 * NCH // 2)

        def gpsimd(pool):
            nc.gpsimd.memset(v_c[:, :, :, HD:VW], 1.0).then_inc(sem["v_ones"], 1)
            pool.wait_ge(sem["cols_done"], 2)
            for c in range(NCH):
                chunk_here(pool, c)
                if c >= 1:
                    pool.wait_ge(sem["num"], c)
                nc.gpsimd.tensor_tensor(qs_c[:], q_t[:, c % 2], winter_b[:, c % 2], ALU.mult).then_inc(sem["qs"], 1)

        def tensor(pe):
            def scores(c):
                chunk_here(pe, c)
                if c >= 1:
                    pe.wait_ge(sem["p"], c)
                    pe.wait_ge(sem["wk"], c)
                for h in range(H):
                    mm = nc.tensor.matmul(psum[:, 0, h * P:(h + 1) * P], k_t[:, c % 2, h], q_t[:, c % 2, h],
                                          start=True, stop=True)
                for h in range(H):
                    mm = nc.tensor.transpose(psum[:, 1, h * P:(h + 1) * P], k_t[:, c % 2, h], ident[:])
                mm.then_inc(sem["scores"], 1)

            def numerators(c):
                pe.wait_ge(sem["p"], c + 1)
                pe.wait_ge(sem["qs"], c + 1)
                pe.wait_ge(sem["wk"], c + 1)
                if c == 0:
                    pe.wait_ge(sem["v_ones"], 1)
                if c >= 1:
                    pe.wait_ge(sem["y_lo"], c)
                pe.wait_ge(sem["state"], c + 1)
                if c >= 4:
                    pe.wait_ge(sem["h2_lo"], 2 * (c - 3))
                for h in range(H):
                    nc.tensor.matmul(head_ps(2, h), p_c[:, h], v_c[:, c % 2, h], start=True, stop=False)
                    mm = nc.tensor.matmul(head_ps(2, h), qs_c[:, h], state[:, h], start=False, stop=True)
                mm.then_inc(sem["num"], 1)
                for h in range(H):
                    mm = nc.tensor.matmul(head_ps(4, h), wk_c[:, h], v_c[:, c % 2, h], start=True, stop=True)
                mm.then_inc(sem["incr"], 1)

            def transpose_y(c):
                pe.wait_ge(sem["y"], c + 1)
                for h in range(H):
                    mm = nc.tensor.transpose(psum[:, 2, h * P:(h + 1) * P], y_c[:, h * P:(h + 1) * P], ident[:])
                mm.then_inc(sem["y_t"], 1)

            def project(c, half):
                b = c % 2
                if half == 0:
                    pe.wait_ge(sem["y_hi"], c + 1)
                    pe.wait_ge(sem["y_lo"], c + 1)
                    pe.wait_ge(sem["yc_hi"], c + 1)
                    pe.wait_ge(sem["yc_lo"], c + 1)
                if c == 0:
                    pe.wait_ge(sem["wo_lo"], KT)
                    pe.wait_ge(sem["wo_hi"], KT)
                else:
                    pe.wait_ge(sem["t_post"], 2 * (c - 1) + half + 1)
                    pe.wait_ge(sem["ss"], 2 * (c - 1) + half + 1)
                cols_ = slice(half * TB, (half + 1) * TB)
                for kt in range(KT):
                    pairs = [(y_hi[:, b, kt], wo_hi[:, kt, cols_]), (y_hi[:, b, kt], wo_lo[:, kt, cols_]),
                             (y_lo[:, b, kt], wo_hi[:, kt, cols_])]
                    for i, (l, r) in enumerate(pairs):
                        mm = nc.tensor.matmul(psum[:, 6 + half, :], l, r, start=kt == 0 and i == 0,
                                              stop=kt == KT - 1 and i == 2)
                mm.then_inc(sem["out_proj"], 1)

            def transpose_h2(c):
                pe.wait_ge(sem["h2"], c + 1)
                if c >= 1:
                    pe.wait_ge(sem["h2_lo"], 2 * c)
                pe.wait_ge(sem["state"], min(c + 4, NCH) + 1)
                for kt in range(KT):
                    mm = nc.tensor.transpose(psum[:, 4 + kt // 4, (kt % 4) * P:(kt % 4 + 1) * P], h2[:, kt * P:(kt + 1) * P],
                                             ident[:])
                    if kt % 4 == 3:
                        mm.then_inc(sem["h2_t"], 1)

            for e in ("act", "dve"):
                pe.wait_ge(sem["evac"][e], evacs(N_SLOTS - 1, e))
            pe.wait_ge(sem["cols_done"], 2)
            scores(0)
            for c in range(NCH + 3):
                if c < NCH:
                    numerators(c)
                if 1 <= c <= NCH:
                    project(c - 1, 0)
                if c + 1 < NCH:
                    scores(c + 1)
                if c < NCH:
                    transpose_y(c)
                if c >= 3:
                    transpose_h2(c - 3)
                if 1 <= c <= NCH:
                    project(c - 1, 1)

        def scalar(act):
            n_self = [0]

            def link(ins):
                n_self[0] += 1
                ins.then_inc(sem["act_b"], 1)
                act.wait_ge(sem["act_b"], n_self[0])

            def rsqrt(out, in_, scale, signal):
                link(nc.scalar.activation(out, in_, ACT.Ln, scale=scale, bias=eps[:, 0:1]))
                nc.scalar.activation(out, out, ACT.Exp, scale=-0.5).then_inc(signal, 1)

            def wk(c):
                act.wait_ge(sem["scores"], c + 1)
                if c >= 1:
                    act.wait_ge(sem["incr"], c)
                for h in range(H):
                    a = nc.scalar.activation(wk_c[:, h], psum[:, 1, h * P:(h + 1) * P], ACT.Copy,
                                             scale=column(c, COL_WK)[:, h:h + 1])
                a.then_inc(sem["wk"], 1)

            def yc_high(c):
                if c >= 2:
                    act.wait_ge(sem["out_proj"], 2 * (c - 1))
                nc.scalar.activation(y_hi[:, c % 2, H:KT], yc_c[:, c % 2], ACT.Copy).then_inc(sem["yc_hi"], 1)

            def denominators(c):
                act.wait_ge(sem["num"], c + 1)
                if c >= 1:
                    act.wait_ge(sem["y"], c)
                for bank in range(2):
                    a = nc.scalar.activation(den[:, 2 * bank:2 * bank + 2], psum[:, 2 + bank, HD:2 * VW:VW], ACT.Abs)
                a.then_inc(sem["den"], 1)

            def squares(c, half):
                act.wait_ge(sem["out_proj"], 2 * c + half + 1)
                if half:
                    act.wait_ge(sem["ss"], 2 * c + 1)
                elif c >= 1:
                    act.wait_ge(sem["ss_sum"], c)
                    act.wait_ge(sem["ss2"], 2 * c)
                nc.scalar.activation(junk[:], psum[:, 6 + half, :], ACT.Square,
                                     accum_out=ss[:, half:half + 1]).then_inc(sem["ss"], 1)

            def pre_mlp_squares(c):
                act.wait_ge(sem["xn"], c + 1)
                for half in range(2):
                    act.wait_ge(sem["ss"], 2 * c + 2)
                    if half:
                        act.wait_ge(sem["ss2"], 2 * c + 1)
                    nc.scalar.activation(junk[:], xn[:, c % 2, half * TB:(half + 1) * TB], ACT.Square,
                                         accum_out=ss2[:, half:half + 1]).then_inc(sem["ss2"], 1)

            def pre_mlp(c):
                act.wait_ge(sem["ss2_sum"], c + 1)
                rsqrt(r2, r2, 1.0 / D, sem["r2"])
                act.wait_ge(sem["r2"], c + 1)
                if c >= 1:
                    act.wait_ge(sem["h2_t"], 2 * c)
                nc.scalar.activation(h2[:], xn[:, c % 2], ACT.Copy, scale=r2).then_inc(sem["h2"], 1)

            def h2_high(c):
                for b in range(2):
                    act.wait_ge(sem["h2_t"], 2 * c + b + 1)
                    if c >= 2:
                        act.wait_ge(sem["h2_out"][c % 2], 32 * (c // 2))
                    nc.scalar.activation(h2_hi[:, c % 2, 4 * b:4 * b + 4], by_head(psum[:, 4 + b, :]), ACT.Copy).then_inc(sem["h2_hi"], 1)

            act.wait_ge(sem["cols_done"], 2)
            wk(0)
            split_wo(act, KT - 1)
            yc_high(0)
            for c in range(NCH + 3):
                if c < NCH:
                    denominators(c)
                    act.wait_ge(sem["var_h"], c + 1)
                    rsqrt(rs_h, var_h, 1.0, sem["rs_h"])
                if c + 1 < NCH:
                    weights(act, c + 1)
                if c + 1 < NCH:
                    wk(c + 1)
                if c < NCH:
                    act.wait_ge(sem["y_t"], c + 1)
                    nc.scalar.activation(y_hi[:, c % 2, 0:H], by_head(psum[:, 2, :]), ACT.Copy).then_inc(sem["y_hi"], 1)
                if c >= 3:
                    h2_high(c - 3)
                if 2 <= c < NCH + 2:
                    pre_mlp_squares(c - 2)
                if NCH - 1 <= c <= NCH:
                    prefetch["split_act"](act, 2 * (c - NCH + 1))
                    prefetch["split_act"](act, 2 * (c - NCH + 1) + 1)
                if 1 <= c <= NCH:
                    squares(c - 1, 0)
                if 2 <= c < NCH + 2:
                    pre_mlp(c - 2)
                if 1 <= c <= NCH:
                    squares(c - 1, 1)
                if c + 1 < NCH:
                    yc_high(c + 1)
                if 1 <= c <= NCH:
                    act.wait_ge(sem["ss_sum"], c)
                    rsqrt(r1, r1, 1.0 / D, sem["r1"])

        def vector(dve):
            n_self = [0]

            def link(ins):
                n_self[0] += 1
                ins.then_inc(sem["dve_b"], 1)
                dve.wait_ge(sem["dve_b"], n_self[0])

            def weigh(c):
                dve.wait_ge(sem["e"], c + 1)
                dve.wait_ge(sem["scores"], c + 1)
                nc.vector.scalar_tensor_tensor(out=p_c[:], in0=by_head(psum[:, 0, :]), scalar=SCALE, in1=e_c[:],
                                               op0=ALU.mult, op1=ALU.mult).then_inc(sem["p"], 1)

            def yc_low(c):
                dve.wait_ge(sem["yc_hi"], c + 1)
                nc.vector.tensor_tensor(y_lo[:, c % 2, H:KT], yc_c[:, c % 2], y_hi[:, c % 2, H:KT].bitcast(F32),
                                        ALU.subtract).then_inc(sem["yc_lo"], 1)

            def update_state(c):
                dve.wait_ge(sem["incr"], c + 1)
                for h in range(H):
                    i = nc.vector.scalar_tensor_tensor(out=state[:, h], in0=state[:, h], scalar=chunk_decay(c, h),
                                                       in1=head_ps(4, h), op0=ALU.mult, op1=ALU.add)
                i.then_inc(sem["state"], 1)

            def normalise_heads(c):
                dve.wait_ge(sem["den"], c + 1)
                for h in range(H):
                    i = nc.vector.bn_stats(stats[:, 6 * h:6 * h + 6], head_ps(2, h)[:, 0:HD])
                link(i)
                for h in range(H):
                    i = nc.vector.bn_aggr(aggr[:, 2 * h:2 * h + 2], stats[:, 6 * h:6 * h + 6])
                link(i)
                link(nc.vector.tensor_tensor(den, den, column(c, COL_FLOOR), ALU.max))
                link(nc.vector.reciprocal(rden, den))
                link(nc.vector.tensor_tensor(var_h, aggr[:, 1:8:2], rden, ALU.mult))
                nc.vector.tensor_tensor(var_h, var_h, rden, ALU.mult).then_inc(sem["var_h"], 1)
                dve.wait_ge(sem["rs_h"], c + 1)
                link(nc.vector.tensor_tensor(s_h, rs_h, rden, ALU.mult))
                if c >= 1:
                    dve.wait_ge(sem["y_t"], c)
                for h in range(H):
                    i = nc.vector.tensor_scalar(y_c[:, h * P:(h + 1) * P], head_ps(2, h)[:, 0:HD],
                                                aggr[:, 2 * h:2 * h + 1], s_h[:, h:h + 1], ALU.subtract, ALU.mult)
                link(i)
                nc.vector.scalar_tensor_tensor(out=y_c[:], in0=o_c[:, c % 2], scalar=1.0, in1=y_c[:], op0=ALU.add,
                                               op1=ALU.mult).then_inc(sem["y"], 1)

            def y_low(c):
                dve.wait_ge(sem["y_hi"], c + 1)
                nc.vector.tensor_tensor(y_lo[:, c % 2, 0:H], by_head(psum[:, 2, :]), y_hi[:, c % 2, 0:H].bitcast(F32),
                                        ALU.subtract).then_inc(sem["y_lo"], 1)

            def post_scale(c, half):
                at = slice(half * TB, (half + 1) * TB)
                if c == 0:
                    dve.wait_ge(sem["post_w"], 16)
                dve.wait_ge(sem["ss"], 2 * c + half + 1)
                if c >= 1:
                    dve.wait_ge(sem["xn"], c)
                if half == 1:
                    nc.vector.tensor_tensor(r1, ss[:, 0:1], ss[:, 1:2], ALU.add).then_inc(sem["ss_sum"], 1)
                nc.vector.tensor_tensor(t_post[:, at], psum[:, 6 + half, :], post_w[:, at],
                                        ALU.mult).then_inc(sem["t_post"], 1)

            def residual(c):
                dve.wait_ge(sem["r1"], c + 1)
                dve.wait_ge(sem["t_post"], 2 * c + 2)
                dve.wait_ge(sem["xc_in_b"][c % 2], 16 * (c // 2 + 1))
                if c >= 2:
                    dve.wait_ge(sem["h2"], c - 1)
                    dve.wait_ge(sem["xn_out"][c % 2], 16 * (c // 2))
                nc.vector.scalar_tensor_tensor(out=xn[:, c % 2], in0=t_post[:], scalar=r1, in1=x_c[:, c % 2],
                                               op0=ALU.mult, op1=ALU.add).then_inc(sem["xn"], 1)

            def sum_squares(c):
                dve.wait_ge(sem["ss2"], 2 * c + 2)
                if c >= 1:
                    dve.wait_ge(sem["h2"], c)
                nc.vector.tensor_tensor(r2, ss2[:, 0:1], ss2[:, 1:2], ALU.add).then_inc(sem["ss2_sum"], 1)

            def h2_low(c):
                for b in range(2):
                    dve.wait_ge(sem["h2_hi"], 2 * c + b + 1)
                    if c >= 2:
                        dve.wait_ge(sem["h2_out"][c % 2], 32 * (c // 2))
                    nc.vector.tensor_tensor(h2_lo[:, c % 2, 4 * b:4 * b + 4], by_head(psum[:, 4 + b, :]),
                                            h2_hi[:, c % 2, 4 * b:4 * b + 4].bitcast(F32), ALU.subtract).then_inc(sem["h2_lo"], 1)

            weigh(0)
            wo_low(dve, (KT - 1,))
            yc_low(0)
            for c in range(NCH + 3):
                if c < NCH:
                    update_state(c)
                    normalise_heads(c)
                if c + 1 < NCH:
                    exponents(dve, c + 1)
                if 2 <= c < NCH + 2:
                    residual(c - 2)
                if NCH <= c <= NCH + 1:
                    prefetch["split_dve"](dve, 2 * (c - NCH))
                    prefetch["split_dve"](dve, 2 * (c - NCH) + 1)
                if c + 1 < NCH:
                    weigh(c + 1)
                if c < NCH:
                    y_low(c)
                if c >= 3:
                    h2_low(c - 3)
                if 2 <= c < NCH + 2:
                    sum_squares(c - 2)
                if 1 <= c <= NCH:
                    post_scale(c - 1, 0)
                    post_scale(c - 1, 1)
                if c + 1 < NCH:
                    yc_low(c + 1)

        return {"sync": sync, "gpsimd": gpsimd, "tensor": tensor, "scalar": scalar, "vector": vector,
                "tail": {"parameters": load_parameters, "w_out": load_w_out, "masks": make_masks, "load_gates": load_gates,
                         "softplus": softplus, "carry_in": carry_in, "carry_out": carry_out, "columns": columns,
                         "exps": exps, "rows": rows, "split_wo": split_wo, "wo_low": wo_low, "exponents": exponents_0,
                         "weights": weights}}


BLOCK = 1024
NBLOCK = S // BLOCK
NT = BLOCK // P
CHUNK_F = 256
NSTEP = FF // CHUNK_F
LAST = NBLOCK * NSTEP - 1
Q_RING = 3


def phase_c(nc, sem, psum, dram, big):
    with ExitStack() as ctx:
        def sb(name, shape, dt=F32):
            return ctx.enter_context(nc.sbuf_tensor(name, shape, dt))

        x_hi, x_lo = big["hi"], big["lo"]
        relu = sb("relu", [P, 2, TB])
        sq = sb("sq", [P, 2, TB])
        hid_hi = sb("hid_hi", [P, 2, 2, BLOCK], F32R)
        hid_lo = sb("hid_lo", [P, 2, 2, BLOCK], F32R)
        acc = sb("acc", [P, NT, D])
        w2_hi = sb("w2_hi", [P, 2, D], F32R)
        w2_lo = sb("w2_lo", [P, 2, D], F32R)
        w2_raw = sb("w2_raw", [P, 2, D])
        xn = sb("xn_c", [P, Q_RING, D])
        junk = sq[:].rearrange("p a b -> p (a b)")
        w1_hi = sb("w1_hi", [P, 2, KT, P], F32R)
        w1_lo = sb("w1_lo", [P, 2, KT, P], F32R)
        w1_raw = sb("w1_raw", [P, 2, KT, P])
        par = sb("par_c", [P, KT])
        wpost = sb("wpost_c", [P, D])
        eps = sb("eps_c", [P, 1])
        ss = sb("ss_c", [P, NT])
        rs = sb("rs_c", [P, NT])

        def w2_parts(f, last):
            if last:
                return tuple(a[:, f].rearrange("p k c -> p (k c)") for a in (w1_hi, w1_lo))
            return w2_hi[:, f], w2_lo[:, f]

        def load_w1(sp, n, m, fresh=False):
            for f in range(2):
                if not fresh:
                    sp.wait_ge(sem["w1_hi"], 2 * n + f - 1)
                    sp.wait_ge(sem["w1_lo"], 2 * n + f - 1)
                sp.dma_start(w1_raw[:, f], dram["w1"][bass.ds(2 * m + f, 1)]
                             .rearrange("a p k c -> (a p) k c")).then_inc(sem["w1_in"][f], 16)

        def load_x(sp, b):
            for tb in range(BLOCK // TB):
                for buf, src in ((x_hi, dram["h2_hi"]), (x_lo, dram["h2_lo"])):
                    at = slice(b * BLOCK + tb * TB, b * BLOCK + (tb + 1) * TB)
                    sp.dma_start(buf[:, :, tb * TB:(tb + 1) * TB].bitcast(F32), src[:, :, at]).then_inc(sem["xc_in"][tb], 16)

        def load_weights(sp):
            sp.dma_start(par[:], dram["params_c"]).then_inc(sem["par_c"], 16)
            sp.dma_start(wpost[:], dram["post_mlp_w"].partition_broadcast(P)).then_inc(sem["par_c"], 16)
            load_w1(sp, 0, 0, fresh=True)

        def split_w1_act(act, n, f, fresh=False, kts=range(KT)):
            act.wait_ge(sem["w1_in"][f], 16 * n + 16)
            if not fresh:
                act.wait_ge(sem["ff1"], 4 * n + 2 * f - 2)
            for kt in kts:
                i = nc.scalar.activation(w1_hi[:, f, kt], w1_raw[:, f, kt], ACT.Copy, scale=par[:, kt:kt + 1])
            if kts[-1] == KT - 1:
                i.then_inc(sem["w1_hi"], 1)

        def split_w1_dve(dve, n, f, kts=range(KT)):
            dve.wait_ge(sem["w1_hi"], 2 * n + f + 1)
            for kt in kts:
                i = nc.vector.scalar_tensor_tensor(out=w1_lo[:, f, kt], in0=w1_raw[:, f, kt], scalar=par[:, kt:kt + 1],
                                                   in1=w1_hi[:, f, kt].bitcast(F32), op0=ALU.mult, op1=ALU.subtract)
            if kts[-1] == KT - 1:
                i.then_inc(sem["w1_lo"], 1)

        def first_w1_act(act, piece):
            if piece == 0:
                act.wait_ge(sem["par_c"], 32)
            split_w1_act(act, 0, piece // 2, fresh=True, kts=range(piece % 2 * KT // 2, (piece % 2 + 1) * KT // 2))

        def first_w1_dve(dve, piece):
            if piece == 0:
                dve.wait_ge(sem["par_c"], 32)
            split_w1_dve(dve, 0, piece // 2, kts=range(piece % 2 * KT // 2, (piece % 2 + 1) * KT // 2))

        def phase_b_done(eng):
            eng.wait_ge(sem["h2_hi"], 2 * NCH)
            eng.wait_ge(sem["h2_lo"], 2 * NCH)
            eng.wait_ge(sem["qs"], NCH)

        def sync(sp):
            def load_w2(n, m, fresh=False):
                for f in range(2):
                    if not fresh:
                        sp.wait_ge(sem["w2_hi"], 2 * n + f - 1)
                        sp.wait_ge(sem["w2_lo"], 2 * n + f - 1)
                    sp.dma_start(w2_raw[:, f], dram["w2"][bass.ds(2 * m + f, 1)]
                                 .rearrange("a p c -> (a p) c")).then_inc(sem["w2_in"][f], 16)

            def load_residual(i):
                if i >= Q_RING:
                    sp.wait_ge(sem["fin"], i - Q_RING + 1)
                sp.dma_start(xn[:, i % Q_RING], dram["xn"][i]).then_inc(sem["xnc_in"][i % Q_RING], 16)

            load_w1(sp, 1, 1)
            load_w2(0, 0, fresh=True)
            for i in range(Q_RING):
                load_residual(i)
            for b in range(NBLOCK):
                n0 = NSTEP * b
                with sp.Fori(1, NSTEP - 1) as m:
                    load_w1(sp, n0 + m + 1, m + 1)
                    load_w2(n0 + m, m)
                if b + 1 < NBLOCK:
                    load_w1(sp, n0 + NSTEP, 0)
                load_w2(n0 + NSTEP - 1, NSTEP - 1)
                if b + 1 < NBLOCK:
                    sp.wait_ge(sem["ff1"], 4 * NSTEP * (b + 1))
                    load_x(sp, b + 1)
                    load_w1(sp, n0 + NSTEP + 1, 1)
                    load_w2(n0 + NSTEP, 0)
                for i in range(NT * b, NT * (b + 1)):
                    sp.wait_ge(sem["fin"], i + 1)
                    sp.dma_start(dram["out"][i], acc[:, i % NT, :]).then_inc(sem["out"], 16)
                    if i + Q_RING < NT * NBLOCK:
                        load_residual(i + Q_RING)
            sp.wait_ge(sem["out"], 16 * S // P)

        def gpsimd(pool):
            for i in range(NT * NBLOCK):
                pool.wait_ge(sem["fmul"], i + 1)
                pool.wait_ge(sem["xnc_in"][i % Q_RING], 16 * (i // Q_RING + 1))
                nc.gpsimd.tensor_tensor(acc[:, i % NT], acc[:, i % NT], xn[:, i % Q_RING], ALU.add).then_inc(sem["fin"], 1)

        def tensor(pe):
            def first(n, x_wait=None, fresh=False):
                for f in range(2):
                    pe.wait_ge(sem["w1_hi"], 2 * n + f + 1)
                    pe.wait_ge(sem["w1_lo"], 2 * n + f + 1)
                    for tb in range(2):
                        if x_wait is not None and f == 0:
                            pe.wait_ge(sem["xc_in"][tb], x_wait)
                        if not fresh or f == 1:
                            pe.wait_ge(sem["relu"], 4 * n + 2 * f + tb - 1)
                        for kt in range(KT):
                            cols = slice(tb * TB, (tb + 1) * TB)
                            pairs = [(w1_hi[:, f, kt], x_hi[:, kt, cols]), (w1_hi[:, f, kt], x_lo[:, kt, cols]),
                                     (w1_lo[:, f, kt], x_hi[:, kt, cols])]
                            for i, (l, r) in enumerate(pairs):
                                mm = nc.tensor.matmul(psum[:, tb, :], l, r, start=kt == 0 and i == 0,
                                                      stop=kt == KT - 1 and i == 2)
                        mm.then_inc(sem["ff1"], 1)

            def second(n, par_, fresh=False, last=False):
                pe.wait_ge(sem["w2_hi"], 2 * n + 2)
                pe.wait_ge(sem["w2_lo"], 2 * n + 2)
                pe.wait_ge(sem["hid_lo"], 4 * n + 4)
                for t in range(NT):
                    for half in range(2):
                        j = 2 * t + half
                        if not fresh or j >= 4:
                            pe.wait_ge(sem["acc"], 16 * n + j - 3)
                        cols = slice(half * TB, (half + 1) * TB)
                        tok = slice(t * P, (t + 1) * P)
                        for f in range(2):
                            hi, lo = (a[:, cols] for a in w2_parts(f, last))
                            pairs = [(hid_hi[:, par_, f, tok], hi), (hid_hi[:, par_, f, tok], lo), (hid_lo[:, par_, f, tok], hi)]
                            for i, (l, r) in enumerate(pairs):
                                mm = nc.tensor.matmul(psum[:, 2 + j % 4, :], l, r, start=f == 0 and i == 0, stop=f == 1 and i == 2)
                        mm.then_inc(sem["ff2"], 1)

            for b in range(NBLOCK):
                n0 = NSTEP * b
                first(n0, x_wait=32 * (b + 1), fresh=b == 0)
                first(n0 + 1)
                if b == 0:
                    pe.wait_ge(sem["h2_lo"], 2 * NCH)
                second(n0, 0, fresh=b == 0)
                with pe.Fori(n0 + 2, n0 + NSTEP, 2) as n:
                    first(n)
                    second(n - 1, 1)
                    first(n + 1)
                    second(n, 0)
                second(n0 + NSTEP - 1, 1, last=b == NBLOCK - 1)

        def scalar(act):
            def split_w2(n, fresh=False, last=False):
                for f in range(2):
                    act.wait_ge(sem["w2_in"][f], 16 * n + 16)
                    if last:
                        act.wait_ge(sem["ff1"], 4 * n + 4)
                    elif not fresh:
                        act.wait_ge(sem["ff2"], 16 * n)
                    nc.scalar.activation(w2_parts(f, last)[0], w2_raw[:, f], ACT.Copy).then_inc(sem["w2_hi"], 1)

            def hidden(n, f, tb, par_, early=0):
                g = 4 * n + 2 * f + tb
                act.wait_ge(sem["ff1"], g + 1)
                if early != 1 or f == 1:
                    act.wait_ge(sem["sq"], g - 1)
                nc.scalar.activation(relu[:, tb], psum[:, tb, :], ACT.Relu).then_inc(sem["relu"], 1)
                act.wait_ge(sem["relu"], g + 1)
                if not early:
                    act.wait_ge(sem["ff2"], 16 * n - 16)
                nc.scalar.activation(hid_hi[:, par_, f, tb * TB:(tb + 1) * TB], relu[:, tb], ACT.Square).then_inc(sem["hid_hi"], 1)

            def step(n, par_, early=0, more=True):
                for f in range(2):
                    for tb in range(2):
                        hidden(n, f, tb, par_, early)
                    if more:
                        split_w1_act(act, n + 1, f)

            def final_norm(b):
                for t in range(NT):
                    i = NT * b + t
                    act.wait_ge(sem["acc"], 16 * NSTEP * (b + 1) - 16 + 2 * t + 2)
                    if i >= 1:
                        act.wait_ge(sem["fss"], i)
                    if t == 0:
                        act.wait_ge(sem["hid_lo"], 4 * NSTEP * (b + 1))
                    nc.scalar.activation(junk, acc[:, t, :], ACT.Square, accum_out=ss[:, t:t + 1]).then_inc(sem["fss"], 1)
                    act.wait_ge(sem["fss"], i + 1)
                    if b >= 1:
                        act.wait_ge(sem["fmul"], i - NT + 1)
                    nc.scalar.activation(rs[:, t:t + 1], ss[:, t:t + 1], ACT.Ln, scale=1.0 / D,
                                         bias=eps[:, 0:1]).then_inc(sem["fln"], 1)
                    act.wait_ge(sem["fln"], i + 1)
                    nc.scalar.activation(rs[:, t:t + 1], rs[:, t:t + 1], ACT.Exp, scale=-0.5).then_inc(sem["frs"], 1)

            act.wait_ge(sem["eps_c"], 1)
            phase_b_done(act)
            for b in range(NBLOCK):
                n0 = NSTEP * b
                step(n0, 0, early=1 if b == 0 else 0)
                split_w2(n0, fresh=b == 0)
                step(n0 + 1, 1, early=2 if b == 0 else 0)
                with act.Fori(n0 + 2, n0 + NSTEP - 2, 2) as n:
                    split_w2(n - 1)
                    step(n, 0)
                    split_w2(n)
                    step(n + 1, 1)
                n = n0 + NSTEP - 2
                split_w2(n - 1)
                step(n, 0)
                split_w2(n)
                step(n + 1, 1, more=b + 1 < NBLOCK)
                split_w2(n + 1, last=b == NBLOCK - 1)
                final_norm(b)

        def vector(dve):
            def split_w2(n, last=False):
                for f in range(2):
                    hi, lo = w2_parts(f, last)
                    dve.wait_ge(sem["w2_hi"], 2 * n + f + 1)
                    nc.vector.tensor_tensor(lo, w2_raw[:, f], hi.bitcast(F32), ALU.subtract).then_inc(sem["w2_lo"], 1)

            def hidden(n, f, tb, par_, fresh=False):
                g = 4 * n + 2 * f + tb
                dve.wait_ge(sem["relu"], g + 1)
                if not fresh or f == 1:
                    dve.wait_ge(sem["hid_lo"], g - 1)
                nc.vector.tensor_tensor(sq[:, tb], relu[:, tb], relu[:, tb], ALU.mult).then_inc(sem["sq"], 1)
                dve.wait_ge(sem["sq"], g + 1)
                dve.wait_ge(sem["hid_hi"], g + 1)
                at = slice(tb * TB, (tb + 1) * TB)
                nc.vector.tensor_tensor(hid_lo[:, par_, f, at], sq[:, tb], hid_hi[:, par_, f, at].bitcast(F32),
                                        ALU.subtract).then_inc(sem["hid_lo"], 1)

            def add(n, j):
                dve.wait_ge(sem["ff2"], 16 * n + j + 1)
                dve.wait_ge(sem["acc"], 16 * n + j - 15)
                out = acc[:, j // 2, j % 2 * TB:(j % 2 + 1) * TB]
                nc.vector.tensor_tensor(out, out, psum[:, 2 + j % 4, :], ALU.add).then_inc(sem["acc"], 1)

            def step(n, par_, fresh=False):
                for f in range(2):
                    for tb in range(2):
                        hidden(n, f, tb, par_, fresh)
                    if f == 0:
                        split_w1_dve(dve, n + 1, 0)

            def turn(n, par_, first=None):
                split_w2(n - 1)
                step(n, par_)
                for j in range(2 * NT):
                    if first is None:
                        add(n - 1, j)
                    else:
                        dve.wait_ge(sem["ff2"], 16 * (n - 1) + j + 1)
                        if first >= 1 and j == 0:
                            dve.wait_ge(sem["out"], 16 * NT * first)
                        nc.vector.tensor_copy(acc[:, j // 2, j % 2 * TB:(j % 2 + 1) * TB],
                                              psum[:, 2 + j % 4, :]).then_inc(sem["acc"], 1)
                    if j == 3:
                        split_w1_dve(dve, n + 1, 1)

            def scale_out(b, t):
                i = NT * b + t
                dve.wait_ge(sem["frs"], i + 1)
                nc.vector.scalar_tensor_tensor(out=acc[:, t], in0=acc[:, t], scalar=rs[:, t:t + 1], in1=wpost[:],
                                               op0=ALU.mult, op1=ALU.mult).then_inc(sem["fmul"], 1)

            nc.vector.memset(eps[:], EPS).then_inc(sem["eps_c"], 1)
            phase_b_done(dve)
            for b in range(NBLOCK):
                n0 = NSTEP * b
                if b >= 1:
                    dve.wait_ge(sem["fss"], NT * b)
                step(n0, 0, fresh=b == 0)
                split_w1_dve(dve, n0 + 1, 1)
                turn(n0 + 1, 1, first=b)
                with dve.Fori(n0 + 2, n0 + NSTEP - 2, 2) as n:
                    turn(n, 0)
                    turn(n + 1, 1)
                turn(n0 + NSTEP - 2, 0)
                n = n0 + NSTEP - 1
                split_w2(n - 1)
                for f in range(2):
                    for tb in range(2):
                        hidden(n, f, tb, 1)
                    if b + 1 < NBLOCK and f == 0:
                        split_w1_dve(dve, n + 1, 0)
                for j in range(2 * NT):
                    add(n - 1, j)
                    if b + 1 < NBLOCK and j == 3:
                        split_w1_dve(dve, n + 1, 1)
                    if b + 1 == NBLOCK and j == 3:
                        split_w2(n, last=True)
                if b + 1 < NBLOCK:
                    split_w2(n)
                for t in range(NT):
                    add(n, 2 * t)
                    add(n, 2 * t + 1)
                    if t >= 1:
                        scale_out(b, t - 1)
                scale_out(b, NT - 1)

        return {"sync": sync, "gpsimd": gpsimd, "tensor": tensor, "scalar": scalar, "vector": vector,
                "prefetch": {"weights": load_weights, "tokens": lambda sp: load_x(sp, 0),
                             "split_act": first_w1_act, "split_dve": first_w1_dve}}


SEM_NAMES = ["par_a", "eps_a", "ones_a", "x_sq", "x_sum", "x_add", "x_ln", "x_rstd", "h", "h_hi", "h_lo", "w_hi", "w_lo", "proj",
             "tap", "tap0", "q_tap0", "q_head", "u_head", "ln_sum", "c_center", "c_sq", "c_rstd", "c_norm", "c_silu", "q_tap", "q_silu", "q_out",
             "dve_a", "dve_rows", "a_max", "carry", "m_in", "post_w",
             "gates_in", "par_b", "rows_done", "rows_out", "cols_done", "scores", "qs", "z", "incr", "y", "yc_lo",
             "xn", "ident", "v_ones", "num", "p", "wk", "h2_lo", "y_lo", "state", "y_t", "y_hi", "yc_hi",
             "wo_lo", "wo_hi", "t_post", "ss", "out_proj", "h2", "h2_t", "cols_t", "act_b", "softplus", "exps", "exps_out",
             "e", "den", "r1", "r2", "ss2", "ss2_sum", "ss_sum", "h2_hi", "var_h", "rs_h", "dve_b",
             "wo_scale",
             "w1_hi", "w1_lo", "w2_hi", "w2_lo", "par_c", "eps_c", "ff1", "ff2", "relu", "sq", "hid_hi", "hid_lo", "acc",
             "fss", "fln", "frs", "fmul", "fin", "out"]
SEM_LISTS = {"w_raw": W_RING, "x_in": 2 * NTB, "th_out": 2, "c_out": 2, "chunk_in": 2, "xc_in_b": 2, "xn_out": 2, "h2_out": 2, "wo_in": KT, "w1_in": 2, "w2_in": 2, "xc_in": 2,
             "xnc_in": 3}


def semaphores(nc, ctx):
    named = {name: ctx.enter_context(nc.semaphore(name)) for name in SEM_NAMES}
    for name, n in SEM_LISTS.items():
        named[name] = [ctx.enter_context(nc.semaphore(f"{name}{i}")) for i in range(n)]
    named["evac"] = {e: ctx.enter_context(nc.semaphore(f"evac_{e}")) for e in ("act", "dve")}
    return named


def layouts(x, pre_mix_norm_w, w_in, qk_conv_w, qk_conv_b, gate_bias, mlstm_norm_w, conv_w, conv_b, conv_norm_w,
            conv_norm_b, w_out, post_mix_norm_w, pre_mlp_norm_w, w_ff1, w_ff2, post_mlp_norm_w):
    def by_channel(a):
        return a.reshape(a.shape[0], -1, P).transpose(2, 1, 0)

    w = w_in[0]
    qk, v, o, gates, val, gate = np.split(w, [2 * DH, 3 * DH, 4 * DH, 4 * DH + 2 * H, 5 * DH + 2 * H], axis=1)

    def tile(a, n):
        return a[:, n * P:(n + 1) * P]

    gate_tile = np.zeros((D, P), w.dtype)
    gate_tile[:, 0:H] = gates[:, 0:H]
    gate_tile[:, 32:32 + H] = gates[:, H:]
    columns = {"gate": gate, "val": val, "qk": qk, "v": v, "o": o}
    tiles = [gate_tile if kind == "gates" else tile(columns[kind], n) for kind, n in TILES]
    params_a = np.concatenate([
        pre_mix_norm_w[0].reshape(KT, P).T,
        by_channel(conv_w[0]).reshape(P, -1),
        conv_b[0].reshape(H, P).T, conv_norm_w[0].reshape(H, P).T, conv_norm_b[0].reshape(H, P).T,
        by_channel(qk_conv_w[0]).reshape(P, -1), qk_conv_b[0].reshape(8, P).T,
    ], axis=1)
    return {
        "xt": np.ascontiguousarray(x[0].T.reshape(KT, P, S).transpose(1, 0, 2)),
        "w_in": np.ascontiguousarray(np.stack(tiles).reshape(N_TILES, KT, P, P).transpose(0, 2, 1, 3)),
        "params_a": np.ascontiguousarray(params_a),
        "x": x[0],
        "w_out": w_out[0].reshape(KT, P, D),
        "params_b": np.ascontiguousarray(np.concatenate([mlstm_norm_w[0].reshape(H, P).T, np.ones((P, H), w.dtype)], axis=1)),
        "gate_bias": np.repeat(gate_bias[0].reshape(2, H).T, NCH, axis=0),
        "post_w": post_mix_norm_w[0],
        "w1": np.ascontiguousarray(w_ff1[0].reshape(KT, P, FF // P, P).transpose(2, 1, 0, 3)),
        "w2": w_ff2[0].reshape(FF // P, P, D),
        "params_c": np.ascontiguousarray(pre_mlp_norm_w[0].reshape(KT, P).T),
        "post_mlp_w": post_mlp_norm_w[0],
    }


INPUTS = ["xt", "w_in", "params_a", "x", "w_out", "params_b", "gate_bias", "post_w", "w1", "w2", "params_c", "post_mlp_w"]
SCRATCH = {
    "qk": ([8, P, S], F32), "v": ([NCH, P, DH], F32), "o": ([NCH, P, DH], F32), "yc": ([H, P, S], F32),
    "gates": ([2 * H, S], F32), "rows": ([2, H, S], F32), "xn": ([NCH, P, D], F32),
    "h2_hi": ([P, KT, S], F32), "h2_lo": ([P, KT, S], F32),
}


def kept(nc, ctx):
    def sb(name, shape, dt=F32):
        return ctx.enter_context(nc.sbuf_tensor(name, shape, dt))

    with nc.sbuf_tensor("big_raw", [P, KT, D], F32) as raw:
        pass
    big = {"raw": raw, "lo": sb("big_lo", [P, KT, D], F32R), "hi": sb("big_hi", [P, KT, D], F32R)}
    return big, {"ones": sb("ones", [P, P]), "eps": sb("eps", [P, 1]), "ident": sb("ident", [P, P]), "mask": sb("mask", [P, P]),
                 "par_b": sb("par_b", [P, PAR_B]), "gate_bias": sb("gate_bias", [NG, 2]), "cols": sb("cols", [P, 3 * NG]),
                 "decay_b": sb("decay_b", [P, NG]), "state": sb("state", [P, H, VW]), "small": sb("small", [P, 64])}


def build(nc, arrays, out):
    scratch = {name: nc.dram_tensor("scratch_" + name, shape, dt).ap() for name, (shape, dt) in SCRATCH.items()}
    dram = {**arrays, **scratch, "out": out.rearrange("a (n p) d -> (a n) p d", p=P)}
    with ExitStack() as ctx:
        sem = semaphores(nc, ctx)
        psum = ctx.enter_context(nc.psum_tensor("psum", [P, 8, TB], F32))
        big, keep = kept(nc, ctx)
        c = phase_c(nc, sem, psum, dram, big)
        b = phase_b(nc, sem, psum, dram, big, keep, c["prefetch"])
        a = phase_a(nc, sem, psum, dram, big, keep, b["tail"])
        block = ctx.enter_context(nc.Block())

        @block.sync
        def _(sp):
            for phase in (a, b, c):
                phase["sync"](sp)

        @block.gpsimd
        def _(pool):
            for phase in (a, b, c):
                phase["gpsimd"](pool)

        @block.tensor
        def _(pe):
            for phase in (a, b, c):
                phase["tensor"](pe)

        @block.scalar
        def _(act):
            for phase in (a, b, c):
                phase["scalar"](act)

        @block.vector
        def _(dve):
            for phase in (a, b, c):
                phase["vector"](dve)


def kernel(**inputs):
    import concourse.bacc as bacc
    from concourse.bass_utils import run_bass_kernel_spmd as run

    nc = bacc.Bacc("TRN2", target_bir_lowering=False, num_devices=1)
    arrays, args = {}, {}
    for name, a in layouts(**{k: np.asarray(v) for k, v in inputs.items()}).items():
        a = np.ascontiguousarray(a)
        arrays[f"in_{name}"] = a
        args[name] = nc.dram_tensor(f"in_{name}", a.shape, mybir.dt.from_np(a.dtype), kind="ExternalInput").ap()
    out = nc.dram_tensor("out_0", (1, S, D), F32, kind="ExternalOutput").ap()
    build(nc, args, out)
    r = run(nc, [arrays], core_ids=[0])
    return r.results[0]["out_0"]
```
